# Optimizing a Trainium2 kernel written in Bass

```python
import math
import jax, jax.numpy as jnp
from jax import lax
import numpy as np

D_MODEL = 1024
BATCH = 1
SEQ = 256
DEPTH = 1

HEAD_DIM = 64
MIX_WIDTH = D_MODEL
ATT_HEADS = 8
GDN_HEADS = 8
ATT_WIDTH = ATT_HEADS * HEAD_DIM
GDN_WIDTH = GDN_HEADS * HEAD_DIM
MOBA_BLOCK = 256
MOBA_TOPK = 3
MOBA_QCHUNK = 32
GDN_CHUNK = 64
CONV_WIDTH = 4
D_FF = 4 * D_MODEL
REL_BUCKETS = 32
REL_MAX_EXACT = 16
REL_MAX_DIST = 128
EPS = 1e-6
IN_SIZES = [ATT_WIDTH, ATT_WIDTH, ATT_WIDTH, 3 * GDN_WIDTH, GDN_WIDTH, GDN_HEADS, GDN_HEADS]
IN_COLS = sum(IN_SIZES)


def rms_norm(x, w):
    xf = x.astype(jnp.float32)
    y = xf * lax.rsqrt(jnp.mean(xf * xf, axis=-1, keepdims=True) + EPS)
    return (y * w.astype(jnp.float32)).astype(x.dtype)

def l2_normalize(x):
    xf = x.astype(jnp.float32)
    return xf * lax.rsqrt(jnp.sum(xf * xf, axis=-1, keepdims=True) + EPS)

def rel_bucket(dist):
    d = jnp.maximum(dist, 0)
    large = REL_MAX_EXACT + (
        jnp.log(jnp.maximum(d, 1).astype(jnp.float32) / REL_MAX_EXACT)
        / math.log(REL_MAX_DIST / REL_MAX_EXACT)
        * (REL_BUCKETS - REL_MAX_EXACT)
    ).astype(jnp.int32)
    large = jnp.minimum(large, REL_BUCKETS - 1)
    return jnp.where(d < REL_MAX_EXACT, d, large)

def moba_attention(q, k, v, rel_bias):
    B, S, H, dh = q.shape
    nb = -(-S // MOBA_BLOCK)
    s_pad = nb * MOBA_BLOCK
    qh = q.transpose(0, 2, 1, 3)
    pad = ((0, 0), (0, 0), (0, s_pad - S), (0, 0))
    kh = jnp.pad(k.transpose(0, 2, 1, 3), pad)
    vh = jnp.pad(v.transpose(0, 2, 1, 3), pad)
    kb = kh.reshape(B, H, nb, MOBA_BLOCK, dh)
    vb = vh.reshape(B, H, nb, MOBA_BLOCK, dh)
    kmean = jnp.mean(kb.astype(jnp.float32), axis=3)
    rel_bias = rel_bias.astype(jnp.float32)

    gate = jnp.einsum('bhsd,bhnd->bhsn', qh.astype(jnp.float32), kmean)
    pos = jnp.arange(S)
    n_past = pos // MOBA_BLOCK
    past = jnp.arange(nb)[None, :] < n_past[:, None]
    gate = jnp.where(past, gate, -jnp.inf)
    kk = min(MOBA_TOPK, nb)
    _, sel = lax.top_k(gate, kk)
    sel_valid = jnp.arange(kk)[None, :] < jnp.minimum(n_past, MOBA_TOPK)[:, None]

    nc = S // MOBA_QCHUNK
    q_c = qh.reshape(B, H, nc, MOBA_QCHUNK, dh).transpose(2, 0, 1, 3, 4)
    sel_c = sel.reshape(B, H, nc, MOBA_QCHUNK, kk).transpose(2, 0, 1, 3, 4)
    valid_c = sel_valid.reshape(nc, MOBA_QCHUNK, kk)
    scale = HEAD_DIM ** -0.5
    off = jnp.arange(MOBA_BLOCK)
    head_idx = jnp.arange(H)[:, None, None, None]
    gather_blocks = jax.vmap(jax.vmap(lambda blocks, idx: blocks[idx]))

    def chunk_fn(args):
        c, qc, sc, vc = args
        q0 = c * MOBA_QCHUNK
        qpos = q0 + jnp.arange(MOBA_QCHUNK)
        own = q0 // MOBA_BLOCK
        k_own = lax.dynamic_slice_in_dim(kb, own, 1, axis=2)[:, :, 0]
        v_own = lax.dynamic_slice_in_dim(vb, own, 1, axis=2)[:, :, 0]
        d_own = qpos[:, None] - (own * MOBA_BLOCK + off)[None, :]
        l_own = jnp.einsum('bhqd,bhkd->bhqk', qc, k_own).astype(jnp.float32) * scale
        l_own = l_own + rel_bias[:, rel_bucket(d_own)]
        l_own = jnp.where(d_own >= 0, l_own, -jnp.inf)
        k_sel = gather_blocks(kb, sc)
        v_sel = gather_blocks(vb, sc)
        d_sel = qpos[:, None, None] - (sc[..., None] * MOBA_BLOCK + off)
        l_sel = jnp.einsum('bhqd,bhqnkd->bhqnk', qc, k_sel).astype(jnp.float32) * scale
        l_sel = l_sel + rel_bias[head_idx, rel_bucket(d_sel)]
        l_sel = jnp.where(vc[:, :, None], l_sel, -jnp.inf)
        logits = jnp.concatenate(
            [l_own, l_sel.reshape(B, H, MOBA_QCHUNK, kk * MOBA_BLOCK)], axis=-1)
        p = jax.nn.softmax(logits, axis=-1)
        p_own = p[..., :MOBA_BLOCK].astype(v.dtype)
        p_sel = p[..., MOBA_BLOCK:].reshape(B, H, MOBA_QCHUNK, kk, MOBA_BLOCK).astype(v.dtype)
        return (jnp.einsum('bhqk,bhkd->bhqd', p_own, v_own)
                + jnp.einsum('bhqnk,bhqnkd->bhqd', p_sel, v_sel))

    o = lax.map(chunk_fn, (jnp.arange(nc), q_c, sel_c, valid_c))
    return o.transpose(1, 0, 3, 2, 4).reshape(B, S, H * dh)

def causal_depthwise_conv_silu(x, w):
    C = x.shape[-1]
    y = lax.conv_general_dilated(
        x, w[:, None, :].astype(x.dtype), window_strides=(1,),
        padding=[(CONV_WIDTH - 1, 0)], dimension_numbers=('NWC', 'WIO', 'NWC'),
        feature_group_count=C)
    return jax.nn.silu(y)

def gated_deltanet(qkv, z, a, b, conv_w, A_log, dt_bias, norm_w):
    B, S, _ = qkv.shape
    H, dh, C = GDN_HEADS, HEAD_DIM, GDN_CHUNK
    nc = S // C
    qkv = causal_depthwise_conv_silu(qkv, conv_w)
    q, k, v = jnp.split(qkv, 3, axis=-1)
    q = l2_normalize(q.reshape(B, S, H, dh)) * (dh ** -0.5)
    k = l2_normalize(k.reshape(B, S, H, dh))
    v = v.reshape(B, S, H, dh).astype(jnp.float32)
    beta = jax.nn.sigmoid(b.astype(jnp.float32))
    g = -jnp.exp(A_log.astype(jnp.float32)) * jax.nn.softplus(
        a.astype(jnp.float32) + dt_bias.astype(jnp.float32))

    def to_chunks(t):
        t = jnp.moveaxis(t, 2, 1)
        return t.reshape((B, H, nc, C) + t.shape[3:])

    qc, kc, vc = to_chunks(q), to_chunks(k), to_chunks(v)
    bc = to_chunks(beta)
    g_cum = jnp.cumsum(to_chunks(g), axis=-1)
    causal = jnp.tril(jnp.ones((C, C), dtype=bool))
    strict = jnp.tril(jnp.ones((C, C), dtype=bool), k=-1)
    decay = jnp.exp(jnp.where(causal, g_cum[..., :, None] - g_cum[..., None, :], -jnp.inf))
    k_beta = kc * bc[..., None]
    m = jnp.where(strict, jnp.einsum('bhnid,bhnjd->bhnij', k_beta, kc) * decay, 0.0)
    a_mat = m + jnp.eye(C, dtype=jnp.float32)
    rhs = jnp.concatenate([vc * bc[..., None], k_beta * jnp.exp(g_cum)[..., None]], axis=-1)
    uw = lax.linalg.triangular_solve(a_mat, rhs, left_side=True, lower=True, unit_diagonal=True)
    u, w = uw[..., :dh], uw[..., dh:]
    attn_intra = jnp.einsum('bhnid,bhnjd->bhnij', qc, kc) * decay
    q_dec = qc * jnp.exp(g_cum)[..., None]
    k_dec = kc * jnp.exp(g_cum[..., -1:] - g_cum)[..., None]
    g_last = jnp.exp(g_cum[..., -1])

    def step(state, xs):
        u_c, w_c, q_c, k_c, a_c, gl = xs
        v_new = u_c - jnp.einsum('bhck,bhkv->bhcv', w_c, state)
        o = jnp.einsum('bhck,bhkv->bhcv', q_c, state) + jnp.einsum('bhcs,bhsv->bhcv', a_c, v_new)
        state = state * gl[..., None, None] + jnp.einsum('bhck,bhcv->bhkv', k_c, v_new)
        return state, o

    xs = tuple(jnp.moveaxis(t, 2, 0) for t in (u, w, q_dec, k_dec, attn_intra, g_last))
    state0 = jnp.zeros((B, H, dh, dh), dtype=jnp.float32)
    _, o = lax.scan(step, state0, xs)
    o = jnp.moveaxis(o, 0, 2).reshape(B, H, S, dh).transpose(0, 2, 1, 3)
    o = o * lax.rsqrt(jnp.mean(o * o, axis=-1, keepdims=True) + EPS) * norm_w.astype(jnp.float32)
    o = o * jax.nn.silu(z.reshape(B, S, H, dh).astype(jnp.float32))
    return o.reshape(B, S, GDN_WIDTH).astype(qkv.dtype)

def first_inputs(seed: int = 0) -> dict:
    key = jax.random.key(seed)
    ks = jax.random.split(key, 16)
    f32 = jnp.float32
    x = jax.random.normal(ks[0], (BATCH, SEQ, D_MODEL), f32)
    w_in = jax.random.normal(ks[1], (DEPTH, D_MODEL, IN_COLS), f32) * D_MODEL ** -0.5
    w_out = jax.random.normal(ks[2], (DEPTH, MIX_WIDTH, D_MODEL), f32) * MIX_WIDTH ** -0.5
    conv_w = jax.random.normal(ks[3], (DEPTH, CONV_WIDTH, 3 * GDN_WIDTH), f32) * CONV_WIDTH ** -0.5
    A_log = jnp.log(jax.random.uniform(ks[4], (DEPTH, GDN_HEADS), f32, 1.0, 16.0))
    dt = jnp.exp(jax.random.uniform(ks[5], (DEPTH, GDN_HEADS), f32, math.log(1e-3), math.log(1e-1)))
    dt_bias = dt + jnp.log(-jnp.expm1(-dt))
    gdn_norm_w = 1.0 + 0.05 * jax.random.normal(ks[6], (DEPTH, HEAD_DIM), f32)
    rel_bias = 0.5 * jax.random.normal(ks[7], (ATT_HEADS, REL_BUCKETS), f32)
    pre_mix_norm = 1.0 + 0.05 * jax.random.normal(ks[8], (DEPTH, D_MODEL), f32)
    post_mix_norm = 1.0 + 0.05 * jax.random.normal(ks[9], (DEPTH, D_MODEL), f32)
    pre_mlp_norm = 1.0 + 0.05 * jax.random.normal(ks[10], (DEPTH, D_MODEL), f32)
    post_mlp_norm = 1.0 + 0.05 * jax.random.normal(ks[11], (DEPTH, D_MODEL), f32)
    w_up = jax.random.normal(ks[12], (DEPTH, D_MODEL, D_FF), f32) * D_MODEL ** -0.5
    w_down = jax.random.normal(ks[13], (DEPTH, D_FF, D_MODEL), f32) * D_FF ** -0.5
    return {"x": x, "w_in": w_in, "w_out": w_out, "conv_w": conv_w, "A_log": A_log,
            "dt_bias": dt_bias, "gdn_norm_w": gdn_norm_w, "rel_bias": rel_bias,
            "pre_mix_norm": pre_mix_norm, "post_mix_norm": post_mix_norm,
            "pre_mlp_norm": pre_mlp_norm, "post_mlp_norm": post_mlp_norm,
            "w_up": w_up, "w_down": w_down}

def first_block(x, w_in, w_out, conv_w, A_log, dt_bias, gdn_norm_w, rel_bias,
              pre_mix_norm, post_mix_norm, pre_mlp_norm, post_mlp_norm, w_up, w_down):
    B, S, _ = x.shape
    split_points = np.cumsum(IN_SIZES)[:-1].tolist()
    for l in range(DEPTH):
        h = rms_norm(x, pre_mix_norm[l])
        proj = jnp.einsum('bsd,dc->bsc', h, w_in[l])
        att_q, att_k, att_v, gdn_qkv, gdn_z, gdn_a, gdn_b = jnp.split(proj, split_points, axis=-1)
        o_att = moba_attention(att_q.reshape(B, S, ATT_HEADS, HEAD_DIM),
                               att_k.reshape(B, S, ATT_HEADS, HEAD_DIM),
                               att_v.reshape(B, S, ATT_HEADS, HEAD_DIM), rel_bias)
        o_gdn = gated_deltanet(gdn_qkv, gdn_z, gdn_a, gdn_b, conv_w[l], A_log[l],
                               dt_bias[l], gdn_norm_w[l])
        mix = jnp.einsum('bsc,cd->bsd', jnp.concatenate([o_att, o_gdn], axis=-1), w_out[l])
        x = x + rms_norm(mix, post_mix_norm[l])
        h = rms_norm(x, pre_mlp_norm[l])
        m = jnp.einsum('bsf,fd->bsd', jnp.square(jax.nn.relu(jnp.einsum('bsd,df->bsf', h, w_up[l]))), w_down[l])
        x = x + rms_norm(m, post_mlp_norm[l])
    return x


DEPTH_2 = 2

N_MIXERS = 2

HG_HEADS = 8
HG_DK = D_MODEL // HG_HEADS
HG_DV = D_MODEL // HG_HEADS
HG_KDIM = HG_HEADS * HG_DK
HG_VDIM = HG_HEADS * HG_DV
HG_CHUNK = 64
N_HGRN = (DEPTH_2 + 1) // 2

LRU_WIDTH = D_MODEL
LRU_BLOCKS = 4
LRU_BW = LRU_WIDTH // LRU_BLOCKS
LRU_C = 8.0
N_LRU = DEPTH_2 // 2

D_FF_2 = ((8 * D_MODEL // 3 + 255) // 256) * 256


def rmsnorm(x, w):
    xf = x.astype(jnp.float32)
    y = xf * lax.rsqrt(jnp.mean(xf * xf, axis=-1, keepdims=True) + EPS) * w.astype(jnp.float32)
    return y.astype(x.dtype)

def hgrn2_mixer(h, w_in, lb, norm_w, w_out):
    B, S, _ = h.shape
    C = HG_CHUNK
    nc = S // C
    proj = h @ w_in
    q, fl, v, g = jnp.split(proj, [HG_KDIM, 2 * HG_KDIM, 2 * HG_KDIM + HG_VDIM], axis=-1)
    q = jax.nn.silu(q.astype(jnp.float32))
    fl = fl.astype(jnp.float32)
    lbv = lb.astype(jnp.float32)
    log_f = jnp.logaddexp(jnp.log(lbv), jnp.log1p(-lbv) + jax.nn.log_sigmoid(fl))
    k = (1.0 - lbv) * jax.nn.sigmoid(-fl)

    def to_chunks(t, d):
        return t.reshape(B, nc, C, HG_HEADS, d).transpose(1, 0, 3, 2, 4)

    qc = to_chunks(q, HG_DK)
    kc = to_chunks(k, HG_DK)
    vc = to_chunks(v.astype(jnp.float32), HG_DV)
    bc = jnp.cumsum(to_chunks(log_f, HG_DK), axis=3)
    causal = jnp.tril(jnp.ones((C, C), dtype=bool))[:, :, None]

    def step(state, inp):
        qb, kb, vb, bb = inp
        rel = bb[:, :, :, None, :] - bb[:, :, None, :, :]
        decay = jnp.exp(jnp.where(causal, rel, -jnp.inf))
        scores = jnp.einsum('bhtk,bhtsk,bhsk->bhts', qb, decay, kb)
        o = jnp.einsum('bhts,bhsv->bhtv', scores, vb) + jnp.einsum('bhtk,bhkv->bhtv', qb * jnp.exp(bb), state)
        b_last = bb[:, :, -1, :]
        state = jnp.exp(b_last)[..., None] * state + jnp.einsum(
            'bhsk,bhsv->bhkv', kb * jnp.exp(b_last[:, :, None, :] - bb), vb)
        return state, o

    s0 = jnp.zeros((B, HG_HEADS, HG_DK, HG_DV), jnp.float32)
    _, oc = lax.scan(step, s0, (qc, kc, vc, bc))
    o = oc.transpose(1, 0, 3, 2, 4).reshape(B, S, HG_HEADS, HG_DV)
    o = o * lax.rsqrt(jnp.mean(o * o, axis=-1, keepdims=True) + EPS) * norm_w.astype(jnp.float32)
    o = o.reshape(B, S, HG_VDIM) * jax.nn.silu(g.astype(jnp.float32))
    return o.astype(h.dtype) @ w_out

def rglru_mixer(h, w_in, conv_w, conv_b, wa, ba, wx, bx, lam, w_out):
    B, S, _ = h.shape
    proj = h @ w_in
    y, u = jnp.split(proj, [LRU_WIDTH], axis=-1)
    y = jax.nn.gelu(y.astype(jnp.float32))
    u = u.astype(jnp.float32)
    u_pad = jnp.pad(u, ((0, 0), (CONV_WIDTH - 1, 0), (0, 0)))
    cw = conv_w.astype(jnp.float32)
    uc = conv_b.astype(jnp.float32)
    for tap in range(CONV_WIDTH):
        uc = uc + u_pad[:, tap:tap + S, :] * cw[tap]
    ub = uc.reshape(B, S, LRU_BLOCKS, LRU_BW)
    r = jax.nn.sigmoid(jnp.einsum('bsnc,ncd->bsnd', ub, wa.astype(jnp.float32)).reshape(B, S, LRU_WIDTH)
                       + ba.astype(jnp.float32))
    ig = jax.nn.sigmoid(jnp.einsum('bsnc,ncd->bsnd', ub, wx.astype(jnp.float32)).reshape(B, S, LRU_WIDTH)
                        + bx.astype(jnp.float32))
    log_a = -LRU_C * r * jax.nn.softplus(-lam.astype(jnp.float32))
    a = jnp.exp(log_a)
    b_in = jnp.sqrt(-jnp.expm1(2.0 * log_a)) * (ig * uc)

    def combine(left, right):
        a1, b1 = left
        a2, b2 = right
        return a1 * a2, a2 * b1 + b2

    _, hs = lax.associative_scan(combine, (a, b_in), axis=1)
    return (hs * y).astype(h.dtype) @ w_out

def swiglu(h, w_in, w_out):
    gate, up = jnp.split(h @ w_in, [D_FF_2], axis=-1)
    return (jax.nn.silu(gate) * up) @ w_out

def second_inputs(seed: int = 0) -> dict:
    key = jax.random.key(seed)
    ks = jax.random.split(key, 24)
    f32 = jnp.float32
    D = D_MODEL

    def nrm(k, shape, fan_in):
        return jax.random.normal(k, shape, f32) * (fan_in ** -0.5)

    x = jax.random.normal(ks[0], (BATCH, SEQ, D), f32)
    norm_mix = 1.0 + 0.02 * jax.random.normal(ks[1], (DEPTH_2, D), f32)
    norm_ffn = 1.0 + 0.02 * jax.random.normal(ks[2], (DEPTH_2, D), f32)
    norm_final = 1.0 + 0.02 * jax.random.normal(ks[3], (D,), f32)

    hgrn_w_in = nrm(ks[4], (N_HGRN, D, 2 * HG_KDIM + 2 * HG_VDIM), D)
    hgrn_lb = 0.1 * jax.random.normal(ks[5], (N_HGRN + 1, HG_KDIM), f32)
    hgrn_norm = 1.0 + 0.02 * jax.random.normal(ks[6], (N_HGRN, HG_DV), f32)
    hgrn_w_out = nrm(ks[7], (N_HGRN, HG_VDIM, D), HG_VDIM)

    lru_w_in = nrm(ks[8], (N_LRU, D, 2 * LRU_WIDTH), D)
    lru_conv_w = nrm(ks[9], (N_LRU, CONV_WIDTH, LRU_WIDTH), CONV_WIDTH)
    lru_conv_b = 0.01 * jax.random.normal(ks[10], (N_LRU, LRU_WIDTH), f32)
    lru_wa = nrm(ks[11], (N_LRU, LRU_BLOCKS, LRU_BW, LRU_BW), LRU_BW)
    lru_ba = 0.01 * jax.random.normal(ks[12], (N_LRU, LRU_WIDTH), f32)
    lru_wx = nrm(ks[13], (N_LRU, LRU_BLOCKS, LRU_BW, LRU_BW), LRU_BW)
    lru_bx = 0.01 * jax.random.normal(ks[14], (N_LRU, LRU_WIDTH), f32)
    a0 = jax.random.uniform(ks[15], (N_LRU, LRU_WIDTH), f32, 0.9, 0.999)
    s = a0 ** (1.0 / LRU_C)
    lru_lambda = jnp.log(s) - jnp.log1p(-s)
    lru_w_out = nrm(ks[16], (N_LRU, LRU_WIDTH, D), LRU_WIDTH)

    ffn_w_in = nrm(ks[17], (DEPTH_2, D, 2 * D_FF_2), D)
    ffn_w_out = nrm(ks[18], (DEPTH_2, D_FF_2, D), D_FF_2)

    return {"x": x, "norm_mix": norm_mix, "norm_ffn": norm_ffn, "norm_final": norm_final,
            "hgrn_w_in": hgrn_w_in, "hgrn_lb": hgrn_lb, "hgrn_norm": hgrn_norm, "hgrn_w_out": hgrn_w_out,
            "lru_w_in": lru_w_in, "lru_conv_w": lru_conv_w, "lru_conv_b": lru_conv_b,
            "lru_wa": lru_wa, "lru_ba": lru_ba, "lru_wx": lru_wx, "lru_bx": lru_bx,
            "lru_lambda": lru_lambda, "lru_w_out": lru_w_out,
            "ffn_w_in": ffn_w_in, "ffn_w_out": ffn_w_out}

def second_block(x, norm_mix, norm_ffn, norm_final, hgrn_w_in, hgrn_lb, hgrn_norm, hgrn_w_out,
              lru_w_in, lru_conv_w, lru_conv_b, lru_wa, lru_ba, lru_wx, lru_bx, lru_lambda, lru_w_out,
              ffn_w_in, ffn_w_out):
    lb_all = jnp.cumsum(jax.nn.softmax(hgrn_lb.astype(jnp.float32), axis=0), axis=0)
    for l in range(DEPTH_2):
        j = l // N_MIXERS
        hn = rmsnorm(x, norm_mix[l])
        if l % N_MIXERS == 0:
            mix = hgrn2_mixer(hn, hgrn_w_in[j], lb_all[j], hgrn_norm[j], hgrn_w_out[j])
        else:
            mix = rglru_mixer(hn, lru_w_in[j], lru_conv_w[j], lru_conv_b[j], lru_wa[j], lru_ba[j],
                              lru_wx[j], lru_bx[j], lru_lambda[j], lru_w_out[j])
        x = x + mix
        x = x + swiglu(rmsnorm(x, norm_ffn[l]), ffn_w_in[l], ffn_w_out[l])
    return rmsnorm(x, norm_final)


def setup_inputs(seed=0):
    out = dict(first_inputs(seed))
    for name, value in second_inputs(seed + 1).items():
        if name != "x":
            out[name + "_2"] = value
    return out


def reference(
    x, w_in, w_out, conv_w, A_log, dt_bias, gdn_norm_w, rel_bias, pre_mix_norm, post_mix_norm,
    pre_mlp_norm, post_mlp_norm, w_up, w_down, norm_mix_2, norm_ffn_2, norm_final_2,
    hgrn_w_in_2, hgrn_lb_2, hgrn_norm_2, hgrn_w_out_2, lru_w_in_2, lru_conv_w_2, lru_conv_b_2,
    lru_wa_2, lru_ba_2, lru_wx_2, lru_bx_2, lru_lambda_2, lru_w_out_2, ffn_w_in_2, ffn_w_out_2,
):
    x = first_block(
        x, w_in, w_out, conv_w, A_log, dt_bias, gdn_norm_w, rel_bias, pre_mix_norm,
        post_mix_norm, pre_mlp_norm, post_mlp_norm, w_up, w_down,
    )
    return second_block(
        x, norm_mix_2, norm_ffn_2, norm_final_2, hgrn_w_in_2, hgrn_lb_2, hgrn_norm_2,
        hgrn_w_out_2, lru_w_in_2, lru_conv_w_2, lru_conv_b_2, lru_wa_2, lru_ba_2, lru_wx_2,
        lru_bx_2, lru_lambda_2, lru_w_out_2, ffn_w_in_2, ffn_w_out_2,
    )


_drawn_inputs = setup_inputs


def setup_inputs(seed=0):
    import zlib

    import numpy as np

    out = dict(_drawn_inputs(seed))
    spreads = {}
    factors = {'norm_mix_2': 3.694,
     'norm_ffn_2': 4.649,
     'norm_final_2': 8.067,
     'hgrn_lb_2': 8.0,
     'hgrn_norm_2': 7.008,
     'lru_conv_b_2': 14.595,
     'lru_ba_2': 64.0,
     'lru_bx_2': 62.279}
    for name, (base, spread) in spreads.items():
        noise = np.random.default_rng([zlib.crc32(name.encode()), seed]).standard_normal(out[name].shape)
        drawn = base * np.exp(spread * noise) if base else spread * noise
        out[name] = __import__('jax').numpy.asarray(drawn.astype(out[name].dtype))
    for name, factor in factors.items():
        out[name] = (out[name] * factor).astype(out[name].dtype)
    return out
```

```python
from contextlib import ExitStack

import numpy as np

import concourse.bass as bass
from concourse import mybir

F32 = mybir.dt.float32
F32R = mybir.dt.float32r
I32 = mybir.dt.int32
ALU = mybir.AluOpType
ACT = mybir.ActivationFunctionType
AX = mybir.AxisListType.X

P = 128
S = 256
D = 1024
KT = D // P
HD = 64
CH = 64
EPS = 1e-6
COLS = 256
NSLOT = 3
D_FF = 4096
D_FF2 = 2816

AQ, AK, AV, GQ, GK, GV, GZ, GA, GB = 0, 512, 1024, 1536, 2048, 2560, 3072, 3584, 3592

C_AQ, C_AK, C_AV, C_GQ, C_GK, C_GV, C_AB, C_Z = 0, 2, 4, 6, 8, 10, 12, 13
C_OUT = 15
C_FF = 19
FF_STEPS = D_FF // COLS
C_HF = C_FF + 2 * FF_STEPS
C_HQ, C_HV, C_HG = C_HF + 4, C_HF + 8, C_HF + 12
C_HOUT = C_HF + 16
C_FA = C_HOUT + 4
FF2_STEPS = D_FF2 // COLS
C_LU = C_FA + 3 * FF2_STEPS
C_LY = C_LU + 4
C_LA, C_LX = C_LY + 4, C_LY + 5
C_LOUT = C_LX + 1
C_FB = C_LOUT + 4
N_CHUNKS = C_FB + 3 * FF2_STEPS

VEC = {}
_at = 0
for _name, _n in (("pre_mix", 8), ("post_mix", 8), ("pre_mlp", 8), ("post_mlp", 8), ("norm_mix", 16),
                  ("norm_ffn", 16), ("final", 8), ("conv_w", 48), ("gdn_w", 1), ("lb", 16), ("hg_w", 1),
                  ("lconv_w", 32), ("lconv_b", 8), ("ba", 8), ("bx", 8), ("lam", 8)):
    VEC[_name] = _at
    _at += _n
N_VEC = _at
BIAS_W = 384


def shape_constants():
    t = np.arange(P)
    s_, t_ = t[:, None], t[None, :]
    up = []
    for l in range(7):
        m = 1 << l
        up.append((s_ // (2 * m) == t_ // (2 * m)) & ((s_ // m) % 2 == 0) & ((t_ // m) % 2 == 1))
    low = [u.T for u in up[:6]]
    ident = s_ == t_
    causal = (s_ <= t_) & (s_ // CH == t_ // CH)
    block = s_ // HD == t_ // HD
    masks = np.stack(up + low + [ident, causal, block], 1).astype(np.float32)
    sel = np.zeros((40, 12, P), np.float32)
    for h in range(8):
        for hp in range(4):
            if h // 2 == hp:
                sel[h, hp, (h % 2) * HD:(h % 2 + 1) * HD] = 1
                sel[32 + h, hp, (h % 2) * HD:(h % 2 + 1) * HD] = 1
        sel[h, 4 + h, :] = 1
    d = 255 - np.arange(BIAS_W)
    dm = np.maximum(d, 1).astype(np.float32)
    large = 16 + (np.log(dm / 16) / np.float32(np.log(128 / 16)) * 16).astype(np.int32)
    bucket = np.where(d < 16, np.maximum(d, 0), np.minimum(large, 31))
    hot = np.zeros((33, BIAS_W), np.float32)
    hot[bucket[d >= 0], np.nonzero(d >= 0)[0]] = 1
    hot[32, d < 0] = 1
    return masks, sel, hot


def build(nc, io):
    ctx = ExitStack()

    def sb(name, shape, dt=F32):
        return ctx.enter_context(nc.sbuf_tensor(name, shape, dt))

    def sem(name):
        return ctx.enter_context(nc.semaphore(name))

    with ctx:
        raw = sb("raw", [P, NSLOT, 8 * COLS])
        w_hi = sb("w_hi", [P, NSLOT, 8 * COLS], F32R)
        w_lo = sb("w_lo", [P, NSLOT, 8 * COLS], F32R)
        xT = sb("xT", [P, KT, S])
        x_hi = sb("x_hi", [P, KT, S], F32R)
        x_lo = sb("x_lo", [P, KT, S], F32R)
        h_hi = sb("h_hi", [P, 3, 2 * S], F32R)
        h_lo = sb("h_lo", [P, 3, 2 * S], F32R)
        masks = sb("masks", [P, 16, P])
        sel = sb("sel", [40, 12, P])
        hot = sb("hot", [33, BIAS_W])
        rel = sb("rel", [33, 8])
        vecs = sb("vecs", [P, N_VEC])
        gdn_rows = sb("gdn_rows", [8, 2])
        mean_mat = sb("mean_mat", [P, P])
        eps_t = sb("eps_t", [P, 1])
        one_t = sb("one_t", [P, 1])
        zeros = sb("zeros", [P, 512], mybir.dt.bfloat16)
        sd = sb("sd", [P, S])
        rstd = sb("rstd", [P, S])
        rcol = sb("rcol", [P, 2])
        reset = sb("reset", [P, S])
        rows = sb("rows", [40, 5, S])
        cols = sb("cols", [P, 8, 16])
        lbv = sb("lbv", [P, 5, 8])
        bias_row = sb("bias_row", [8, BIAS_W])
        ARENA = 17920
        arena = sb("arena", [P, ARENA])
        bank = [ctx.enter_context(nc.psum_tensor(f"bank{i}", [P, 512], F32)) for i in range(8)]
        STAT = bank[3]
        bias_dram = nc.dram_tensor("bias_dram", (8, P, BIAS_W), F32, kind="Internal").ap()

        def ar(off, *dims):
            n = int(np.prod(dims))
            assert off + n <= ARENA
            v = arena[:, off:off + n]
            if len(dims) == 1:
                return v
            names = "abc"[:len(dims)]
            return v.rearrange(f"p ({' '.join(names)}) -> p {' '.join(names)}",
                               **{c: d for c, d in zip(names[1:], dims[1:])})

        def vec(name, k):
            c = VEC[name] + k
            return vecs[:, c:c + 1]

        IDENT, CAUSAL, BLOCK = masks[:, 13, :], masks[:, 14, :], masks[:, 15, :]

        s_small = sem("s_small")
        s_const = sem("s_const")
        s_landed = [sem(f"s_landed{i}") for i in range(NSLOT)]
        s_whi = sem("s_whi")
        s_wlo = sem("s_wlo")
        s_used = sem("s_used")
        s_gate = sem("s_gate")
        s_free = sem("s_free")
        s_xhi = sem("s_xhi")
        s_xlo = sem("s_xlo")
        s_x = sem("s_x")
        s_sq, s_stat, s_sd, s_rs = sem("s_sq"), sem("s_stat"), sem("s_sd"), sem("s_rs")
        s_xin, s_bar, s_out = sem("s_xin"), sem("s_bar"), sem("s_out")
        s_h, s_hhi, s_hlo = sem("s_h"), sem("s_hhi"), sem("s_hlo")
        s_g2, s_silu = sem("s_g2"), sem("s_silu")
        s_y = sem("s_y")
        s_mT, s_ab, s_gr, s_vec = sem("s_mT"), sem("s_ab"), sem("s_gr"), sem("s_vec")
        s_bias = [sem(f"s_bias{i}") for i in range(4)]
        s_rc = [sem(f"s_rc{i}") for i in range(2)]
        named = {}

        def sg(name):
            if name not in named:
                named[name] = sem("m_" + name)
            return named[name]

        def up_view(w, c0):
            return w.rearrange("(k p) n -> p k n", p=P)[:, :, c0:c0 + COLS]

        def down_view(w, r0):
            return w[r0:r0 + COLS, :].rearrange("(k p) n -> p k n", p=P)

        def slot(t, n, shape):
            v = t[:, n % NSLOT, :]
            return v.rearrange("p (k n) -> p k n", k=8) if shape == "up" else \
                v.rearrange("p (k n) -> p k n", k=2)

        w_in, w_out, w_up, w_down = io["w_in"], io["w_out"], io["w_up"], io["w_down"]
        plan = {}
        for c, base in ((C_AQ, AQ), (C_AK, AK), (C_AV, AV), (C_GQ, GQ), (C_GK, GK), (C_GV, GV), (C_Z, GZ)):
            for j in range(2):
                plan[c + j] = ("up", w_in[0], base + j * COLS)
        for j in range(4):
            plan[C_OUT + j] = ("up", w_out[0], j * COLS)
            plan[C_HF + j] = ("up", io["hgrn_w_in_2"][0], D + j * COLS)
            plan[C_HQ + j] = ("up", io["hgrn_w_in_2"][0], j * COLS)
            plan[C_HV + j] = ("up", io["hgrn_w_in_2"][0], 2 * D + j * COLS)
            plan[C_HG + j] = ("up", io["hgrn_w_in_2"][0], 3 * D + j * COLS)
            plan[C_HOUT + j] = ("up", io["hgrn_w_out_2"][0], j * COLS)
            plan[C_LU + j] = ("up", io["lru_w_in_2"][0], D + j * COLS)
            plan[C_LY + j] = ("up", io["lru_w_in_2"][0], j * COLS)
            plan[C_LOUT + j] = ("up", io["lru_w_out_2"][0], j * COLS)
        plan[C_LA] = ("up", io["lru_wa_2"][0].rearrange("n c d -> (n c) d"), 0)
        plan[C_LX] = ("up", io["lru_wx_2"][0].rearrange("n c d -> (n c) d"), 0)

        def wait_slot_free(sp, n):
            if not isinstance(n, int) or n >= NSLOT:
                sp.wait_ge(s_wlo, n - NSLOT + 1)

        def load(sp, n, j, kind, w, c0):
            wait_slot_free(sp, n)
            if kind == "up":
                sp.dma_start(slot(raw, j, "up"), w.rearrange("(k p) n -> p k n", p=P)[:, :, bass.ds(c0, COLS)]
                             ).then_inc(s_landed[j % NSLOT], 16)
            else:
                sp.dma_start(slot(raw, j, "down"), w[bass.ds(c0, COLS), :].rearrange("(k p) n -> p k n", p=P)
                             ).then_inc(s_landed[j % NSLOT], 16)

        def landed_count(n):
            return 16 * (n // NSLOT + 1)

        def hi_part(act, n, i=None):
            d = 0 if i is None else i * 6
            act.wait_ge(s_landed[n % NSLOT], landed_count(n) + (0 if i is None else i * 32))
            if n == C_AB:
                act.wait_ge(s_ab, 16)
            if n >= NSLOT:
                act.wait_ge(s_used, n - NSLOT + 1 + d)
            nc.scalar.activation(w_hi[:, n % NSLOT, :], raw[:, n % NSLOT, :], ACT.Copy).then_inc(s_whi, 1)

        def lo_part(dve, n, i=None):
            dve.wait_ge(s_whi, n + 1 + (0 if i is None else i * 6))
            nc.vector.tensor_tensor(w_lo[:, n % NSLOT, :], raw[:, n % NSLOT, :],
                                    w_hi[:, n % NSLOT, :].bitcast(F32), ALU.subtract).then_inc(s_wlo, 1)

        AHEAD = 2

        def exists(n, i):
            return n + (6 * i if isinstance(i, int) else 0) < N_CHUNKS

        def swiglu_rounds(c):
            return (FF2_STEPS - 1) // 2 - (c == C_FB)

        def hi_ahead(act, n, i=None):
            if exists(n + AHEAD, i):
                hi_part(act, n + AHEAD, i)

        def lo_ahead(dve, n, i=None):
            if exists(n + AHEAD, i):
                lo_part(dve, n + AHEAD, i)

        def pair_mm(out, wh, wl, xh, xl, start, stop):
            nc.tensor.matmul(out, wh, xh, start=start, stop=False, skip_group_check=True)
            nc.tensor.matmul(out, wh, xl, start=False, stop=False, skip_group_check=True)
            return nc.tensor.matmul(out, wl, xh, start=False, stop=stop, skip_group_check=True)

        def gemm_feat(pe, n, u, b, prod=None, i=None, di=0, ktiles=8, ntiles=2):
            off = 0 if i is None else i * 6
            pe.wait_ge(s_wlo, n + 1 + off)
            if u >= 2:
                pe.wait_ge(s_free, u - 1 + (0 if i is None else i * di))
            wh, wl = slot(w_hi, n, "up"), slot(w_lo, n, "up")
            for t in range(ntiles):
                for k in range(ktiles):
                    if prod is not None and t == 0:
                        pe.wait_ge(s_xlo, 8 * prod + k + 1)
                    last = pair_mm(b[:, t * S:(t + 1) * S], wh[:, k, t * P:(t + 1) * P], wl[:, k, t * P:(t + 1) * P],
                                   x_hi[:, k, :], x_lo[:, k, :], k == 0, k == ktiles - 1)
            last.then_inc(s_used, 1)

        def gemm_tok(pe, n, u, b, prod=None):
            pe.wait_ge(s_wlo, n + 1)
            if u >= 2:
                pe.wait_ge(s_free, u - 1)
            wh, wl = slot(w_hi, n, "up"), slot(w_lo, n, "up")
            for t in range(2):
                o = b[:, t * COLS:(t + 1) * COLS]
                for k in range(8):
                    xh, xl = x_hi[:, k, t * P:(t + 1) * P], x_lo[:, k, t * P:(t + 1) * P]
                    last = pair_mm(o, xh, xl, wh[:, k, :], wl[:, k, :], k == 0, k == 7)
            last.then_inc(s_used, 1)

        def gemm_down(pe, n, hslot, hcount, i=None, dh=0):
            pe.wait_ge(s_wlo, n + 1 + (0 if i is None else i * 6))
            pe.wait_ge(s_hlo, hcount + (0 if i is None else i * dh))
            wh, wl = slot(w_hi, n, "down"), slot(w_lo, n, "down")
            for k in range(2):
                for t in range(KT):
                    last = pair_mm(bank[4 + t // 2][:, (t % 2) * S:(t % 2 + 1) * S],
                                   wh[:, k, t * P:(t + 1) * P], wl[:, k, t * P:(t + 1) * P],
                                   h_hi[:, hslot, k * S:(k + 1) * S], h_lo[:, hslot, k * S:(k + 1) * S],
                                   False, True)
            last.then_inc(s_used, 1)
            return last

        def bank_of(u):
            return bank[u % 2]

        def ff_bank(j):
            return (j - 1) % 3

        def x_parts_hi(act, e, src, used, w=None, ks=range(8), after=None):
            act.wait_ge(s_used, used)
            for k in ks:
                if w is None:
                    nc.scalar.activation(x_hi[:, k, :], src[:, k, :], ACT.Copy).then_inc(s_xhi, 1)
                else:
                    nc.scalar.activation(x_hi[:, k, :], src[:, k, :], ACT.Copy,
                                         scale=vec(w[0], w[1] + k)).then_inc(s_xhi, 1)

        def x_parts_lo(dve, e, src, w=None, ks=range(8)):
            for k in ks:
                dve.wait_ge(s_xhi, 8 * e + k + 1)
                if w is None:
                    nc.vector.tensor_tensor(x_lo[:, k, :], src[:, k, :], x_hi[:, k, :].bitcast(F32),
                                            ALU.subtract).then_inc(s_xlo, 1)
                else:
                    nc.vector.scalar_tensor_tensor(x_lo[:, k, :], src[:, k, :], vec(w[0], w[1] + k),
                                                   x_hi[:, k, :].bitcast(F32), ALU.mult, ALU.subtract
                                                   ).then_inc(s_xlo, 1)

        SQ = ar(0, KT, S)

        def stat_square(act, r, src):
            if r:
                act.wait_ge(s_stat, r)
            nc.scalar.activation(SQ, src, ACT.Square).then_inc(s_sq, 1)

        def stat_sum(pe, r):
            pe.wait_ge(s_sq, r + 1)
            if r:
                pe.wait_ge(s_sd, r)
            for k in range(KT):
                last = nc.tensor.matmul(STAT[:, 0:S], mean_mat[:, :], SQ[:, k, :], start=(k == 0), stop=(k == KT - 1))
            last.then_inc(s_stat, 1)

        def stat_sqrt(act, r):
            act.wait_ge(s_stat, r + 1)
            if r:
                act.wait_ge(s_rs, r)
            nc.scalar.activation(sd[:, :], STAT[:, 0:S], ACT.Sqrt, bias=eps_t[:, 0:1]).then_inc(s_sd, 1)

        def stat_recip(dve, r):
            dve.wait_ge(s_sd, r + 1)
            nc.vector.reciprocal(rstd[:, :], sd[:, :]).then_inc(s_rs, 1)
            dve.drain()

        rb2 = rstd[:, :].unsqueeze(1).to_broadcast([P, 2, S])

        def b2(b):
            return b[:, :].rearrange("p (a b) -> p a b", a=2)

        def barrier(eng, k):
            eng.drain().then_inc(s_bar, 1)
            eng.wait_ge(s_bar, 4 * (k + 1))

        xin = ar(0, 2, D)
        mixA = ar(4096, 4, S)
        a_q, a_k = ar(5120, 4, S), ar(6144, 4, S)
        a_v = ar(7168, 2, 512)
        biasM = ar(8192, 8, S)
        Lg = ar(10240, 8, 384)
        PTs = ar(2048, 2, 2, 384)
        GP = ar(13312, 12, S + 3)
        HM, HN = ar(0, 8, P), ar(1024, 8, P)
        HT, HMm = ar(2048, 8, P), ar(3072, 8, P)
        qT, kT, vT = ar(5120, 4, S), ar(6144, 4, S), ar(7168, 4, S)
        EQ, qd = ar(8192, 4, S), ar(9216, 4, S)
        kbT, kbg, kdec = ar(10240, 4, S), ar(11264, 2, 512), ar(12288, 2, 512)
        bv, AT, YB = ar(13312, 2, 512), ar(14336, 16, P), ar(16384, 2, 4, P)
        wT = ar(7168, 4, S)
        zs, St, vn, oT = ar(0, 4, S), ar(1024, 4, P), ar(2048, 2, 512), ar(3072, 4, S)
        St2 = ar(1536, 4, P)
        sqo, ro, mixG = ar(10240, 4, S), ar(16384, 4, S), ar(14336, 4, S)
        mT = ar(10240, KT, S)
        gcol, bcol, ecol, kcol, gecol = (cols[:, j, :].rearrange("p (i h) -> p i h", i=2) for j in range(5))
        nmx, sums = cols[:, 5, :], cols[:, 6, :]
        R_A, R_G, R_T, R_B, R_L = range(5)

        def heads_of(g):
            return (4 * (g // 2) + g % 2, 4 * (g // 2) + g % 2 + 2)

        HX, HB, HQ, HK = ar(0, KT, S), ar(2048, KT, S), ar(4096, KT, S), ar(6144, KT, S)
        HV = ar(8192, 2, D)
        QK = [ar(10240, KT, S), ar(12288, KT, S)]
        HAT = ar(14336, 8, 2, P)
        OFF = ar(16384, 8, P)
        HG = QK[0]
        LU = ar(0, KT, S + 3)
        UC, LY, LR, LI, LA, LE, LB = (ar(2304 + 2048 * j, KT, S) for j in range(7))
        HS = ar(0, KT, S)
        FT = ar(4096, 3, 2 * S)
        FH = ar(5632, 3, 2 * S)
        FU = ar(7168, 3, 2 * S)
        FS = ar(8704, 3, 2 * S)
        yT = ar(2048, KT, S)
        ytok = ar(4096, 2, D)

        U_W1 = 0
        U_OUT = 15
        U_FF = 19
        U_HG = U_FF + FF_STEPS
        U_HOUT = U_HG + 16
        U_FA = U_HOUT + 4
        U_LU = U_FA + 2 * FF2_STEPS
        U_LA = U_LU + 8
        U_LOUT = U_LA + 8
        U_FB = U_LOUT + 4

        def done(u):
            for first, c, n in ((U_W1, 0, C_FF + 1), (U_HG, C_HF, 22), (U_LU, C_LU, 8), (U_LOUT, C_LOUT, 6)):
                if first <= u < first + n:
                    return c + u - first + 1
            raise ValueError(u)

        block = ctx.enter_context(nc.Block())

        @block.sync
        def _(sp):
            sp.dma_start(xin, io["x"][0].rearrange("(i p) d -> p i d", p=P)).then_inc(s_xin, 16)
            sp.dma_start(masks[:, 13, :], io["masks"][:, 13, :]).then_inc(s_xin, 16)
            sp.dma_start(vecs[:, :], io["vecs"]).then_inc(s_vec, 16)
            for n in range(3):
                load(sp, n, n, *plan[n])
            sp.dma_start(masks[:, 0:13, :], io["masks"][:, 0:13, :]).then_inc(s_small, 16)
            sp.dma_start(masks[:, 14:16, :], io["masks"][:, 14:16, :]).then_inc(s_small, 16)
            sp.dma_start(sel[:, :, :], io["sel"]).then_inc(s_small, 16)
            for n in range(3, C_FF):
                if n == C_AB:
                    wait_slot_free(sp, n)
                    v = w_in[0].rearrange("(k p) n -> p k n", p=P)
                    o = slot(raw, n, "up")
                    sp.dma_start(o[:, :, 0:8], v[:, :, GA:GA + 8]).then_inc(s_landed[n % NSLOT], 16)
                    sp.dma_start(o[:, :, 32:40], v[:, :, GB:GB + 8]).then_inc(s_ab, 16)
                else:
                    load(sp, n, n, *plan[n])
            load(sp, C_FF, C_FF, "up", w_up[0], 0)
            with sp.Fori(0, (FF_STEPS - 1) // 3) as i:
                for j in range(6):
                    n = C_FF + 1 + j
                    w = w_up[0] if j % 2 == 0 else w_down[0]
                    load(sp, n + i * 6, n, "up" if j % 2 == 0 else "down", w,
                         i * (3 * COLS) + (j // 2 + 1 - j % 2) * COLS)
            load(sp, C_HF - 1, C_HF - 1, "down", w_down[0], D_FF - COLS)
            for n in range(C_HF, C_FA):
                load(sp, n, n, *plan[n])

            def swiglu_loads(c, l):
                wi, wo = io["ffn_w_in_2"][l], io["ffn_w_out_2"][l]
                load(sp, c, c, "up", wi, 0)
                load(sp, c + 1, c + 1, "up", wi, D_FF2)
                with sp.Fori(0, (FF2_STEPS - 1) // 2) as i:
                    for j in range(6):
                        n = c + 2 + j
                        st = j // 3
                        if j % 3 < 2:
                            load(sp, n + i * 6, n, "up", wi, i * (2 * COLS) + (st + 1) * COLS + (j % 3) * D_FF2)
                        else:
                            load(sp, n + i * 6, n, "down", wo, i * (2 * COLS) + st * COLS)
                n = c + 3 * FF2_STEPS - 1
                load(sp, n, n, "down", wo, D_FF2 - COLS)

            swiglu_loads(C_FA, 0)
            for n in range(C_LU, C_FB):
                load(sp, n, n, *plan[n])
            swiglu_loads(C_FB, 1)
            for i in range(2):
                sp.wait_ge(s_y, i + 1)
                sp.dma_start(io["out"][0].rearrange("(i p) d -> p i d", p=P)[:, i, :], ytok[:, i, :]
                             ).then_inc(s_out, 16)
            sp.wait_ge(s_out, 32)

        @block.gpsimd
        def _(pool):
            pool.memset(eps_t[:, :], EPS)
            pool.memset(one_t[:, :], 1.0)
            pool.memset(mean_mat[:, :], 1.0 / D)
            pool.memset(reset[:, :], 1.0)
            pool.memset(zeros[:, :], 0.0)
            pool.memset(GP[:, :, 0:3], 0.0)
            pool.drain()
            pool.memset(reset[:, :].rearrange("p (c t) -> p c t", t=CH)[:, :, 0:1], 0.0)
            pool.drain()
            pool.memset(rel[32:33, :], -1e30)
            pool.drain().then_inc(s_const, 1)
            pool.dma_start(rel[0:32, :], io["rel_t"]).then_inc(s_bias[0], 16)
            pool.dma_start(hot[:, :], io["hot"]).then_inc(s_bias[0], 16)
            pool.dma_start(gdn_rows[:, :], io["gdn_rows"]).then_inc(s_gr, 16)
            pool.wait_ge(s_bias[2], 1)
            pool.dma_start(bias_dram, bias_row[:, :].unsqueeze(1).to_broadcast([8, P, BIAS_W])
                           ).then_inc(s_bias[3], 16)
            pool.wait_ge(s_bias[3], 16)
            pool.dma_start(biasM, bass.AP(bias_dram.tensor, P - 1, [[BIAS_W - 1, P], [P * BIAS_W, 8], [1, S]])
                           ).then_inc(s_bias[3], 16)
            pool.wait_ge(s_small, 48)
            barrier(pool, 0)
            for hf in range(2):
                for l in range(1, 6):
                    e = 5 * hf + l - 1
                    if l == 1:
                        pool.wait_ge(sg("M"), hf + 1)
                    else:
                        pool.wait_ge(sg("Y"), 2 * e)
                    nc.gpsimd.tensor_tensor(HMm, HM, masks[:, 7 + l, :].unsqueeze(1).to_broadcast([P, 8, P]),
                                            ALU.mult).then_inc(sg("Mm"), 1)
            pool.wait_ge(sg("lev"), 2)
            pool.memset(St, 0.0)
            pool.drain().then_inc(sg("S"), 1)
            barrier(pool, 1)
            barrier(pool, 2)
            barrier(pool, 3)
            pool.memset(HAT, 0.0)
            pool.drain().then_inc(sg("HAT0"), 1)
            for l in range(8):
                pool.wait_ge(sg("hE"), l + 1)
                if l >= 2:
                    pool.wait_ge(sg("hS"), 4 * (l - 1))
                q = QK[l % 2]
                if l < 7:
                    m = 1 << l
                    v = lambda t: t.rearrange("p k (b e m) -> p (k b) e m", e=2, m=m)
                    nc.gpsimd.tensor_tensor(v(q)[:, :, 0, :], v(HK)[:, :, 0, :], v(HX)[:, :, 0, :], ALU.mult)
                    last = nc.gpsimd.tensor_tensor(v(q)[:, :, 1, :], v(HQ)[:, :, 1, :], v(HX)[:, :, 1, :], ALU.mult)
                else:
                    nc.gpsimd.tensor_tensor(q[:, :, 0:P], HK[:, :, 0:P], HX[:, :, 0:P], ALU.mult)
                    last = nc.gpsimd.tensor_tensor(q[:, :, P:S], HQ[:, :, P:S], HX[:, :, P:S], ALU.mult)
                pool.drain().then_inc(sg("hQK"), 1)
            barrier(pool, 4)
            barrier(pool, 5)

        @block.scalar
        def _(act):
            def copy(o, i):
                return nc.scalar.activation(o, i, ACT.Copy)

            act.wait_ge(s_const, 1)
            act.wait_ge(s_vec, 16)
            for n in range(AHEAD):
                hi_part(act, n)
            act.wait_ge(s_x, 1)
            x_parts_hi(act, 0, xT, 0, ("pre_mix", 0))
            stat_square(act, 0, xT[:, :, :])
            hi_ahead(act, 0)
            stat_sqrt(act, 0)
            act.wait_ge(s_bias[1], 1)
            copy(bias_row[:, :], bank[4][0:8, 0:BIAS_W]).then_inc(s_bias[2], 1)
            for n in range(1, C_Z):
                hi_ahead(act, n)
            act.wait_ge(sg("am"), 1)
            for h in range(8):
                for qt, (a, b) in enumerate(((0, 256), (256, 384))):
                    j = 2 * h + qt
                    last = nc.scalar.activation(Lg[:, h, a:b], Lg[:, h, a:b], ACT.Exp, bias=nmx[:, j:j + 1],
                                                accum_out=sums[:, j:j + 1])
            act.drain().then_inc(sg("ae"), 1)
            barrier(act, 0)
            for g, dst in enumerate((qT, kT, vT)):
                act.wait_ge(sg("conv"), g + 1)
                nc.scalar.activation(dst, dst, ACT.Silu).then_inc(sg("silu"), 1)
            act.drain()
            for g, dst in enumerate((qT, kT)):
                nc.scalar.activation(ar(2048 * 0 + 1024 * g, 4, S), dst, ACT.Square).then_inc(sg("gsq"), 1)
            for g in range(2):
                act.wait_ge(sg("gss"), g + 1)
                for j in range(2):
                    last = nc.scalar.activation(ar(2048 + 1024 * g + 512 * j, 2 * S), bank[4 + 2 * g + j][:, :],
                                                ACT.Ln, bias=eps_t[:, 0:1])
            act.drain()
            for g in range(2):
                nc.scalar.activation(ar(2048 + 1024 * g, 4, S), ar(2048 + 1024 * g, 4, S), ACT.Exp,
                                     scale=-0.5).then_inc(sg("grs"), 1)
            act.wait_ge(sg("ab"), 1)
            nc.scalar.activation(gdn_rows[:, 0:1], gdn_rows[:, 0:1], ACT.Exp)
            nc.scalar.activation(rows[0:8, R_T, :], rows[0:8, R_A, :], ACT.Abs)
            act.drain()
            nc.scalar.activation(rows[0:8, R_T, :], rows[0:8, R_T, :], ACT.Exp, scale=-1.0)
            act.drain()
            nc.scalar.activation(rows[0:8, R_T, :], rows[0:8, R_T, :], ACT.Ln, bias=one_t[0:8, 0:1])
            nc.scalar.activation(rows[32:40, R_B, :], rows[32:40, R_B, :], ACT.Sigmoid)
            act.drain().then_inc(sg("sp"), 1)
            act.wait_ge(sg("colT"), 1)
            copy(cols[:, 0, :], bank[4][:, 0:16])
            copy(cols[:, 1, :], bank[5][:, 0:16])
            copy(cols[:, 3, :], bank[4][:, 32:48])
            act.drain()
            nc.scalar.activation(ecol, gcol, ACT.Exp)
            nc.scalar.activation(kcol, kcol, ACT.Exp)
            act.drain().then_inc(sg("cols"), 1)
            act.wait_ge(sg("gpair"), 1)
            for j in range(2):
                nc.scalar.activation(EQ[:, 2 * j:2 * j + 2, :], b2(bank[6 + j]), ACT.Exp)
            act.drain().then_inc(sg("EQ"), 1)
            for hf in range(2):
                act.wait_ge(sg("DTx"), hf + 1)
                nc.scalar.activation(HM, HM, ACT.Exp).then_inc(sg("DTe"), 1)
                act.wait_ge(sg("Mt"), hf + 1)
                for g in range(2):
                    copy(HM[:, 4 * g:4 * g + 4, :], bank[4 + g][:, :].rearrange("p (a b) -> p a b", a=4))
                act.drain().then_inc(sg("M"), 1)
                for l in range(1, 6):
                    e = 5 * hf + l - 1
                    for g in range(2):
                        act.wait_ge(sg("Y"), 2 * e + g + 1)
                        if e:
                            act.wait_ge(sg("X"), 2 * (e - 1) + g + 1)
                        copy(YB[:, g, :, :], bank[4 + g][:, :].rearrange("p (a b) -> p a b", a=4)
                             ).then_inc(sg("Yc"), 1)
                act.wait_ge(sg("uw"), hf + 1)
                copy(wT[:, 2 * hf:2 * hf + 2, :], b2(bank[6])).then_inc(sg("uwc"), 1)
            barrier(act, 1)
            for n in (C_Z, C_Z + 1):
                hi_ahead(act, n)
            act.wait_ge(sg("z"), 1)
            nc.scalar.activation(zs, zs, ACT.Silu).then_inc(sg("zs"), 1)
            for c in range(4):
                act.wait_ge(sg("o"), c + 1)
                copy(oT[:, :, c * CH:(c + 1) * CH], bank[5][:, 0:256].rearrange("p (a b) -> p a b", a=4)
                     ).then_inc(sg("oc"), 1)
            act.drain()
            nc.scalar.activation(sqo, oT, ACT.Square).then_inc(sg("osq"), 1)
            act.wait_ge(sg("oss"), 1)
            for j in range(2):
                nc.scalar.activation(ro[:, 2 * j:2 * j + 2, :], b2(bank[6 + j]), ACT.Ln, bias=eps_t[:, 0:1],
                                     scale=1.0 / HD)
            act.drain()
            nc.scalar.activation(ro, ro, ACT.Exp, scale=-0.5).then_inc(sg("ors"), 1)
            x_parts_hi(act, 1, mixA, C_OUT, None, range(4))
            act.wait_ge(sg("mixG"), 1)
            for k in range(4):
                nc.scalar.activation(x_hi[:, 4 + k, :], mixG[:, k, :], ACT.Copy).then_inc(s_xhi, 1)
            for n in range(C_OUT, C_FF):
                hi_ahead(act, n)

            def norm_then_input(r_post, r, e, version, used, w, first):
                if r_post is not None:
                    act.wait_ge(s_mT, 1 if r_post == 1 else 2)
                    stat_square(act, r_post, mT)
                    stat_sqrt(act, r_post)
                act.wait_ge(s_x, version)
                x_parts_hi(act, e, xT, used, w)
                stat_square(act, r, xT[:, :, :])
                hi_ahead(act, first)
                stat_sqrt(act, r)

            def mlp_hi(hslot, count, i=None, d=0):
                act.wait_ge(s_h, count + (0 if i is None else i * d))
                nc.scalar.activation(h_hi[:, hslot, :], FH[:, hslot, :], ACT.Copy).then_inc(s_hhi, 1)

            norm_then_input(1, 2, 2, 2, C_FF, ("pre_mlp", 0), C_FF)
            mlp_hi(0, 1)
            with act.Fori(0, (FF_STEPS - 1) // 3) as i:
                for j in range(3):
                    n = C_FF + 1 + 2 * j
                    hi_ahead(act, n, i)
                    hi_ahead(act, n + 1, i)
                    mlp_hi((j + 1) % 3, j + 2, i, 3)
            hi_ahead(act, C_HF - 1)
            act.wait_ge(s_used, C_HF)
            for j in range(4):
                copy(mT[:, 2 * j:2 * j + 2, :], b2(bank[4 + j]))
            act.drain().then_inc(s_mT, 1)
            norm_then_input(3, 4, 3, 3, C_HF, ("norm_mix", 0), C_HF)
            barrier(act, 2)
            act.wait_ge(sg("lb"), 1)
            nc.scalar.activation(lbv[:, 2:4, :], lbv[:, 2:4, :], ACT.Exp).then_inc(sg("lbe"), 1)
            for n in range(C_HF + 1, C_HG):
                hi_ahead(act, n)
                if n == C_HF + 4:
                    act.wait_ge(sg("fl"), 1)
                    nc.scalar.activation(QK[0], HX, ACT.Sigmoid)
                    nc.scalar.activation(HK, HX, ACT.Sigmoid, scale=-1.0)
                    act.drain().then_inc(sg("sig"), 1)
                if n == C_HF + 6:
                    act.wait_ge(sg("f"), 1)
                    nc.scalar.activation(HX, QK[0], ACT.Ln).then_inc(sg("logf"), 1)
            act.wait_ge(sg("hq"), 1)
            nc.scalar.activation(HQ, HQ, ACT.Silu)
            act.drain().then_inc(sg("hqs"), 1)
            barrier(act, 3)
            for l in range(8):
                act.wait_ge(sg("hX"), l + 1)
                nc.scalar.activation(HX, HX, ACT.Exp).then_inc(sg("hE"), 1)
            act.wait_ge(sg("hS"), 32)
            for b in range(2):
                copy(OFF[:, 4 * b:4 * b + 4, :], bank[4 + b][:, :].rearrange("p (a b) -> p a b", a=4))
            act.drain().then_inc(sg("off"), 1)
            for n in range(C_HG, C_HOUT):
                hi_ahead(act, n)
            act.wait_ge(sg("hg"), 1)
            nc.scalar.activation(HG, HG, ACT.Silu).then_inc(sg("hgs"), 1)
            act.wait_ge(sg("ho"), 1)
            for b in range(4):
                copy(HX[:, 2 * b:2 * b + 2, :], b2(bank[4 + b]))
            act.drain()
            nc.scalar.activation(HB, HX, ACT.Square).then_inc(sg("hsq"), 1)
            act.wait_ge(sg("hss"), 1)
            for b in range(4):
                nc.scalar.activation(HQ[:, 2 * b:2 * b + 2, :], b2(bank[4 + b]), ACT.Ln, bias=eps_t[:, 0:1],
                                     scale=float(D // P))
            act.drain()
            nc.scalar.activation(HQ, HQ, ACT.Exp, scale=-0.5).then_inc(sg("hrs"), 1)
            act.wait_ge(sg("hm"), 1)
            x_parts_hi(act, 4, HX, C_HOUT)
            for n in range(C_HOUT, C_FA):
                hi_ahead(act, n)

            def swiglu_act(c, e, r, version, w, step0, used):
                norm_then_input(None, r, e, version, used, w, c)
                hi_ahead(act, c + 1)

                def step(k, hslot, i=None):
                    d = 0 if i is None else i * 2
                    act.wait_ge(s_g2, k + 1 + d)
                    nc.scalar.activation(FS[:, hslot, :], FT[:, hslot, :], ACT.Silu).then_inc(s_silu, 1)
                    mlp_hi(hslot, k + FF_STEPS + 1, i, 2)
                step(step0, 0)

                def two_steps(i):
                    for j in range(2):
                        n = c + 2 + 3 * j
                        for t in range(3):
                            hi_ahead(act, n + t, i)
                        step(step0 + j + 1, (j + 1) % 2, i)

                with act.Fori(0, swiglu_rounds(c)) as i:
                    two_steps(i)
                if c == C_FB:
                    two_steps(swiglu_rounds(c))
                hi_ahead(act, c + 3 * FF2_STEPS - 1)

            swiglu_act(C_FA, 5, 5, 4, ("norm_ffn", 0), 0, C_FA)
            norm_then_input(None, 6, 6, 5, C_LU, ("norm_mix", 8), C_LU)
            barrier(act, 4)
            for n in range(C_LU + 1, C_LA):
                hi_ahead(act, n)
            nc.scalar.activation(lbv[:, 3, :], vecs[:, VEC["lam"]:VEC["lam"] + 8], ACT.Abs)
            act.drain()
            nc.scalar.activation(lbv[:, 3, :], lbv[:, 3, :], ACT.Exp, scale=-1.0)
            act.drain().then_inc(sg("lam"), 1)
            act.wait_ge(sg("uc"), 1)
            x_parts_hi(act, 7, UC, C_LA)
            hi_ahead(act, C_LA)
            act.wait_ge(sg("ly"), 1)
            nc.scalar.activation(LY, LY, ACT.Gelu_apprx_tanh)
            for gate, (dst, vb) in enumerate(((LR, "ba"), (LI, "bx"))):
                for b in range(4):
                    if b < 3:
                        act.wait_ge(s_gate, 3 * gate + b + 1)
                    else:
                        act.wait_ge(s_used, C_LA + gate + 1)
                    for t in range(2):
                        last = nc.scalar.activation(dst[:, 2 * b + t, :], b2(bank_of(U_LA + b))[:, t, :],
                                                    ACT.Sigmoid, bias=vec(vb, 2 * b + t))
                    last.then_inc(s_free, 1)
                if gate == 0:
                    hi_ahead(act, C_LX)
            act.wait_ge(sg("spl"), 1)
            act.drain().then_inc(sg("ri"), 1)
            for k in range(KT):
                nc.scalar.activation(LA[:, k, :], LR[:, k, :], ACT.Exp, scale=lbv[:, 1, k:k + 1])
            for k in range(KT):
                nc.scalar.activation(LE[:, k, :], LR[:, k, :], ACT.Tanh, scale=lbv[:, 2, k:k + 1])
            act.drain()
            nc.scalar.activation(LB, LE, ACT.Ln, bias=one_t[:, 0:1])
            nc.scalar.activation(LE, LE, ACT.Sqrt, scale=2.0)
            act.drain()
            nc.scalar.activation(LB, LB, ACT.Exp, scale=-0.5)
            act.drain().then_inc(sg("ab2"), 1)
            act.wait_ge(sg("lm"), 1)
            x_parts_hi(act, 8, HS, C_LOUT)
            for n in range(C_LOUT, C_FB):
                hi_ahead(act, n)
            swiglu_act(C_FB, 9, 7, 6, ("norm_ffn", 8), FF2_STEPS, C_FB)
            act.wait_ge(s_x, 7)
            stat_square(act, 8, xT[:, :, :])
            stat_sqrt(act, 8)
            for i in range(2):
                act.wait_ge(sg("yt"), i + 1)
                for j in range(2):
                    copy(ytok[:, i, 512 * j:512 * j + 512], bank[4 + 2 * i + j][:, :])
                act.drain().then_inc(s_y, 1)
            barrier(act, 5)

        @block.tensor
        def _(pe):
            def feat(n, u, **kw):
                gemm_feat(pe, n, u, bank_of(u), **kw)

            pe.wait_ge(s_xin, 32)
            for k in range(KT):
                for i in range(2):
                    last = nc.tensor.transpose(bank[4 + k // 2][:, (k % 2) * S + i * P:(k % 2) * S + (i + 1) * P],
                                               xin[:, i, k * P:(k + 1) * P], IDENT)
                if k % 2:
                    last.then_inc(sg("xt"), 1)
            pe.wait_ge(s_bias[0], 32)
            pe.wait_ge(s_const, 1)
            pe.wait_ge(s_x, 1)
            nc.tensor.matmul(bank[4][0:8, 0:BIAS_W], rel[:, :], hot[:, :], start=True, stop=True
                             ).then_inc(s_bias[1], 1)
            feat(0, 0, prod=0)
            stat_sum(pe, 0)
            for n in range(1, C_AV):
                feat(n, n)
            pe.wait_ge(s_rs, 1)
            pe.wait_ge(s_bias[2], 1)
            for i in range(2):
                last = nc.tensor.matmul(bank[5][:, i:i + 1], rstd[0:1, i * P:(i + 1) * P], one_t[0:1, 0:1],
                                        start=True, stop=True)
            last.then_inc(s_rc[0], 1)
            for n in (C_AV, C_AV + 1):
                gemm_tok(pe, n, n, bank_of(n))
            for n in range(C_GQ, C_AB):
                feat(n, n)
            gemm_feat(pe, C_AB, C_AB, bank_of(C_AB), ntiles=1)
            pe.wait_ge(sg("aqk"), 1)
            for p in range(4):
                if p >= 2:
                    pe.wait_ge(sg("al"), p - 1)
                for h2 in range(2):
                    o = bank[4 + 2 * (p % 2) + h2]
                    r = slice(64 * h2, 64 * h2 + 64)
                    nc.tensor.matmul(o[:, 0:256], a_q[r, p, P:S], a_k[r, p, :], start=True, stop=True)
                    last = nc.tensor.matmul(o[:, 256:384], a_q[r, p, 0:P], a_k[r, p, 0:P], start=True, stop=True)
                last.then_inc(sg("as"), 1)
            pe.wait_ge(sg("ap"), 1)

            def prob_t(p):
                if p >= 2:
                    pe.wait_ge(sg("apt"), p - 1)
                for h2 in range(2):
                    h = 2 * p + h2
                    for j in range(3):
                        last = nc.tensor.transpose(bank[4 + 2 * (p % 2) + h2][:, j * P:(j + 1) * P],
                                                   Lg[:, h, j * P:(j + 1) * P], IDENT)
                last.then_inc(sg("at"), 1)

            prob_t(0)
            for p in range(4):
                if p < 3:
                    prob_t(p + 1)
                pe.wait_ge(sg("apt"), p + 1)
                for h2 in range(2):
                    h = 2 * p + h2
                    r = slice(64 * h2, 64 * h2 + 64)
                    o = bank[3 - p // 2][r, (p % 2) * S:(p % 2 + 1) * S]
                    pt = PTs[:, p % 2, h2, :]
                    v0, v1 = a_v[:, 0, h * HD:(h + 1) * HD], a_v[:, 1, h * HD:(h + 1) * HD]
                    nc.tensor.matmul(o[:, P:S], v0, pt[:, 0:P], start=True, stop=False)
                    nc.tensor.matmul(o[:, P:S], v1, pt[:, P:2 * P], start=False, stop=True)
                    last = nc.tensor.matmul(o[:, 0:P], v0, pt[:, 2 * P:3 * P], start=True, stop=True)
                last.then_inc(sg("ao"), 1)
            pe.wait_ge(s_small, 48)
            barrier(pe, 0)
            for g in range(2):
                pe.wait_ge(sg("gsq"), g + 1)
                for hp in range(4):
                    last = nc.tensor.matmul(bank[4 + 2 * g + hp // 2][:, (hp % 2) * S:(hp % 2 + 1) * S], BLOCK,
                                            ar(1024 * g, 4, S)[:, hp, :], start=True, stop=True)
                last.then_inc(sg("gss"), 1)
            pe.wait_ge(sg("grs"), 2)
            pe.wait_ge(sg("rows"), 1)
            for i in range(2):
                t = slice(i * P, (i + 1) * P)
                nc.tensor.transpose(bank[4][:, i * 8:i * 8 + 8], rows[0:8, R_G, t], IDENT[0:8, 0:8])
                nc.tensor.transpose(bank[5][:, i * 8:i * 8 + 8], rows[32:40, R_B, t], IDENT[32:40, 32:40])
                last = nc.tensor.transpose(bank[4][:, 32 + i * 8:40 + i * 8], rows[0:8, R_L, t], IDENT[0:8, 0:8])
            last.then_inc(sg("colT"), 1)
            for hp in range(4):
                last = nc.tensor.matmul(bank[6 + hp // 2][:, (hp % 2) * S:(hp % 2 + 1) * S], sel[0:8, hp, :],
                                        rows[0:8, R_G, :], start=True, stop=True)
            last.then_inc(sg("gpair"), 1)
            pe.wait_ge(sg("cols"), 1)
            pe.wait_ge(sg("qkn"), 1)
            for hp in range(4):
                last = nc.tensor.matmul(bank[4 + hp // 2][:, (hp % 2) * S:(hp % 2 + 1) * S], sel[32:40, hp, :],
                                        rows[32:40, R_B, :], start=True, stop=True)
            last.then_inc(sg("bpair"), 1)
            pe.wait_ge(sg("EQ"), 1)
            for w, src in enumerate((vT, kT)):
                if w:
                    pe.wait_ge(sg("tk"), 1)
                for i in range(2):
                    for hp in range(4):
                        last = nc.tensor.transpose(bank[6 + i][:, hp * P:(hp + 1) * P],
                                                   src[:, hp, i * P:(i + 1) * P], IDENT)
                last.then_inc(sg("tok"), 1)
            pe.wait_ge(sg("tk"), 2)
            pe.wait_ge(sg("kb"), 1)
            for hf in range(2):
                if hf:
                    pe.wait_ge(sg("lev"), 1)
                for g in range(2):
                    for a, h in enumerate(heads_of(2 * hf + g)):
                        last = nc.tensor.matmul(bank[4 + g][:, a * S:(a + 1) * S], sel[0:8, 4 + h, :],
                                                rows[0:8, R_G, :], start=True, stop=True)
                last.then_inc(sg("gb"), 1)
                pe.wait_ge(sg("DTx"), hf + 1)
                for g in range(2):
                    for dst, rhs in ((4 + g, kbT), (6 + g, qT)):
                        for a, h in enumerate(heads_of(2 * hf + g)):
                            r = slice(64 * (h % 2), 64 * (h % 2) + 64)
                            for i in range(2):
                                t = slice(i * P, (i + 1) * P)
                                q = 2 * a + i
                                last = nc.tensor.matmul(bank[dst][:, q * P:(q + 1) * P], kT[r, h // 2, t],
                                                        rhs[r, h // 2, t], start=True, stop=True)
                last.then_inc(sg("NA"), 1)
                pe.wait_ge(sg("N"), hf + 1)
                for q in range(8):
                    last = nc.tensor.transpose(bank[4 + q // 4][:, (q % 4) * P:(q % 4 + 1) * P], HN[:, q, :], IDENT)
                last.then_inc(sg("Mt"), 1)
                for l in range(1, 6):
                    e = 5 * hf + l - 1
                    pe.wait_ge(sg("Mm"), e + 1)
                    for g in range(2):
                        pe.wait_ge(sg("UT"), 2 * (e + hf) + g + 1)
                        for q in range(4):
                            last = nc.tensor.matmul(bank[4 + g][:, q * P:(q + 1) * P], HMm[:, 4 * g + q, :],
                                                    HN[:, 4 * g + q, :], start=True, stop=True)
                        last.then_inc(sg("Y"), 1)
                    for g in range(2):
                        pe.wait_ge(sg("Yc"), 2 * e + g + 1)
                        for q in range(4):
                            last = nc.tensor.matmul(bank[6 + g][:, q * P:(q + 1) * P], HT[:, 4 * g + q, :],
                                                    YB[:, g, q, :], start=True, stop=True)
                        if l < 5:
                            for q in range(4):
                                last = nc.tensor.matmul(bank[2 + g][:, q * P:(q + 1) * P], YB[:, g, q, :],
                                                        HT[:, 4 * g + q, :], start=True, stop=True)
                        last.then_inc(sg("X"), 1)
                pe.wait_ge(sg("UT"), 12 * (hf + 1))
                for i in range(2):
                    for g in range(2):
                        for a, h in enumerate(heads_of(2 * hf + g)):
                            q = 4 * g + 2 * a + i
                            hh = h - 4 * hf
                            nc.tensor.matmul(bank[4][:, i * S + hh * HD:i * S + (hh + 1) * HD], HN[:, q, :],
                                             bv[:, i, h * HD:(h + 1) * HD], start=True, stop=True)
                            last = nc.tensor.matmul(bank[6][64 * (h % 2):64 * (h % 2) + 64,
                                                            (hh // 2) * S + i * P:(hh // 2) * S + (i + 1) * P],
                                             kbg[:, i, h * HD:(h + 1) * HD], HN[:, q, :], start=True, stop=True)
                last.then_inc(sg("uw"), 1)
            barrier(pe, 1)
            for n in (C_Z, C_Z + 1):
                feat(n, n)
            for c in range(4):
                i, r = c // 2, slice(64 * (c % 2), 64 * (c % 2) + 64)
                t = slice(c * CH, (c + 1) * CH)
                pe.wait_ge(sg("S"), c + 1)
                for hp in range(4):
                    last = nc.tensor.matmul(bank[4][r, hp * P:(hp + 1) * P], wT[:, hp, t], St[:, hp, :],
                                            start=True, stop=True)
                last.then_inc(sg("wS"), 1)
                pe.wait_ge(sg("vn"), c + 1)
                if c < 3:
                    for hp in range(4):
                        last = nc.tensor.matmul(bank[6][:, hp * P:(hp + 1) * P], kdec[r, i, hp * P:(hp + 1) * P],
                                                vn[r, i, hp * P:(hp + 1) * P], start=True, stop=True)
                    last.then_inc(sg("kv"), 1)
                if c:
                    pe.wait_ge(sg("oc"), c)
                for hp in range(4):
                    nc.tensor.matmul(bank[5][:, hp * CH:(hp + 1) * CH], St[:, hp, :], qd[:, hp, t],
                                     start=True, stop=False, skip_group_check=True)
                    for h2 in range(2):
                        h = 2 * hp + h2
                        g = 2 * (h // 4) + h % 2
                        q = 4 * g + 2 * ((h % 4) // 2) + i
                        last = nc.tensor.matmul(bank[5][64 * h2:64 * h2 + 64, hp * CH:(hp + 1) * CH],
                                                vn[r, i, h * HD:(h + 1) * HD], AT[r, q, 64 * (c % 2):64 * (c % 2) + 64],
                                                start=False, stop=True, skip_group_check=True)
                last.then_inc(sg("o"), 1)
            pe.wait_ge(sg("osq"), 1)
            for hp in range(4):
                last = nc.tensor.matmul(bank[6 + hp // 2][:, (hp % 2) * S:(hp % 2 + 1) * S], BLOCK, sqo[:, hp, :],
                                        start=True, stop=True)
            last.then_inc(sg("oss"), 1)
            for j in range(4):
                feat(C_OUT + j, U_OUT + j, prod=1 if j == 0 else None)
            stat_sum(pe, 1)

            def open_acc(pe):
                for b in range(4, 8):
                    nc.tensor.matmul(bank[b][:, :], zeros[:, 0:P], zeros[:, :], start=True, stop=False,
                                     skip_group_check=True)

            gemm_feat(pe, C_FF, U_FF, bank_of(U_FF), prod=2)
            stat_sum(pe, 2)
            open_acc(pe)
            with pe.Fori(0, (FF_STEPS - 1) // 3) as i:
                for j in range(3):
                    n = C_FF + 1 + 2 * j
                    gemm_feat(pe, n, U_FF + 1 + j, bank[ff_bank(j + 1)], i=i, di=3)
                    gemm_down(pe, n + 1, j % 3, j + 1, i, 3)
            gemm_down(pe, C_HF - 1, (FF_STEPS - 1) % 3, FF_STEPS)
            stat_sum(pe, 3)
            feat(C_HF, U_HG, prod=3)
            stat_sum(pe, 4)
            barrier(pe, 2)
            for j in range(1, 8):
                feat(C_HF + j, U_HG + j)
            pe.wait_ge(s_rs, 5)
            for i in range(2):
                last = nc.tensor.matmul(bank[7][:, i:i + 1], rstd[0:1, i * P:(i + 1) * P], one_t[0:1, 0:1],
                                        start=True, stop=True)
            last.then_inc(s_rc[1], 1)
            for j in range(8, 12):
                gemm_tok(pe, C_HF + j, U_HG + j, bank_of(U_HG + j))
            barrier(pe, 3)
            for l in range(-1, 8):
                if l >= 0:
                    pe.wait_ge(sg("hQK"), l + 1)
                for b in range(4):
                    if l >= 0:
                        pe.wait_ge(sg("hC"), 4 * l + b + 1)
                    if l == 7 and b >= 2:
                        continue
                    if l == 7:
                        for q in range(4):
                            h = 4 * b + q
                            last = nc.tensor.matmul(bank[4 + b][:, q * P:(q + 1) * P], QK[1][:, h, 0:P],
                                                    QK[1][:, h, P:S], start=True, stop=True)
                    else:
                        for q in range(4):
                            h, i = 2 * b + q // 2, q % 2
                            t = slice(i * P, (i + 1) * P)
                            lhs = HK if l < 0 else QK[l % 2]
                            rhs = HQ if l < 0 else QK[l % 2]
                            last = nc.tensor.matmul(bank[4 + b][:, q * P:(q + 1) * P], lhs[:, h, t],
                                                    rhs[:, h, t], start=True, stop=True)
                    if l >= 0:
                        last.then_inc(sg("hS"), 2 if l == 7 else 1)
                    else:
                        last.then_inc(sg("hD"), 1)
            for j in range(12, 16):
                feat(C_HF + j, U_HG + j)
            pe.wait_ge(sg("off"), 1)
            pe.wait_ge(sg("hC"), 32)
            for h in range(8):
                o = bank[4 + h // 2][:, (h % 2) * S:(h % 2 + 1) * S]
                v0, v1 = HV[:, 0, h * P:(h + 1) * P], HV[:, 1, h * P:(h + 1) * P]
                nc.tensor.matmul(o[:, 0:P], v0, HAT[:, h, 0, :], start=True, stop=True)
                nc.tensor.matmul(o[:, P:S], v0, OFF[:, h, :], start=True, stop=False)
                last = nc.tensor.matmul(o[:, P:S], v1, HAT[:, h, 1, :], start=False, stop=True)
            last.then_inc(sg("ho"), 1)
            pe.wait_ge(sg("hsq"), 1)
            for h in range(8):
                last = nc.tensor.matmul(bank[4 + h // 2][:, (h % 2) * S:(h % 2 + 1) * S], mean_mat[:, :],
                                        HB[:, h, :], start=True, stop=True)
            last.then_inc(sg("hss"), 1)
            for j in range(4):
                feat(C_HOUT + j, U_HOUT + j, prod=4 if j == 0 else None)

            def swiglu_pe(c, u, e, r, step0):
                for j in range(2):
                    feat(c + j, u + j, prod=e if j == 0 else None)
                    if j == 0:
                        stat_sum(pe, r)
                open_acc(pe)
                h0 = FF_STEPS + step0
                with pe.Fori(0, (FF2_STEPS - 1) // 2) as i:
                    for j in range(2):
                        n = c + 2 + 3 * j
                        for t in range(2):
                            uu = u + 2 + 2 * j + t
                            gemm_feat(pe, n + t, uu, bank_of(uu), i=i, di=4)
                        gemm_down(pe, n + 2, j % 2, h0 + j + 1, i, 2)
                gemm_down(pe, c + 3 * FF2_STEPS - 1, (FF2_STEPS - 1) % 2, h0 + FF2_STEPS)

            swiglu_pe(C_FA, U_FA, 5, 5, 0)
            feat(C_LU, U_LU, prod=6)
            stat_sum(pe, 6)
            barrier(pe, 4)
            for j in range(1, 8):
                feat(C_LU + j, U_LU + j)
            for gate in range(2):
                n = C_LA + gate
                pe.wait_ge(s_wlo, n + 1)
                wh, wl = slot(w_hi, n, "up"), slot(w_lo, n, "up")
                if gate == 0:
                    pe.wait_ge(s_xlo, 64)
                for b in range(4):
                    u = U_LA + 4 * gate + b
                    pe.wait_ge(s_free, u if (gate == 0 and b == 0) else u - 1)
                    for t in range(2):
                        for k in range(2):
                            last = pair_mm(bank_of(u)[:, t * S:(t + 1) * S], wh[:, 2 * b + k, t * P:(t + 1) * P],
                                           wl[:, 2 * b + k, t * P:(t + 1) * P], x_hi[:, 2 * b + k, :],
                                           x_lo[:, 2 * b + k, :], k == 0, k == 1)
                    last.then_inc(s_used if b == 3 else s_gate, 1)
            for j in range(4):
                if j == 0:
                    pe.wait_ge(s_free, U_LOUT)
                feat(C_LOUT + j, U_LOUT + j, prod=8 if j == 0 else None)
            swiglu_pe(C_FB, U_FB, 9, 7, FF2_STEPS)
            stat_sum(pe, 8)
            pe.wait_ge(sg("y"), 1)
            for i in range(2):
                for k in range(KT):
                    last = nc.tensor.transpose(bank[4 + 2 * i + k // 4][:, (k % 4) * P:(k % 4 + 1) * P],
                                               yT[:, k, i * P:(i + 1) * P], IDENT)
                last.then_inc(sg("yt"), 1)
            barrier(pe, 5)

        @block.vector
        def _(dve):
            V = nc.vector

            def fence():
                dve.drain()

            def evac_scaled(u, dst):
                dve.wait_ge(s_used, done(u))
                V.tensor_tensor(dst, b2(bank_of(u)), rb2, ALU.mult).then_inc(s_free, 1)

            def evac_tok(u, dst):
                dve.wait_ge(s_used, done(u))
                for i in range(2):
                    last = V.tensor_scalar(dst[:, i, :], bank_of(u)[:, i * COLS:(i + 1) * COLS], rcol[:, i:i + 1],
                                           None, ALU.mult)
                last.then_inc(s_free, 1)

            def add_result(dve, u, j):
                dve.wait_ge(s_used, done(u))
                x = xT[:, 2 * j:2 * j + 2, :]
                V.tensor_tensor(x, x, b2(bank_of(u)), ALU.add).then_inc(s_free, 1)

            for k in range(4):
                dve.wait_ge(sg("xt"), k + 1)
                last = V.tensor_copy(xT[:, 2 * k:2 * k + 2, :], b2(bank[4 + k]))
            last.then_inc(s_x, 1)
            dve.wait_ge(s_vec, 16)
            lo_part(dve, 0)
            x_parts_lo(dve, 0, xT, ("pre_mix", 0))
            lo_part(dve, 1)
            lo_ahead(dve, 0)
            stat_recip(dve, 0)
            dve.wait_ge(s_const, 1)
            dsts = {}
            for j in range(2):
                dsts[C_AQ + j] = a_q[:, 2 * j:2 * j + 2, :]
                dsts[C_AK + j] = a_k[:, 2 * j:2 * j + 2, :]
            for g in range(3):
                for j in range(2):
                    dsts[C_GQ + 2 * g + j] = GP[:, 4 * g + 2 * j:4 * g + 2 * j + 2, 3:3 + S]
            for n in range(0, C_AB + 1):
                if n:
                    lo_ahead(dve, n)
                if n in dsts:
                    evac_scaled(n, dsts[n])
                elif n in (C_AV, C_AV + 1):
                    if n == C_AV:
                        dve.wait_ge(s_rc[0], 1)
                        V.tensor_copy(rcol[:, :], bank[5][:, 0:2])
                        fence()
                    evac_tok(n, a_v[:, :, (n - C_AV) * COLS:(n - C_AV + 1) * COLS])
                elif n == C_AB:
                    dve.wait_ge(s_used, n + 1)
                    dve.wait_ge(s_gr, 16)
                    b = bank_of(n)
                    V.tensor_tensor(rows[0:8, R_A, :], b[0:8, 0:S], rstd[0:8, :], ALU.mult)
                    V.tensor_tensor(rows[32:40, R_B, :], b[32:40, 0:S], rstd[32:40, :], ALU.mult
                                    ).then_inc(s_free, 1)
                    fence()
                    V.tensor_scalar(rows[0:8, R_A, :], rows[0:8, R_A, :], gdn_rows[:, 1:2], None, ALU.add)
            dve.drain().then_inc(sg("aqk"), 1)
            dve.wait_ge(s_bias[3], 32)
            for p in range(4):
                dve.wait_ge(sg("as"), p + 1)
                for h2 in range(2):
                    b, h = bank[4 + 2 * (p % 2) + h2], 2 * p + h2
                    V.scalar_tensor_tensor(Lg[:, h, 0:256], b[:, 0:256], HD ** -0.5, biasM[:, h, :],
                                           ALU.mult, ALU.add)
                    last = V.scalar_tensor_tensor(Lg[:, h, 256:384], b[:, 256:384], HD ** -0.5,
                                                  biasM[:, h, P:S], ALU.mult, ALU.add)
                last.then_inc(sg("al"), 1)
            fence()
            mx2 = nmx.rearrange("p (h t) -> p h t", t=2)
            V.tensor_reduce(mx2[:, :, 0:1], Lg[:, :, 0:256], AX, ALU.max)
            V.tensor_reduce(mx2[:, :, 1:2], Lg[:, :, 256:384], AX, ALU.max)
            fence()
            V.tensor_scalar(nmx, nmx, -1.0, None, ALU.mult)
            dve.drain().then_inc(sg("am"), 1)
            dve.wait_ge(sg("ae"), 1)
            V.reciprocal(sums, sums)
            fence()
            sm2 = sums.rearrange("p (h t) -> p h t", t=2)
            V.tensor_tensor(Lg[:, :, 0:256], Lg[:, :, 0:256], sm2[:, :, 0:1].to_broadcast([P, 8, 256]), ALU.mult)
            V.tensor_tensor(Lg[:, :, 256:384], Lg[:, :, 256:384], sm2[:, :, 1:2].to_broadcast([P, 8, P]), ALU.mult)
            dve.drain().then_inc(sg("ap"), 1)
            for p in range(4):
                dve.wait_ge(sg("at"), p + 1)
                if p >= 2:
                    dve.wait_ge(sg("ao"), p - 1)
                for h2 in range(2):
                    last = V.tensor_copy(PTs[:, p % 2, h2, :], bank[4 + 2 * (p % 2) + h2][:, 0:384])
                last.then_inc(sg("apt"), 1)
            for j in range(2):
                dve.wait_ge(sg("ao"), 2 * j + 2)
                V.tensor_copy(mixA[:, 2 * j:2 * j + 2, :], b2(bank[3 - j]))
            dve.wait_ge(s_small, 48)
            barrier(dve, 0)
            for g, dst in enumerate((qT, kT, vT)):
                for k in range(4):
                    x = GP[:, 4 * g + k, :]
                    V.tensor_scalar(dst[:, k, :], x[:, 0:S], vec("conv_w", 4 * g + k), None, ALU.mult)
                for tap in range(1, 4):
                    fence()
                    for k in range(4):
                        x = GP[:, 4 * g + k, :]
                        V.scalar_tensor_tensor(dst[:, k, :], x[:, tap:tap + S], vec("conv_w", 12 * tap + 4 * g + k),
                                               dst[:, k, :], ALU.mult, ALU.add)
                dve.drain().then_inc(sg("conv"), 1)
            dve.drain().then_inc(sg("ab"), 1)
            dve.wait_ge(sg("silu"), 3)
            dve.wait_ge(sg("gsq"), 2)
            for g, dst in enumerate((qT, kT)):
                dve.wait_ge(sg("grs"), g + 1)
                V.scalar_tensor_tensor(dst, dst, HD ** -0.5 if g == 0 else 1.0, ar(2048 + 1024 * g, 4, S),
                                       ALU.mult, ALU.mult)
            fence()
            dve.wait_ge(sg("sp"), 1)
            V.scalar_tensor_tensor(rows[0:8, R_A, :], rows[0:8, R_A, :], 0.0, rows[0:8, R_T, :], ALU.max, ALU.add)
            fence()
            V.tensor_scalar(rows[0:8, R_A, :], rows[0:8, R_A, :], gdn_rows[:, 0:1], -1.0, ALU.mult, ALU.mult)
            fence()
            V.tensor_tensor_scan(rows[0:8, R_G, :], reset[0:8, :], rows[0:8, R_A, :], 0.0, ALU.mult, ALU.add)
            fence()
            rg = rows[0:8, R_G, :].rearrange("p (c t) -> p c t", t=CH)
            V.tensor_tensor(rows[0:8, R_L, :].rearrange("p (c t) -> p c t", t=CH),
                            rg[:, :, CH - 1:CH].to_broadcast([8, 4, CH]), rg, ALU.subtract)
            dve.drain().then_inc(sg("rows"), 1)
            dve.drain().then_inc(sg("qkn"), 1)
            dve.wait_ge(sg("bpair"), 1)
            for j in range(2):
                V.tensor_tensor(kbT[:, 2 * j:2 * j + 2, :], kT[:, 2 * j:2 * j + 2, :], b2(bank[4 + j]), ALU.mult)
            dve.drain().then_inc(sg("kb"), 1)
            dve.wait_ge(sg("EQ"), 1)
            V.tensor_tensor(qd, qT, EQ, ALU.mult)
            dve.wait_ge(sg("cols"), 1)
            V.tensor_tensor(gecol, bcol, ecol, ALU.mult)
            fence()

            def col64(c, i):
                return c[:, i, :].unsqueeze(2).to_broadcast([P, 8, HD])

            def h64(t):
                return t.rearrange("p (h d) -> p h d", d=HD)
            dve.wait_ge(sg("tok"), 1)
            for i in range(2):
                V.tensor_tensor(h64(bv[:, i, :]), h64(bank[6 + i][:, :]), col64(bcol, i), ALU.mult)
            dve.drain().then_inc(sg("tk"), 1)
            dve.wait_ge(sg("tok"), 2)
            for i in range(2):
                V.tensor_tensor(h64(kbg[:, i, :]), h64(bank[6 + i][:, :]), col64(gecol, i), ALU.mult)
                V.tensor_tensor(h64(kdec[:, i, :]), h64(bank[6 + i][:, :]), col64(kcol, i), ALU.mult)
            dve.drain().then_inc(sg("tk"), 1)
            i4 = IDENT.unsqueeze(1).to_broadcast([P, 4, P])
            for hf in range(2):
                dve.wait_ge(sg("gb"), hf + 1)
                for g in range(2):
                    for a, h in enumerate(heads_of(2 * hf + g)):
                        for i in range(2):
                            V.tensor_scalar(HM[:, 4 * g + 2 * a + i, :],
                                            bank[4 + g][:, a * S + i * P:a * S + (i + 1) * P],
                                            gcol[:, i, h:h + 1], 0.0, ALU.subtract, ALU.min)
                dve.drain().then_inc(sg("DTx"), 1)
                dve.wait_ge(sg("DTe"), hf + 1)
                V.tensor_tensor(HM, HM, CAUSAL.unsqueeze(1).to_broadcast([P, 8, P]), ALU.mult)
                fence()
                dve.wait_ge(sg("NA"), hf + 1)
                for g in range(2):
                    m = HM[:, 4 * g:4 * g + 4, :]
                    V.tensor_tensor(HN[:, 4 * g:4 * g + 4, :], bank[4 + g][:, :].rearrange("p (a b) -> p a b", a=4),
                                    m, ALU.mult)
                    V.tensor_tensor(AT[:, 8 * hf + 4 * g:8 * hf + 4 * g + 4, :],
                                    bank[6 + g][:, :].rearrange("p (a b) -> p a b", a=4), m, ALU.mult)
                dve.drain().then_inc(sg("N"), 1)
                dve.wait_ge(sg("M"), hf + 1)
                for g in range(2):
                    s4 = slice(4 * g, 4 * g + 4)
                    V.tensor_tensor(HN[:, s4, :], HN[:, s4, :], masks[:, 0, :].unsqueeze(1).to_broadcast([P, 4, P]),
                                    ALU.mult)
                    V.tensor_tensor(HT[:, s4, :], HM[:, s4, :], masks[:, 7, :].unsqueeze(1).to_broadcast([P, 4, P]),
                                    ALU.mult)
                    fence()
                    V.tensor_tensor(HN[:, s4, :], i4, HN[:, s4, :], ALU.subtract)
                    V.tensor_tensor(HT[:, s4, :], i4, HT[:, s4, :], ALU.subtract)
                    dve.drain().then_inc(sg("UT"), 1)
                for l in range(1, 6):
                    e = 5 * hf + l - 1
                    for g in range(2):
                        s4 = slice(4 * g, 4 * g + 4)
                        dve.wait_ge(sg("X"), 2 * e + g + 1)
                        V.tensor_tensor(HN[:, s4, :], HN[:, s4, :],
                                        bank[6 + g][:, :].rearrange("p (a b) -> p a b", a=4), ALU.subtract)
                        if l < 5:
                            V.tensor_tensor(HT[:, s4, :], HT[:, s4, :],
                                            bank[2 + g][:, :].rearrange("p (a b) -> p a b", a=4), ALU.subtract)
                        dve.drain().then_inc(sg("UT"), 1)
                dve.wait_ge(sg("uw"), hf + 1)
                for i in range(2):
                    V.tensor_copy(bv[:, i, 256 * hf:256 * hf + 256], bank[4][:, i * S:(i + 1) * S])
                dve.wait_ge(sg("uwc"), hf + 1)
                dve.drain().then_inc(sg("lev"), 1)
            barrier(dve, 1)
            for j in range(2):
                lo_ahead(dve, C_Z + j)
                evac_scaled(C_Z + j, zs[:, 2 * j:2 * j + 2, :])
            dve.drain().then_inc(sg("z"), 1)
            for c in range(4):
                i, r = c // 2, slice(64 * (c % 2), 64 * (c % 2) + 64)
                dve.wait_ge(sg("wS"), c + 1)
                V.tensor_tensor(vn[r, i, :], bv[r, i, :], bank[4][r, :], ALU.subtract).then_inc(sg("vn"), 1)
                if c < 3:
                    gl = EQ[:, :, c * CH + CH - 1:c * CH + CH]
                    dve.wait_ge(sg("kv"), c + 1)
                    if c == 0:
                        dve.wait_ge(sg("S"), 1)
                    for h2 in range(2):
                        hr = slice(64 * h2, 64 * h2 + 64)
                        V.tensor_tensor(St2[hr, :, hr], St[hr, :, hr], gl[hr, :, :].to_broadcast([64, 4, HD]), ALU.mult)
                    fence()
                    dve.wait_ge(sg("o"), c + 1)
                    for h2 in range(2):
                        hr = slice(64 * h2, 64 * h2 + 64)
                        V.tensor_tensor(St[hr, :, hr], St2[hr, :, hr],
                                        bank[6][hr, :].rearrange("p (a b) -> p a b", a=4)[:, :, hr], ALU.add)
                    dve.drain().then_inc(sg("S"), 1)
            dve.wait_ge(sg("ors"), 1)
            dve.wait_ge(sg("zs"), 1)
            V.scalar_tensor_tensor(mixG, oT, vec("gdn_w", 0), ro, ALU.mult, ALU.mult)
            fence()
            V.tensor_tensor(mixG, mixG, zs, ALU.mult)
            dve.drain().then_inc(sg("mixG"), 1)
            x_parts_lo(dve, 1, mixA, None, range(4))
            for k in range(4):
                dve.wait_ge(s_xhi, 8 + 4 + k + 1)
                V.tensor_tensor(x_lo[:, 4 + k, :], mixG[:, k, :], x_hi[:, 4 + k, :].bitcast(F32), ALU.subtract
                                ).then_inc(s_xlo, 1)
            for j in range(4):
                lo_ahead(dve, C_OUT + j)
                dve.wait_ge(s_used, done(U_OUT + j))
                V.tensor_copy(mT[:, 2 * j:2 * j + 2, :], b2(bank_of(U_OUT + j))).then_inc(s_free, 1)
            dve.drain().then_inc(s_mT, 1)

            def add_normed(r, w):
                stat_recip(dve, r)
                for k in range(KT):
                    V.scalar_tensor_tensor(mT[:, k, :], mT[:, k, :], vec(w, k), rstd[:, :], ALU.mult, ALU.mult)
                fence()
                V.tensor_tensor(xT[:, :, :], xT[:, :, :], mT, ALU.add)
                dve.drain().then_inc(s_x, 1)

            def mlp_lo(hslot, count, i=None, d=0):
                dve.wait_ge(s_hhi, count + (0 if i is None else i * d))
                V.tensor_tensor(h_lo[:, hslot, :], FH[:, hslot, :], h_hi[:, hslot, :].bitcast(F32), ALU.subtract
                                ).then_inc(s_hlo, 1)

            def relu2(n, b, hslot, i=None):
                dve.wait_ge(s_used, n + 1 + (0 if i is None else i * 6))
                ft = FT[:, hslot, :]
                V.tensor_tensor(ft.rearrange("p (a b) -> p a b", a=2), b2(b), rb2, ALU.mult).then_inc(s_free, 1)
                fence()
                V.scalar_tensor_tensor(FH[:, hslot, :], ft, 0.0, ft, ALU.max, ALU.mult).then_inc(s_h, 1)

            add_normed(1, "post_mix")
            x_parts_lo(dve, 2, xT, ("pre_mlp", 0))
            lo_ahead(dve, C_FF)
            stat_recip(dve, 2)
            relu2(C_FF, bank_of(U_FF), 0)
            mlp_lo(0, 1)
            with dve.Fori(0, (FF_STEPS - 1) // 3) as i:
                for j in range(3):
                    n = C_FF + 1 + 2 * j
                    lo_ahead(dve, n, i)
                    relu2(n, bank[ff_bank(j + 1)], (j + 1) % 3, i)
                    lo_ahead(dve, n + 1, i)
                    mlp_lo((j + 1) % 3, j + 2, i, 3)
            lo_ahead(dve, C_HF - 1)
            dve.wait_ge(s_mT, 2)
            add_normed(3, "post_mlp")
            x_parts_lo(dve, 3, xT, ("norm_mix", 0))
            lo_ahead(dve, C_HF)
            stat_recip(dve, 4)
            barrier(dve, 2)
            l0, l1 = vecs[:, VEC["lb"]:VEC["lb"] + 8], vecs[:, VEC["lb"] + 8:VEC["lb"] + 16]
            LBV, OML = lbv[:, 0, :], lbv[:, 4, :]
            V.tensor_tensor(lbv[:, 1, :], l0, l1, ALU.max)
            fence()
            V.tensor_tensor(lbv[:, 2, :], l0, lbv[:, 1, :], ALU.subtract)
            V.tensor_tensor(lbv[:, 3, :], l1, lbv[:, 1, :], ALU.subtract)
            dve.drain().then_inc(sg("lb"), 1)
            for j in range(8):
                if j:
                    lo_ahead(dve, C_HF + j)
                evac_scaled(U_HG + j, (HX if j < 4 else HQ)[:, 2 * (j % 4):2 * (j % 4) + 2, :])
                if j == 3:
                    dve.drain().then_inc(sg("fl"), 1)
                    dve.wait_ge(sg("lbe"), 1)
                    V.tensor_tensor(lbv[:, 1, :], lbv[:, 2, :], lbv[:, 3, :], ALU.add)
                    fence()
                    V.reciprocal(lbv[:, 1, :], lbv[:, 1, :])
                    fence()
                    V.tensor_tensor(LBV, lbv[:, 2, :], lbv[:, 1, :], ALU.mult)
                    V.tensor_tensor(OML, lbv[:, 3, :], lbv[:, 1, :], ALU.mult)
                    fence()
                if j == 4:
                    dve.wait_ge(sg("sig"), 1)
                    for k in range(KT):
                        V.tensor_scalar(QK[0][:, k, :], QK[0][:, k, :], OML[:, k:k + 1], LBV[:, k:k + 1],
                                        ALU.mult, ALU.add)
                    dve.drain().then_inc(sg("f"), 1)
                    for k in range(KT):
                        V.tensor_scalar(HK[:, k, :], HK[:, k, :], OML[:, k:k + 1], None, ALU.mult)
                if j == 6:
                    dve.wait_ge(sg("logf"), 1)
                    for k in range(KT):
                        V.tensor_tensor_scan(HB[:, k, :], reset[:, :], HX[:, k, :], 0.0, ALU.mult, ALU.add)
            dve.drain().then_inc(sg("hq"), 1)
            dve.wait_ge(s_rc[1], 1)
            V.tensor_copy(rcol[:, :], bank[7][:, 0:2])
            fence()
            for j in range(4):
                lo_ahead(dve, C_HV + j)
                evac_tok(U_HG + 8 + j, HV[:, :, j * COLS:(j + 1) * COLS])
            barrier(dve, 3)

            def exps(l):
                if l:
                    dve.wait_ge(sg("hQK"), l)
                if l < 6:
                    m = 1 << l
                    x = HX.rearrange("p k (b e m) -> p (k b) e m", e=2, m=m)
                    b = HB.rearrange("p k (b e m) -> p (k b) e m", e=2, m=m)
                    nb = KT * S // (2 * m)
                    ref = b[:, :, 0, m - 1:m].to_broadcast([P, nb, m])
                    V.tensor_tensor(x[:, :, 1, :], b[:, :, 1, :], ref, ALU.subtract)
                    V.tensor_tensor(x[:, :, 0, :], ref, b[:, :, 0, :], ALU.subtract)
                else:
                    x = HX.rearrange("p k (c t) -> p k c t", t=CH)
                    b = HB.rearrange("p k (c t) -> p k c t", t=CH)

                    def last(c):
                        return b[:, :, c, CH - 1:CH].to_broadcast([P, KT, CH])
                    if l == 6:
                        for c in (0, 2):
                            V.tensor_tensor(x[:, :, c, :], last(c), b[:, :, c, :], ALU.subtract)
                            V.tensor_copy(x[:, :, c + 1, :], b[:, :, c + 1, :])
                    else:
                        V.tensor_tensor(x[:, :, 0, :], last(0), b[:, :, 0, :], ALU.subtract)
                        V.tensor_tensor(x[:, :, 1, :], last(1), b[:, :, 1, :], ALU.subtract)
                        V.tensor_copy(x[:, :, 2, :], b[:, :, 2, :])
                        V.tensor_tensor(x[:, :, 3, :], b[:, :, 3, :], last(2), ALU.add)
                        fence()
                        V.tensor_tensor(x[:, :, 0, :], x[:, :, 0, :], last(1), ALU.add)
                dve.drain().then_inc(sg("hX"), 1)

            def place(l, semname, first):
                m = (IDENT if l < 0 else masks[:, l, :]).bitcast(I32).unsqueeze(1).to_broadcast([P, 4, P])
                for b in range(4):
                    dve.wait_ge(sg(semname), first + b + 1)
                    V.copy_predicated(HAT[:, 2 * b:2 * b + 2, :, :].rearrange("p h i t -> p (h i) t"), m,
                                      bank[4 + b][:, :].rearrange("p (a b) -> p a b", a=4)).then_inc(sg("hC"), 1)
                fence()

            exps(0)
            dve.wait_ge(sg("HAT0"), 1)
            place(-1, "hD", 0)
            for l in range(7):
                exps(l + 1)
                place(l, "hS", 4 * l)
            for j in range(4):
                lo_ahead(dve, C_HG + j)
                evac_scaled(U_HG + 12 + j, HG[:, 2 * j:2 * j + 2, :])
            dve.drain().then_inc(sg("hg"), 1)
            dve.wait_ge(sg("hrs"), 1)
            dve.wait_ge(sg("hgs"), 1)
            V.scalar_tensor_tensor(HX, HX, vec("hg_w", 0), HQ, ALU.mult, ALU.mult)
            fence()
            V.tensor_tensor(HX, HX, HG, ALU.mult)
            dve.drain().then_inc(sg("hm"), 1)
            x_parts_lo(dve, 4, HX)
            for j in range(4):
                lo_ahead(dve, C_HOUT + j)
                add_result(dve, U_HOUT + j, j)
            dve.drain().then_inc(s_x, 1)

            def swiglu_dve(c, u, e, r, w, step0):
                x_parts_lo(dve, e, xT, w)
                lo_ahead(dve, c)
                stat_recip(dve, r)
                h0 = FF_STEPS + step0

                def gate(n, uu, hslot, i=None):
                    dve.wait_ge(s_used, n + 1 + (0 if i is None else i * 6))
                    V.tensor_tensor(FT[:, hslot, :].rearrange("p (a b) -> p a b", a=2), b2(bank_of(uu)), rb2,
                                    ALU.mult).then_inc(s_free, 1)
                    dve.drain().then_inc(s_g2, 1)

                def up(n, uu, hslot, i=None):
                    dve.wait_ge(s_used, n + 1 + (0 if i is None else i * 6))
                    V.tensor_tensor(FU[:, hslot, :].rearrange("p (a b) -> p a b", a=2), b2(bank_of(uu)), rb2,
                                    ALU.mult).then_inc(s_free, 1)
                    fence()

                def hidden(k, hslot, i=None):
                    dve.wait_ge(s_silu, k + 1 + (0 if i is None else i * 2))
                    V.tensor_tensor(FH[:, hslot, :], FS[:, hslot, :], FU[:, hslot, :], ALU.mult).then_inc(s_h, 1)

                gate(c, u, 0)
                lo_ahead(dve, c + 1)
                up(c + 1, u + 1, 0)
                hidden(step0, 0)
                mlp_lo(0, h0 + 1)

                def two_steps(i):
                    for j in range(2):
                        n, uu, hs = c + 2 + 3 * j, u + 2 + 2 * j, (j + 1) % 2
                        lo_ahead(dve, n, i)
                        gate(n, uu, hs, i)
                        lo_ahead(dve, n + 1, i)
                        up(n + 1, uu + 1, hs, i)
                        hidden(step0 + j + 1, hs, i)
                        lo_ahead(dve, n + 2, i)
                        mlp_lo(hs, h0 + j + 2, i, 2)

                with dve.Fori(0, swiglu_rounds(c)) as i:
                    two_steps(i)
                if c == C_FB:
                    two_steps(swiglu_rounds(c))
                lo_ahead(dve, c + 3 * FF2_STEPS - 1)

            def add_acc(chunks):
                dve.wait_ge(s_used, chunks)
                for b in range(4):
                    x = xT[:, 2 * b:2 * b + 2, :]
                    V.tensor_tensor(x, x, b2(bank[4 + b]), ALU.add)
                dve.drain().then_inc(s_x, 1)

            swiglu_dve(C_FA, U_FA, 5, 5, ("norm_ffn", 0), 0)
            add_acc(C_LU)
            x_parts_lo(dve, 6, xT, ("norm_mix", 8))
            lo_ahead(dve, C_LU)
            stat_recip(dve, 6)
            barrier(dve, 4)
            V.memset(LU[:, :, 0:3], 0.0)
            for j in range(8):
                if j:
                    lo_ahead(dve, C_LU + j)
                if j < 4:
                    evac_scaled(U_LU + j, LU[:, 2 * j:2 * j + 2, 3:3 + S])
                    fence()
                    for k in (2 * j, 2 * j + 1):
                        V.tensor_scalar(UC[:, k, :], LU[:, k, 0:S], vec("lconv_w", k), vec("lconv_b", k),
                                        ALU.mult, ALU.add)
                    for tap in range(1, 4):
                        fence()
                        for k in (2 * j, 2 * j + 1):
                            V.scalar_tensor_tensor(UC[:, k, :], LU[:, k, tap:tap + S], vec("lconv_w", 8 * tap + k),
                                                   UC[:, k, :], ALU.mult, ALU.add)
                    if j == 3:
                        dve.drain().then_inc(sg("uc"), 1)
                else:
                    evac_scaled(U_LU + j, LY[:, 2 * (j - 4):2 * (j - 4) + 2, :])
            dve.drain().then_inc(sg("ly"), 1)
            dve.wait_ge(sg("lam"), 1)
            y, z, z2, acc = lbv[:, 3, :], lbv[:, 0, :], lbv[:, 1, :], lbv[:, 2, :]
            V.tensor_scalar(z, y, 2.0, None, ALU.add)
            fence()
            V.reciprocal(z, z)
            fence()
            V.tensor_tensor(z, z, y, ALU.mult)
            fence()
            V.tensor_tensor(z2, z, z, ALU.mult)
            fence()
            V.tensor_scalar(acc, z2, 1.0 / 17, 1.0 / 15, ALU.mult, ALU.add)
            for c in (13, 11, 9, 7, 5, 3, 1):
                fence()
                V.tensor_tensor(acc, acc, z2, ALU.mult)
                fence()
                V.tensor_scalar(acc, acc, 1.0 / c, None, ALU.add)
            fence()
            V.scalar_tensor_tensor(acc, acc, 2.0, z, ALU.mult, ALU.mult)
            V.tensor_scalar(y, vecs[:, VEC["lam"]:VEC["lam"] + 8], -1.0, 0.0, ALU.mult, ALU.max)
            fence()
            V.tensor_tensor(y, y, acc, ALU.add)
            fence()
            V.tensor_scalar(lbv[:, 1, :], y, -8.0, None, ALU.mult)
            V.tensor_scalar(lbv[:, 2, :], y, 8.0, None, ALU.mult)
            dve.drain().then_inc(sg("spl"), 1)
            x_parts_lo(dve, 7, UC)
            lo_ahead(dve, C_LA)
            lo_ahead(dve, C_LX)
            dve.wait_ge(sg("ri"), 1)
            V.tensor_tensor(LI, LI, UC, ALU.mult)
            fence()
            dve.wait_ge(sg("ab2"), 1)
            V.tensor_tensor(LE, LE, LB, ALU.mult)
            fence()
            V.tensor_tensor(LI, LI, LE, ALU.mult)
            fence()
            for k in range(KT):
                V.tensor_tensor_scan(LR[:, k, :], LA[:, k, :], LI[:, k, :], 0.0, ALU.mult, ALU.add)
            fence()
            V.tensor_tensor(HS, LR, LY, ALU.mult)
            dve.drain().then_inc(sg("lm"), 1)
            x_parts_lo(dve, 8, HS)
            for j in range(4):
                lo_ahead(dve, C_LOUT + j)
                add_result(dve, U_LOUT + j, j)
            dve.drain().then_inc(s_x, 1)
            swiglu_dve(C_FB, U_FB, 9, 7, ("norm_ffn", 8), FF2_STEPS)
            add_acc(N_CHUNKS)
            stat_recip(dve, 8)
            for k in range(KT):
                V.scalar_tensor_tensor(yT[:, k, :], xT[:, k, :], vec("final", k), rstd[:, :], ALU.mult, ALU.mult)
            dve.drain().then_inc(sg("y"), 1)
            barrier(dve, 5)


_WEIGHTS = ["w_in", "w_out", "w_up", "w_down", "hgrn_w_in_2", "hgrn_w_out_2", "lru_w_in_2", "lru_wa_2",
            "lru_wx_2", "lru_w_out_2", "ffn_w_in_2", "ffn_w_out_2"]
_OTHERS = ["x"]


def lay_out(inputs):
    a = {n: np.ascontiguousarray(inputs[n]) for n in _WEIGHTS + _OTHERS}

    def columns(v):
        v = np.asarray(v)
        return v.reshape(-1, P).T

    parts = [columns(inputs[n]) for n in ("pre_mix_norm", "post_mix_norm", "pre_mlp_norm", "post_mlp_norm",
                                          "norm_mix_2", "norm_ffn_2", "norm_final_2", "conv_w")]
    parts.append(np.concatenate([np.asarray(inputs["gdn_norm_w"])[0]] * 2)[:, None])
    parts.append(columns(inputs["hgrn_lb_2"]))
    parts += [columns(inputs[n]) for n in ("hgrn_norm_2", "lru_conv_w_2", "lru_conv_b_2", "lru_ba_2", "lru_bx_2",
                                           "lru_lambda_2")]
    a["rel_t"] = np.ascontiguousarray(np.asarray(inputs["rel_bias"]).T)
    a["gdn_rows"] = np.stack([np.asarray(inputs["A_log"])[0], np.asarray(inputs["dt_bias"])[0]], 1)
    a["vecs"] = np.ascontiguousarray(np.concatenate(parts, 1))
    a["masks"], a["sel"], a["hot"] = shape_constants()
    return a


def program(nc, arrays):
    io = {n: nc.dram_tensor(f"in_{n}", a.shape, mybir.dt.from_np(a.dtype), kind="ExternalInput").ap()
          for n, a in arrays.items()}
    io["out"] = nc.dram_tensor("result", (1, S, D), F32, kind="ExternalOutput").ap()
    build(nc, io)


def kernel(**inputs):
    import concourse.bacc as bacc
    from concourse.bass_utils import run_bass_kernel_spmd

    nc = bacc.Bacc("TRN2", target_bir_lowering=False, num_devices=1)
    arrays = lay_out(inputs)
    program(nc, arrays)
    r = run_bass_kernel_spmd(nc, [{f"in_{n}": a for n, a in arrays.items()}], core_ids=[0])
    return r.results[0]["result"]
```

```python
from contextlib import ExitStack

import numpy as np

import concourse.bass as bass
from concourse import mybir

F32 = mybir.dt.float32
F32R = mybir.dt.float32r
I32 = mybir.dt.int32
ALU = mybir.AluOpType
ACT = mybir.ActivationFunctionType
AX = mybir.AxisListType.X

P = 128
S = 256
D = 1024
KT = D // P
HD = 64
CH = 64
EPS = 1e-6
COLS = 256
NSLOT = 3
D_FF = 4096
D_FF2 = 2816

AQ, AK, AV, GQ, GK, GV, GZ, GA, GB = 0, 512, 1024, 1536, 2048, 2560, 3072, 3584, 3592

C_AQ, C_AK, C_AV, C_GQ, C_GK, C_GV, C_AB, C_Z = 0, 2, 4, 6, 8, 10, 12, 13
C_OUT = 15
C_FF = 19
FF_STEPS = D_FF // COLS
C_HF = C_FF + 2 * FF_STEPS
C_HQ, C_HV, C_HG = C_HF + 4, C_HF + 8, C_HF + 12
C_HOUT = C_HF + 16
C_FA = C_HOUT + 4
FF2_STEPS = D_FF2 // COLS
C_LU = C_FA + 3 * FF2_STEPS
C_LA, C_LX = C_LU + 4, C_LU + 5
C_LY = C_LX + 1
C_LOUT = C_LY + 4
C_FB = C_LOUT + 4
N_CHUNKS = C_FB + 3 * FF2_STEPS

VEC = {}
_at = 0
for _name, _n in (("pre_mix", 8), ("post_mix", 8), ("pre_mlp", 8), ("post_mlp", 8), ("norm_mix", 16),
                  ("norm_ffn", 16), ("final", 8), ("conv_w", 48), ("gdn_w", 1), ("lb", 16), ("hg_w", 1),
                  ("lconv_w", 32), ("lconv_b", 8), ("ba", 8), ("bx", 8), ("lam", 8)):
    VEC[_name] = _at
    _at += _n
N_VEC = _at
BIAS_W = 384


def shape_constants():
    t = np.arange(P)
    s_, t_ = t[:, None], t[None, :]
    up = []
    for l in range(7):
        m = 1 << l
        up.append((s_ // (2 * m) == t_ // (2 * m)) & ((s_ // m) % 2 == 0) & ((t_ // m) % 2 == 1))
    low = [u.T for u in up[:6]]
    ident = s_ == t_
    causal = (s_ <= t_) & (s_ // CH == t_ // CH)
    block = s_ // HD == t_ // HD
    masks = np.stack(up + low + [ident, causal, block], 1).astype(np.float32)
    sel = np.zeros((40, 12, P), np.float32)
    for h in range(8):
        for hp in range(4):
            if h // 2 == hp:
                sel[h, hp, (h % 2) * HD:(h % 2 + 1) * HD] = 1
                sel[32 + h, hp, (h % 2) * HD:(h % 2 + 1) * HD] = 1
        sel[h, 4 + h, :] = 1
    d = 255 - np.arange(BIAS_W)
    dm = np.maximum(d, 1).astype(np.float32)
    large = 16 + (np.log(dm / 16) / np.float32(np.log(128 / 16)) * 16).astype(np.int32)
    bucket = np.where(d < 16, np.maximum(d, 0), np.minimum(large, 31))
    hot = np.zeros((33, BIAS_W), np.float32)
    hot[bucket[d >= 0], np.nonzero(d >= 0)[0]] = 1
    hot[32, d < 0] = 1
    return masks, sel, hot


def build(nc, io):
    ctx = ExitStack()

    def sb(name, shape, dt=F32):
        return ctx.enter_context(nc.sbuf_tensor(name, shape, dt))

    def sem(name):
        return ctx.enter_context(nc.semaphore(name))

    with ctx:
        raw = sb("raw", [P, NSLOT, 8 * COLS])
        w_hi = sb("w_hi", [P, NSLOT, 8 * COLS], F32R)
        w_lo = sb("w_lo", [P, NSLOT, 8 * COLS], F32R)
        xT = sb("xT", [P, KT, S])
        x_hi = sb("x_hi", [P, KT, S], F32R)
        x_lo = sb("x_lo", [P, KT, S], F32R)
        h_hi = sb("h_hi", [P, 3, 2 * S], F32R)
        h_lo = sb("h_lo", [P, 3, 2 * S], F32R)
        masks = sb("masks", [P, 16, P])
        shared = sb("shared", [P, 2048])
        sel = shared[0:40, 0:12 * P].rearrange("p (a b) -> p a b", a=12)
        hot = shared[0:33, 12 * P:12 * P + BIAS_W]
        rel = sb("rel", [33, 8])
        vecs = sb("vecs", [P, N_VEC])
        gdn_rows = sb("gdn_rows", [8, 2])
        mean_mat = sb("mean_mat", [P, P])
        eps_t = sb("eps_t", [P, 1])
        one_t = sb("one_t", [P, 1])
        zeros = sb("zeros", [P, 512], mybir.dt.bfloat16)
        sd = sb("sd", [P, S])
        rstd = sb("rstd", [P, S])
        rcol = sb("rcol", [P, 2])
        reset = sb("reset", [P, S])
        cols = sb("cols", [P, 8, 16])
        lbv = sb("lbv", [P, 5, 8])
        MIXERS = 17920
        ARENA = MIXERS + BIAS_W + 5 * S
        arena = sb("arena", [P, ARENA])
        bank = [ctx.enter_context(nc.psum_tensor(f"bank{i}", [P, 512], F32)) for i in range(8)]
        STAT = bank[3]
        bias_dram = nc.dram_tensor("bias_dram", (8, P, BIAS_W), F32, kind="Internal").ap()

        def ar(off, *dims):
            n = int(np.prod(dims))
            assert off + n <= ARENA
            v = arena[:, off:off + n]
            if len(dims) == 1:
                return v
            names = "abc"[:len(dims)]
            return v.rearrange(f"p ({' '.join(names)}) -> p {' '.join(names)}",
                               **{c: d for c, d in zip(names[1:], dims[1:])})

        bias_row = arena[0:8, MIXERS:MIXERS + BIAS_W]
        rows = arena[0:40, MIXERS + BIAS_W:ARENA].rearrange("p (a b) -> p a b", a=5)

        def vec(name, k):
            c = VEC[name] + k
            return vecs[:, c:c + 1]

        IDENT, CAUSAL, BLOCK = masks[:, 13, :], masks[:, 14, :], masks[:, 15, :]

        s_small = sem("s_small")
        s_const = sem("s_const")
        s_landed = [sem(f"s_landed{i}") for i in range(NSLOT)]
        s_whi = sem("s_whi")
        s_wlo = sem("s_wlo")
        s_used = sem("s_used")
        s_gate = sem("s_gate")
        s_free = sem("s_free")
        s_xhi = sem("s_xhi")
        s_xlo = sem("s_xlo")
        s_x = sem("s_x")
        s_sq, s_stat, s_sd, s_rs = sem("s_sq"), sem("s_stat"), sem("s_sd"), sem("s_rs")
        s_xin, s_bar, s_out = sem("s_xin"), sem("s_bar"), sem("s_out")
        s_h, s_hhi, s_hlo = sem("s_h"), sem("s_hhi"), sem("s_hlo")
        s_g2, s_silu = sem("s_g2"), sem("s_silu")
        s_y = sem("s_y")
        s_mT, s_ab, s_gr, s_vec = sem("s_mT"), sem("s_ab"), sem("s_gr"), sem("s_vec")
        s_bias = [sem(f"s_bias{i}") for i in range(4)]
        s_rc = [sem(f"s_rc{i}") for i in range(2)]
        named = {}

        def sg(name):
            if name not in named:
                named[name] = sem("m_" + name)
            return named[name]

        def up_view(w, c0):
            return w.rearrange("(k p) n -> p k n", p=P)[:, :, c0:c0 + COLS]

        def down_view(w, r0):
            return w[r0:r0 + COLS, :].rearrange("(k p) n -> p k n", p=P)

        def slot(t, n, shape):
            v = t[:, n % NSLOT, :]
            return v.rearrange("p (k n) -> p k n", k=8) if shape == "up" else \
                v.rearrange("p (k n) -> p k n", k=2)

        w_in, w_out, w_up, w_down = io["w_in"], io["w_out"], io["w_up"], io["w_down"]
        plan = {}
        for c, base in ((C_AQ, AQ), (C_AK, AK), (C_AV, AV), (C_GQ, GQ), (C_GK, GK), (C_GV, GV), (C_Z, GZ)):
            for j in range(2):
                plan[c + j] = ("up", w_in[0], base + j * COLS)
        for j in range(4):
            plan[C_OUT + j] = ("up", w_out[0], j * COLS)
            plan[C_HF + j] = ("up", io["hgrn_w_in_2"][0], D + j * COLS)
            plan[C_HQ + j] = ("up", io["hgrn_w_in_2"][0], j * COLS)
            plan[C_HV + j] = ("up", io["hgrn_w_in_2"][0], 2 * D + j * COLS)
            plan[C_HG + j] = ("up", io["hgrn_w_in_2"][0], 3 * D + j * COLS)
            plan[C_HOUT + j] = ("up", io["hgrn_w_out_2"][0], j * COLS)
            plan[C_LU + j] = ("up", io["lru_w_in_2"][0], D + j * COLS)
            plan[C_LY + j] = ("up", io["lru_w_in_2"][0], j * COLS)
            plan[C_LOUT + j] = ("up", io["lru_w_out_2"][0], j * COLS)
        plan[C_LA] = ("up", io["lru_wa_2"][0].rearrange("n c d -> (n c) d"), 0)
        plan[C_LX] = ("up", io["lru_wx_2"][0].rearrange("n c d -> (n c) d"), 0)

        def wait_slot_free(sp, n):
            if not isinstance(n, int) or n >= NSLOT:
                sp.wait_ge(s_wlo, n - NSLOT + 1)

        def load(sp, n, j, kind, w, c0):
            wait_slot_free(sp, n)
            if kind == "up":
                sp.dma_start(slot(raw, j, "up"), w.rearrange("(k p) n -> p k n", p=P)[:, :, bass.ds(c0, COLS)]
                             ).then_inc(s_landed[j % NSLOT], 16)
            else:
                sp.dma_start(slot(raw, j, "down"), w[bass.ds(c0, COLS), :].rearrange("(k p) n -> p k n", p=P)
                             ).then_inc(s_landed[j % NSLOT], 16)

        def landed_count(n):
            return 16 * (n // NSLOT + 1)

        def hi_part(act, n, i=None, on_pool=False):
            if on_pool:
                act.wait_ge(s_whi, n)
            d = 0 if i is None else i * 6
            act.wait_ge(s_landed[n % NSLOT], landed_count(n) + (0 if i is None else i * 32))
            if n == C_AB:
                act.wait_ge(s_ab, 16)
            if n >= NSLOT:
                act.wait_ge(s_used, n - NSLOT + 1 + d)
            if on_pool:
                nc.gpsimd.tensor_copy(w_hi[:, n % NSLOT, :], raw[:, n % NSLOT, :]).then_inc(s_whi, 1)
            else:
                nc.scalar.activation(w_hi[:, n % NSLOT, :], raw[:, n % NSLOT, :], ACT.Copy).then_inc(s_whi, 1)

        def lo_part(dve, n, i=None):
            dve.wait_ge(s_whi, n + 1 + (0 if i is None else i * 6))
            nc.vector.tensor_tensor(w_lo[:, n % NSLOT, :], raw[:, n % NSLOT, :],
                                    w_hi[:, n % NSLOT, :].bitcast(F32), ALU.subtract).then_inc(s_wlo, 1)

        AHEAD = 2

        def exists(n, i):
            return n + (6 * i if isinstance(i, int) else 0) < N_CHUNKS

        def swiglu_rounds(c):
            return (FF2_STEPS - 1) // 2 - (c == C_FB)

        def hi_ahead(act, n, i=None):
            if exists(n + AHEAD, i):
                hi_part(act, n + AHEAD, i)

        def lo_ahead(dve, n, i=None):
            if exists(n + AHEAD, i):
                lo_part(dve, n + AHEAD, i)

        def pair_mm(out, wh, wl, xh, xl, start, stop):
            nc.tensor.matmul(out, wh, xh, start=start, stop=False, skip_group_check=True)
            nc.tensor.matmul(out, wh, xl, start=False, stop=False, skip_group_check=True)
            return nc.tensor.matmul(out, wl, xh, start=False, stop=stop, skip_group_check=True)

        def gemm_feat(pe, n, u, b, prod=None, i=None, di=0, ktiles=8, ntiles=2):
            off = 0 if i is None else i * 6
            pe.wait_ge(s_wlo, n + 1 + off)
            if u >= 2:
                pe.wait_ge(s_free, u - 1 + (0 if i is None else i * di))
            wh, wl = slot(w_hi, n, "up"), slot(w_lo, n, "up")
            for t in range(ntiles):
                for k in range(ktiles):
                    if prod is not None and t == 0:
                        pe.wait_ge(s_xlo, 8 * prod + k + 1)
                    last = pair_mm(b[:, t * S:(t + 1) * S], wh[:, k, t * P:(t + 1) * P], wl[:, k, t * P:(t + 1) * P],
                                   x_hi[:, k, :], x_lo[:, k, :], k == 0, k == ktiles - 1)
            last.then_inc(s_used, 1)

        def gemm_tok(pe, n, u, b, prod=None):
            pe.wait_ge(s_wlo, n + 1)
            if u >= 2:
                pe.wait_ge(s_free, u - 1)
            wh, wl = slot(w_hi, n, "up"), slot(w_lo, n, "up")
            for t in range(2):
                o = b[:, t * COLS:(t + 1) * COLS]
                for k in range(8):
                    xh, xl = x_hi[:, k, t * P:(t + 1) * P], x_lo[:, k, t * P:(t + 1) * P]
                    last = pair_mm(o, xh, xl, wh[:, k, :], wl[:, k, :], k == 0, k == 7)
            last.then_inc(s_used, 1)

        def gemm_down(pe, n, hslot, hcount, i=None, dh=0):
            pe.wait_ge(s_wlo, n + 1 + (0 if i is None else i * 6))
            pe.wait_ge(s_hlo, hcount + (0 if i is None else i * dh))
            wh, wl = slot(w_hi, n, "down"), slot(w_lo, n, "down")
            for k in range(2):
                for t in range(KT):
                    last = pair_mm(bank[4 + t // 2][:, (t % 2) * S:(t % 2 + 1) * S],
                                   wh[:, k, t * P:(t + 1) * P], wl[:, k, t * P:(t + 1) * P],
                                   h_hi[:, hslot, k * S:(k + 1) * S], h_lo[:, hslot, k * S:(k + 1) * S],
                                   False, True)
            last.then_inc(s_used, 1)
            return last

        def bank_of(u):
            return bank[u % 2]

        def ff_bank(j):
            return (j - 1) % 3

        def x_parts_hi(act, e, src, used, w=None, ks=range(8), version=None):
            act.wait_ge(s_used, used)
            for k in ks:
                if version is not None and k % 2 == 0:
                    act.wait_ge(s_x, 4 * (version - 1) + k // 2 + 1)
                if w is None:
                    nc.scalar.activation(x_hi[:, k, :], src[:, k, :], ACT.Copy).then_inc(s_xhi, 1)
                else:
                    nc.scalar.activation(x_hi[:, k, :], src[:, k, :], ACT.Copy,
                                         scale=vec(w[0], w[1] + k)).then_inc(s_xhi, 1)

        def x_parts_lo(dve, e, src, w=None, ks=range(8)):
            for k in ks:
                dve.wait_ge(s_xhi, 8 * e + k + 1)
                if w is None:
                    nc.vector.tensor_tensor(x_lo[:, k, :], src[:, k, :], x_hi[:, k, :].bitcast(F32),
                                            ALU.subtract).then_inc(s_xlo, 1)
                else:
                    nc.vector.scalar_tensor_tensor(x_lo[:, k, :], src[:, k, :], vec(w[0], w[1] + k),
                                                   x_hi[:, k, :].bitcast(F32), ALU.mult, ALU.subtract
                                                   ).then_inc(s_xlo, 1)

        SQ = ar(0, KT, S)

        def stat_square(act, r, src, sem_=None, before=0):
            if r:
                act.wait_ge(s_stat, r)
            for j in range(4):
                if sem_ is not None:
                    act.wait_ge(sem_, before + j + 1)
                nc.scalar.activation(SQ[:, 2 * j:2 * j + 2, :], src(j), ACT.Square).then_inc(s_sq, 1)

        def x_pair(j):
            return xT[:, 2 * j:2 * j + 2, :]

        def stat_sum(pe, r):
            if r:
                pe.wait_ge(s_sd, r)
            for k in range(KT):
                if k % 2 == 0:
                    pe.wait_ge(s_sq, 4 * r + k // 2 + 1)
                last = nc.tensor.matmul(STAT[:, 0:S], mean_mat[:, :], SQ[:, k, :], start=(k == 0), stop=(k == KT - 1))
            last.then_inc(s_stat, 1)

        def stat_sqrt(act, r):
            act.wait_ge(s_stat, r + 1)
            if r:
                act.wait_ge(s_rs, r)
            nc.scalar.activation(sd[:, :], STAT[:, 0:S], ACT.Sqrt, bias=eps_t[:, 0:1]).then_inc(s_sd, 1)

        def stat_recip(dve, r):
            dve.wait_ge(s_sd, r + 1)
            nc.vector.reciprocal(rstd[:, :], sd[:, :]).then_inc(s_rs, 1)
            dve.drain()

        rb2 = rstd[:, :].unsqueeze(1).to_broadcast([P, 2, S])

        def b2(b):
            return b[:, :].rearrange("p (a b) -> p a b", a=2)

        def barrier(eng, k):
            eng.drain().then_inc(s_bar, 1)
            eng.wait_ge(s_bar, 4 * (k + 1))

        xin = ar(0, 2, D)
        mixA = ar(4096, 4, S)
        a_q, a_k = ar(5120, 4, S), ar(6144, 4, S)
        a_v = ar(7168, 2, 512)
        biasM = ar(8192, 8, S)
        Lg = ar(10240, 8, 384)
        PTs = ar(2048, 2, 2, 384)
        GP = ar(13312, 12, S + 3)
        HM, HN = ar(0, 8, P), ar(1024, 8, P)
        HT, HMm = ar(2048, 8, P), ar(3072, 8, P)
        qT, kT, vT = ar(5120, 4, S), ar(6144, 4, S), ar(7168, 4, S)
        EQ, qd = ar(8192, 4, S), ar(9216, 4, S)
        kbT, kbg, kdec = ar(10240, 4, S), ar(11264, 2, 512), ar(12288, 2, 512)
        bv, AT, YB = ar(13312, 2, 512), ar(14336, 16, P), ar(16384, 2, 4, P)
        wT = ar(7168, 4, S)
        zs, St, vn, oT = ar(0, 4, S), ar(1024, 4, P), ar(2048, 2, 512), ar(3072, 4, S)
        St2 = ar(1536, 4, P)
        sqo, ro, mixG = ar(10240, 4, S), ar(16384, 4, S), ar(14336, 4, S)
        mT = ar(10240, KT, S)
        gcol, bcol, ecol, kcol, gecol = (cols[:, j, :].rearrange("p (i h) -> p i h", i=2) for j in range(5))
        nmx, sums = cols[:, 5, :], cols[:, 6, :]
        R_A, R_G, R_T, R_B, R_L = range(5)

        def heads_of(g):
            return (4 * (g // 2) + g % 2, 4 * (g // 2) + g % 2 + 2)

        HX, HB, HQ, HK = ar(0, KT, S), ar(2048, KT, S), ar(4096, KT, S), ar(6144, KT, S)
        HV = ar(8192, 2, D)
        QK = [ar(10240, KT, S), ar(12288, KT, S)]
        HAT = ar(14336, 8, 2, P)
        OFF = ar(16384, 8, P)
        HXs = [HX, ar(17408, KT, S)]
        HG = shared[:, :].rearrange("p (a b) -> p a b", a=KT)
        LU = ar(0, KT, S + 3)
        UC, LY, LR, LI, LA, LE, LB = (ar(2304 + 2048 * j, KT, S) for j in range(7))
        HS = ar(0, KT, S)
        FT = ar(4096, 3, 2 * S)
        FH = ar(5632, 3, 2 * S)
        FU = ar(7168, 3, 2 * S)
        FS = ar(8704, 3, 2 * S)
        yT = ar(2048, KT, S)
        ytok = ar(4096, 2, D)

        H_GATES = FF_STEPS + FF2_STEPS
        U_W1 = 0
        U_OUT = 15
        U_FF = 19
        U_HG = U_FF + FF_STEPS
        U_HOUT = U_HG + 16
        U_FA = U_HOUT + 4
        U_LU = U_FA + 2 * FF2_STEPS
        U_LA = U_LU + 4
        U_LY = U_LA + 8
        U_LOUT = U_LY + 4
        U_FB = U_LOUT + 4

        def done(u):
            for first, c, n in ((U_W1, 0, C_FF + 1), (U_HG, C_HF, 22), (U_LU, C_LU, 4), (U_LY, C_LY, 4), (U_LOUT, C_LOUT, 6)):
                if first <= u < first + n:
                    return c + u - first + 1
            raise ValueError(u)

        def conv_weights(tap, g):
            c = VEC["conv_w"] + 12 * tap + 4 * g
            return vecs[:, c:c + 4].unsqueeze(2).to_broadcast([P, 4, S])

        block = ctx.enter_context(nc.Block())

        @block.sync
        def _(sp):
            sp.dma_start(xin, io["x"][0].rearrange("(i p) d -> p i d", p=P)).then_inc(s_xin, 16)
            sp.dma_start(masks[:, 13, :], io["masks"][:, 13, :]).then_inc(s_xin, 16)
            sp.dma_start(vecs[:, :], io["vecs"]).then_inc(s_vec, 16)
            for n in range(3):
                load(sp, n, n, *plan[n])
            sp.dma_start(masks[:, 0:13, :], io["masks"][:, 0:13, :]).then_inc(s_small, 16)
            sp.dma_start(masks[:, 14:16, :], io["masks"][:, 14:16, :]).then_inc(s_small, 16)
            sp.dma_start(sel[:, :, :], io["sel"]).then_inc(s_small, 16)
            for n in range(3, C_FF):
                if n == C_AB:
                    wait_slot_free(sp, n)
                    v = w_in[0].rearrange("(k p) n -> p k n", p=P)
                    o = slot(raw, n, "up")
                    sp.dma_start(o[:, :, 0:8], v[:, :, GA:GA + 8]).then_inc(s_landed[n % NSLOT], 16)
                    sp.dma_start(o[:, :, 32:40], v[:, :, GB:GB + 8]).then_inc(s_ab, 16)
                else:
                    load(sp, n, n, *plan[n])
            load(sp, C_FF, C_FF, "up", w_up[0], 0)
            with sp.Fori(0, (FF_STEPS - 1) // 3) as i:
                for j in range(6):
                    n = C_FF + 1 + j
                    w = w_up[0] if j % 2 == 0 else w_down[0]
                    load(sp, n + i * 6, n, "up" if j % 2 == 0 else "down", w,
                         i * (3 * COLS) + (j // 2 + 1 - j % 2) * COLS)
            load(sp, C_HF - 1, C_HF - 1, "down", w_down[0], D_FF - COLS)
            for n in range(C_HF, C_FA):
                load(sp, n, n, *plan[n])

            def swiglu_loads(c, l):
                wi, wo = io["ffn_w_in_2"][l], io["ffn_w_out_2"][l]
                load(sp, c, c, "up", wi, 0)
                load(sp, c + 1, c + 1, "up", wi, D_FF2)
                with sp.Fori(0, (FF2_STEPS - 1) // 2) as i:
                    for j in range(6):
                        n = c + 2 + j
                        st = j // 3
                        if j % 3 < 2:
                            load(sp, n + i * 6, n, "up", wi, i * (2 * COLS) + (st + 1) * COLS + (j % 3) * D_FF2)
                        else:
                            load(sp, n + i * 6, n, "down", wo, i * (2 * COLS) + st * COLS)
                n = c + 3 * FF2_STEPS - 1
                load(sp, n, n, "down", wo, D_FF2 - COLS)

            swiglu_loads(C_FA, 0)
            for n in range(C_LU, C_FB):
                load(sp, n, n, *plan[n])
            swiglu_loads(C_FB, 1)
            for i in range(2):
                sp.wait_ge(s_y, i + 1)
                sp.dma_start(io["out"][0].rearrange("(i p) d -> p i d", p=P)[:, i, :], ytok[:, i, :]
                             ).then_inc(s_out, 16)
            sp.wait_ge(s_out, 32)

        @block.gpsimd
        def _(pool):
            pool.memset(eps_t[:, :], EPS)
            pool.memset(one_t[:, :], 1.0)
            pool.memset(mean_mat[:, :], 1.0 / D)
            pool.memset(reset[:, :], 1.0)
            pool.memset(zeros[:, :], 0.0)
            pool.memset(GP[:, :, 0:3], 0.0)
            pool.drain()
            pool.memset(reset[:, :].rearrange("p (c t) -> p c t", t=CH)[:, :, 0:1], 0.0)
            pool.drain()
            pool.memset(rel[32:33, :], -1e30)
            pool.drain().then_inc(s_const, 1)
            pool.dma_start(rel[0:32, :], io["rel_t"]).then_inc(s_bias[0], 16)
            pool.dma_start(hot[:, :], io["hot"]).then_inc(s_bias[0], 16)
            pool.dma_start(gdn_rows[:, :], io["gdn_rows"]).then_inc(s_gr, 16)
            pool.wait_ge(s_bias[2], 1)
            pool.dma_start(bias_dram, bias_row[:, :].unsqueeze(1).to_broadcast([8, P, BIAS_W])
                           ).then_inc(s_bias[3], 16)
            pool.wait_ge(s_bias[3], 16)
            pool.dma_start(biasM, bass.AP(bias_dram.tensor, P - 1, [[BIAS_W - 1, P], [P * BIAS_W, 8], [1, S]])
                           ).then_inc(s_bias[3], 16)
            pool.wait_ge(s_vec, 16)
            pool.wait_ge(sg("as"), 4)
            for g, dst in enumerate((qT, kT)):
                pool.wait_ge(sg("gp"), g + 1)
                x, tap_term = GP[:, 4 * g:4 * g + 4, :], ar(1024, 4, S)
                nc.gpsimd.tensor_tensor(dst, x[:, :, 0:S], conv_weights(0, g), ALU.mult)
                for tap in range(1, 4):
                    nc.gpsimd.tensor_tensor(tap_term, x[:, :, tap:tap + S], conv_weights(tap, g), ALU.mult)
                    pool.drain()
                    nc.gpsimd.tensor_tensor(dst, dst, tap_term, ALU.add)
                    pool.drain()
                pool.drain().then_inc(sg("conv"), 1)
            pool.wait_ge(s_small, 48)
            barrier(pool, 0)
            for hf in range(2):
                for l in range(1, 6):
                    e = 5 * hf + l - 1
                    if l == 1:
                        pool.wait_ge(sg("M"), hf + 1)
                    else:
                        pool.wait_ge(sg("Y"), 2 * e)
                    nc.gpsimd.tensor_tensor(HMm, HM, masks[:, 7 + l, :].unsqueeze(1).to_broadcast([P, 8, P]),
                                            ALU.mult).then_inc(sg("Mm"), 1)
            pool.wait_ge(sg("lev"), 2)
            pool.memset(St, 0.0)
            pool.drain().then_inc(sg("S"), 1)
            barrier(pool, 1)
            barrier(pool, 2)
            barrier(pool, 3)
            pool.memset(HAT, 0.0)
            pool.drain().then_inc(sg("HAT0"), 1)

            def even_exponents(l):
                if l >= 2:
                    pool.wait_ge(sg("hQd"), l - 1)
                if l < 6:
                    m = 1 << l
                    x = HXs[l % 2].rearrange("p k (b e m) -> p (k b) e m", e=2, m=m)
                    b = HB.rearrange("p k (b e m) -> p (k b) e m", e=2, m=m)
                    ref = b[:, :, 0, m - 1:m].to_broadcast([P, KT * S // (2 * m), m])
                    nc.gpsimd.tensor_tensor(x[:, :, 0, :], ref, b[:, :, 0, :], ALU.subtract)
                else:
                    x = HXs[l % 2].rearrange("p k (c t) -> p k c t", t=CH)
                    b = HB.rearrange("p k (c t) -> p k c t", t=CH)
                    for c in ((0, 2) if l == 6 else (0, 1)):
                        nc.gpsimd.tensor_tensor(x[:, :, c, :], b[:, :, c, CH - 1:CH].to_broadcast([P, KT, CH]),
                                                b[:, :, c, :], ALU.subtract)
                    if l == 7:
                        pool.drain()
                        nc.gpsimd.tensor_tensor(x[:, :, 0, :], x[:, :, 0, :],
                                                b[:, :, 1, CH - 1:CH].to_broadcast([P, KT, CH]), ALU.add)
                pool.drain().then_inc(sg("hXp"), 1)

            even_exponents(0)
            for l in range(8):
                if l < 7:
                    even_exponents(l + 1)
                pool.wait_ge(sg("hE"), l + 1)
                if l >= 2:
                    pool.wait_ge(sg("hS"), 4 * (l - 1))
                q, x = QK[l % 2], HXs[l % 2]
                if l < 7:
                    m = 1 << l
                    v = lambda t: t.rearrange("p k (b e m) -> p (k b) e m", e=2, m=m)
                    nc.gpsimd.tensor_tensor(v(q)[:, :, 0, :], v(HK)[:, :, 0, :], v(x)[:, :, 0, :], ALU.mult)
                else:
                    nc.gpsimd.tensor_tensor(q[:, :, 0:P], HK[:, :, 0:P], x[:, :, 0:P], ALU.mult)
                pool.drain().then_inc(sg("hQK"), 1)
            barrier(pool, 4)
            for n in range(C_LY + 1, C_LY + 3):
                hi_part(pool, n + AHEAD, on_pool=True)
            barrier(pool, 5)

        @block.scalar
        def _(act):
            def copy(o, i):
                return nc.scalar.activation(o, i, ACT.Copy)

            act.wait_ge(s_const, 1)
            act.wait_ge(s_vec, 16)
            for n in range(AHEAD):
                hi_part(act, n)
            x_parts_hi(act, 0, xT, 0, ("pre_mix", 0), version=1)
            stat_square(act, 0, x_pair)
            hi_ahead(act, 0)
            stat_sqrt(act, 0)
            act.wait_ge(s_bias[1], 1)
            copy(bias_row[:, :], bank[4][0:8, 0:BIAS_W]).then_inc(s_bias[2], 1)
            def probabilities(hs):
                for h in hs:
                    for qt, (a, b) in enumerate(((0, 256), (256, 384))):
                        j = 2 * h + qt
                        nc.scalar.activation(Lg[:, h, a:b], Lg[:, h, a:b], ACT.Exp, bias=nmx[:, j:j + 1],
                                             accum_out=sums[:, j:j + 1])

            for n in range(1, C_Z):
                hi_ahead(act, n)
                if n == C_GK + 1:
                    act.wait_ge(sg("am"), 1)
                    probabilities(range(4))
                if n == C_GV:
                    probabilities(range(4, 8))
                    act.drain().then_inc(sg("ae"), 1)
            for g, dst in enumerate((qT, kT)):
                act.wait_ge(sg("conv"), g + 1)
                nc.scalar.activation(dst, dst, ACT.Silu).then_inc(sg("silu"), 1)
            act.drain()
            for g, dst in enumerate((qT, kT)):
                nc.scalar.activation(ar(1024 * g, 4, S), dst, ACT.Square).then_inc(sg("gsq"), 1)
            act.wait_ge(sg("ab"), 1)
            nc.scalar.activation(gdn_rows[:, 0:1], gdn_rows[:, 0:1], ACT.Exp)
            nc.scalar.activation(rows[0:8, R_T, :], rows[0:8, R_A, :], ACT.Abs)
            act.drain()
            nc.scalar.activation(rows[0:8, R_T, :], rows[0:8, R_T, :], ACT.Exp, scale=-1.0)
            act.drain()
            nc.scalar.activation(rows[0:8, R_T, :], rows[0:8, R_T, :], ACT.Ln, bias=one_t[0:8, 0:1])
            nc.scalar.activation(rows[32:40, R_B, :], rows[32:40, R_B, :], ACT.Sigmoid)
            act.drain().then_inc(sg("sp"), 1)
            barrier(act, 0)
            act.wait_ge(sg("conv"), 3)
            nc.scalar.activation(vT, vT, ACT.Silu).then_inc(sg("silu"), 1)
            for g in range(2):
                act.wait_ge(sg("gss"), g + 1)
                for j in range(2):
                    last = nc.scalar.activation(ar(2048 + 1024 * g + 512 * j, 2 * S), bank[4 + 2 * g + j][:, :],
                                                ACT.Ln, bias=eps_t[:, 0:1])
            act.drain()
            for g in range(2):
                nc.scalar.activation(ar(2048 + 1024 * g, 4, S), ar(2048 + 1024 * g, 4, S), ACT.Exp,
                                     scale=-0.5).then_inc(sg("grs"), 1)
            act.wait_ge(sg("colT"), 1)
            copy(cols[:, 0, :], bank[4][:, 0:16])
            copy(cols[:, 1, :], bank[5][:, 0:16])
            copy(cols[:, 3, :], bank[4][:, 32:48])
            act.drain()
            nc.scalar.activation(ecol, gcol, ACT.Exp)
            nc.scalar.activation(kcol, kcol, ACT.Exp)
            act.drain().then_inc(sg("cols"), 1)
            act.wait_ge(sg("gpair"), 1)
            for j in range(2):
                nc.scalar.activation(EQ[:, 2 * j:2 * j + 2, :], b2(bank[6 + j]), ACT.Exp)
            act.drain().then_inc(sg("EQ"), 1)
            for hf in range(2):
                act.wait_ge(sg("DTx"), hf + 1)
                nc.scalar.activation(HM, HM, ACT.Exp).then_inc(sg("DTe"), 1)
                act.wait_ge(sg("Mt"), hf + 1)
                for g in range(2):
                    copy(HM[:, 4 * g:4 * g + 4, :], bank[4 + g][:, :].rearrange("p (a b) -> p a b", a=4))
                act.drain().then_inc(sg("M"), 1)
                for l in range(1, 6):
                    e = 5 * hf + l - 1
                    for g in range(2):
                        act.wait_ge(sg("Y"), 2 * e + g + 1)
                        if e:
                            act.wait_ge(sg("X"), 2 * (e - 1) + g + 1)
                        copy(YB[:, g, :, :], bank[4 + g][:, :].rearrange("p (a b) -> p a b", a=4)
                             ).then_inc(sg("Yc"), 1)
                act.wait_ge(sg("uw"), hf + 1)
                copy(wT[:, 2 * hf:2 * hf + 2, :], b2(bank[6])).then_inc(sg("uwc"), 1)
            barrier(act, 1)
            for c in range(4):
                if c == 2:
                    act.wait_ge(sg("z"), 2)
                    nc.scalar.activation(zs, zs, ACT.Silu).then_inc(sg("zs"), 1)
                    hi_ahead(act, C_Z)
                if c == 3:
                    hi_ahead(act, C_Z + 1)
                act.wait_ge(sg("o"), c + 1)
                copy(oT[:, :, c * CH:(c + 1) * CH], bank[5][:, 0:256].rearrange("p (a b) -> p a b", a=4)
                     ).then_inc(sg("oc"), 1)
            act.drain()
            nc.scalar.activation(sqo, oT, ACT.Square).then_inc(sg("osq"), 1)
            x_parts_hi(act, 1, mixA, C_OUT, None, range(4))
            act.wait_ge(sg("oss"), 1)
            for j in range(2):
                nc.scalar.activation(ro[:, 2 * j:2 * j + 2, :], b2(bank[6 + j]), ACT.Ln, bias=eps_t[:, 0:1],
                                     scale=1.0 / HD)
            act.drain()
            nc.scalar.activation(ro, ro, ACT.Exp, scale=-0.5).then_inc(sg("ors"), 1)
            act.wait_ge(sg("mixG"), 1)
            for k in range(4):
                nc.scalar.activation(x_hi[:, 4 + k, :], mixG[:, k, :], ACT.Copy).then_inc(s_xhi, 1)
            for n in range(C_OUT, C_FF):
                hi_ahead(act, n)

            def norm_then_input(r_post, r, e, version, used, w, first):
                if r_post is not None:
                    stat_square(act, r_post, lambda j: mT[:, 2 * j:2 * j + 2, :], s_mT, 0 if r_post == 1 else 4)
                    stat_sqrt(act, r_post)
                x_parts_hi(act, e, xT, used, w, version=version)
                stat_square(act, r, x_pair)
                hi_ahead(act, first)
                stat_sqrt(act, r)

            def mlp_hi(hslot, count, i=None, d=0):
                act.wait_ge(s_h, count + (0 if i is None else i * d))
                nc.scalar.activation(h_hi[:, hslot, :], FH[:, hslot, :], ACT.Copy).then_inc(s_hhi, 1)

            norm_then_input(1, 2, 2, 2, C_FF, ("pre_mlp", 0), C_FF)
            mlp_hi(0, 1)
            with act.Fori(0, (FF_STEPS - 1) // 3) as i:
                for j in range(3):
                    n = C_FF + 1 + 2 * j
                    hi_ahead(act, n, i)
                    hi_ahead(act, n + 1, i)
                    mlp_hi((j + 1) % 3, j + 2, i, 3)
            hi_ahead(act, C_HF - 1)
            norm_then_input(3, 4, 3, 3, C_HF, ("norm_mix", 0), C_HF)
            barrier(act, 2)
            act.wait_ge(sg("lb"), 1)
            nc.scalar.activation(lbv[:, 2:4, :], lbv[:, 2:4, :], ACT.Exp).then_inc(sg("lbe"), 1)
            for n in range(C_HF + 1, C_HG):
                hi_ahead(act, n)
                if n == C_HF + 4:
                    act.wait_ge(sg("fl"), 1)
                    nc.scalar.activation(QK[0], HX, ACT.Sigmoid)
                    nc.scalar.activation(HK, HX, ACT.Sigmoid, scale=-1.0)
                    act.drain().then_inc(sg("sig"), 1)
                if n == C_HF + 6:
                    act.wait_ge(sg("f"), 1)
                    nc.scalar.activation(HX, QK[0], ACT.Ln).then_inc(sg("logf"), 1)
            act.wait_ge(sg("hq"), 1)
            nc.scalar.activation(HQ, HQ, ACT.Silu)
            act.drain().then_inc(sg("hqs"), 1)
            barrier(act, 3)
            for l in range(8):
                act.wait_ge(sg("hX"), l + 1)
                act.wait_ge(sg("hXp"), l + 1)
                nc.scalar.activation(HXs[l % 2], HXs[l % 2], ACT.Exp).then_inc(sg("hE"), 1)
                if l == 0:
                    for n in range(C_HG, C_HOUT):
                        hi_ahead(act, n)
                    act.wait_ge(sg("hg"), 1)
                    nc.scalar.activation(HG, HG, ACT.Silu).then_inc(sg("hgs"), 1)
            act.wait_ge(sg("hS"), 32)
            for b in range(2):
                copy(OFF[:, 4 * b:4 * b + 4, :], bank[4 + b][:, :].rearrange("p (a b) -> p a b", a=4))
            act.drain().then_inc(sg("off"), 1)
            for b in range(4):
                act.wait_ge(sg("hog"), b + 1)
                nc.scalar.activation(HB[:, 2 * b:2 * b + 2, :], b2(bank[4 + b]), ACT.Square).then_inc(sg("hsq"), 1)
            for b in range(4):
                act.wait_ge(sg("hss"), b + 1)
                nc.scalar.activation(HQ[:, 2 * b:2 * b + 2, :], b2(bank[2 + b]), ACT.Ln, bias=eps_t[:, 0:1],
                                     scale=float(D // P))
            act.drain()
            for b in range(2):
                nc.scalar.activation(HQ[:, 4 * b:4 * b + 4, :], HQ[:, 4 * b:4 * b + 4, :], ACT.Exp, scale=-0.5
                                     ).then_inc(sg("hrs"), 1)
            for b in range(4):
                act.wait_ge(sg("hm"), b + 1)
                x_parts_hi(act, 4, HX, C_HOUT, None, (2 * b, 2 * b + 1))
            for n in range(C_HOUT, C_FA):
                hi_ahead(act, n)

            def swiglu_act(c, e, r, version, w, step0, used):
                norm_then_input(None, r, e, version, used, w, c)
                hi_ahead(act, c + 1)

                def step(k, hslot, i=None):
                    d = 0 if i is None else i * 2
                    act.wait_ge(s_g2, k + 1 + d)
                    nc.scalar.activation(FS[:, hslot, :], FT[:, hslot, :], ACT.Silu).then_inc(s_silu, 1)
                    mlp_hi(hslot, k + FF_STEPS + 1, i, 2)
                step(step0, 0)

                def two_steps(i):
                    for j in range(2):
                        n = c + 2 + 3 * j
                        for t in range(3):
                            hi_ahead(act, n + t, i)
                        step(step0 + j + 1, (j + 1) % 2, i)

                with act.Fori(0, swiglu_rounds(c)) as i:
                    two_steps(i)
                if c == C_FB:
                    two_steps(swiglu_rounds(c))
                hi_ahead(act, c + 3 * FF2_STEPS - 1)

            swiglu_act(C_FA, 5, 5, 4, ("norm_ffn", 0), 0, C_FA)
            norm_then_input(None, 6, 6, 5, C_LU, ("norm_mix", 8), C_LU)
            barrier(act, 4)
            nc.scalar.activation(lbv[:, 3, :], vecs[:, VEC["lam"]:VEC["lam"] + 8], ACT.Abs)
            act.drain()
            nc.scalar.activation(lbv[:, 3, :], lbv[:, 3, :], ACT.Exp, scale=-1.0)
            act.drain().then_inc(sg("lam"), 1)
            def gate_input_hi(j):
                act.wait_ge(sg("uc"), j + 1)
                if j == 3:
                    act.wait_ge(s_gate, 2)
                nc.scalar.activation(h_hi[:, j % 3, :].rearrange("p (a b) -> p a b", a=2),
                                     UC[:, 2 * j:2 * j + 2, :], ACT.Copy).then_inc(s_hhi, 1)

            def gate_sigmoids(b):
                for gate, (dst, vb) in enumerate(((LR, "ba"), (LI, "bx"))):
                    if b < 3:
                        act.wait_ge(s_gate, 2 * b + gate + 1)
                    else:
                        act.wait_ge(s_used, C_LA + gate + 1)
                    for t in range(2):
                        last = nc.scalar.activation(dst[:, 2 * b + t, :], b2(bank[(U_LA + gate) % 2])[:, t, :],
                                                    ACT.Sigmoid, bias=vec(vb, 2 * b + t))
                    last.then_inc(s_free, 1)

            for j in range(3):
                hi_ahead(act, C_LU + 1 + j)
                gate_input_hi(j)
            hi_ahead(act, C_LA)
            gate_sigmoids(0)
            gate_input_hi(3)
            for b in range(1, 4):
                gate_sigmoids(b)
            hi_ahead(act, C_LX)
            hi_ahead(act, C_LY)
            act.drain().then_inc(sg("ri"), 1)
            act.wait_ge(sg("spl"), 1)
            for k in range(KT):
                nc.scalar.activation(LE[:, k, :], LR[:, k, :], ACT.Tanh, scale=lbv[:, 2, k:k + 1])
            for k in range(KT):
                nc.scalar.activation(LA[:, k, :], LR[:, k, :], ACT.Exp, scale=lbv[:, 1, k:k + 1])
            act.drain()
            nc.scalar.activation(LB, LE, ACT.Ln, bias=one_t[:, 0:1])
            nc.scalar.activation(LE, LE, ACT.Sqrt, scale=2.0)
            act.drain().then_inc(sg("le"), 1)
            nc.scalar.activation(LB, LB, ACT.Exp, scale=-0.5).then_inc(sg("ab2"), 1)
            for i, t in enumerate((slice(0, 6), slice(6, 8))):
                act.wait_ge(sg("ly"), i + 1)
                nc.scalar.activation(LY[:, t, :], LY[:, t, :], ACT.Gelu_apprx_tanh).then_inc(sg("gelu"), 1)
            act.wait_ge(s_used, C_LOUT)
            for j in range(4):
                act.wait_ge(sg("lm"), j + 1)
                for k in (2 * j, 2 * j + 1):
                    nc.scalar.activation(x_hi[:, k, :], HS[:, k, :], ACT.Copy).then_inc(s_xhi, 1)
            act.wait_ge(s_whi, C_LOUT + 1)
            hi_ahead(act, C_LY + 3)
            for n in range(C_LOUT, C_FB):
                hi_ahead(act, n)
            swiglu_act(C_FB, 8, 7, 6, ("norm_ffn", 8), FF2_STEPS, C_FB)
            stat_square(act, 8, x_pair, s_x, 4 * 6)
            stat_sqrt(act, 8)
            act.wait_ge(sg("yt"), 1)
            for j in range(2):
                copy(ytok[:, 0, 512 * j:512 * j + 512], bank[4 + j][:, :])
            act.drain().then_inc(s_y, 1)
            barrier(act, 5)

        @block.tensor
        def _(pe):
            def feat(n, u, **kw):
                gemm_feat(pe, n, u, bank_of(u), **kw)

            pe.wait_ge(s_xin, 32)
            for k in range(KT):
                for i in range(2):
                    last = nc.tensor.transpose(bank[4 + k // 2][:, (k % 2) * S + i * P:(k % 2) * S + (i + 1) * P],
                                               xin[:, i, k * P:(k + 1) * P], IDENT)
                if k % 2:
                    last.then_inc(sg("xt"), 1)
            pe.wait_ge(s_bias[0], 32)
            pe.wait_ge(s_const, 1)
            pe.wait_ge(s_x, 1)
            nc.tensor.matmul(bank[4][0:8, 0:BIAS_W], rel[:, :], hot[:, :], start=True, stop=True
                             ).then_inc(s_bias[1], 1)
            feat(0, 0, prod=0)
            stat_sum(pe, 0)
            for n in range(1, C_AV):
                feat(n, n)
            pe.wait_ge(s_rs, 1)
            pe.wait_ge(s_bias[2], 1)
            for i in range(2):
                last = nc.tensor.matmul(bank[5][:, i:i + 1], rstd[0:1, i * P:(i + 1) * P], one_t[0:1, 0:1],
                                        start=True, stop=True)
            last.then_inc(s_rc[0], 1)
            for n in (C_AV, C_AV + 1):
                gemm_tok(pe, n, n, bank_of(n))
            def scores(p):
                if p >= 2:
                    pe.wait_ge(sg("al"), p - 1)
                for h2 in range(2):
                    o = bank[4 + 2 * (p % 2) + h2]
                    r = slice(64 * h2, 64 * h2 + 64)
                    nc.tensor.matmul(o[:, 0:256], a_q[r, p, P:S], a_k[r, p, :], start=True, stop=True)
                    last = nc.tensor.matmul(o[:, 256:384], a_q[r, p, 0:P], a_k[r, p, 0:P], start=True, stop=True)
                last.then_inc(sg("as"), 1)

            def prob_t(p):
                if p >= 2:
                    pe.wait_ge(sg("apt"), p - 1)
                for h2 in range(2):
                    h = 2 * p + h2
                    for j in range(3):
                        last = nc.tensor.transpose(bank[4 + 2 * (p % 2) + h2][:, j * P:(j + 1) * P],
                                                   Lg[:, h, j * P:(j + 1) * P], IDENT)
                last.then_inc(sg("at"), 1)

            def weighted_values(p):
                pe.wait_ge(sg("apt"), p + 1)
                for h2 in range(2):
                    h = 2 * p + h2
                    r = slice(64 * h2, 64 * h2 + 64)
                    o = bank[3 - p // 2][r, (p % 2) * S:(p % 2 + 1) * S]
                    pt = PTs[:, p % 2, h2, :]
                    v0, v1 = a_v[:, 0, h * HD:(h + 1) * HD], a_v[:, 1, h * HD:(h + 1) * HD]
                    nc.tensor.matmul(o[:, P:S], v0, pt[:, 0:P], start=True, stop=False)
                    nc.tensor.matmul(o[:, P:S], v1, pt[:, P:2 * P], start=False, stop=True)
                    last = nc.tensor.matmul(o[:, 0:P], v0, pt[:, 2 * P:3 * P], start=True, stop=True)
                last.then_inc(sg("ao"), 1)

            pe.wait_ge(sg("aqk"), 1)
            scores(0)
            scores(1)
            feat(C_GQ, C_GQ)
            scores(2)
            scores(3)
            for n in range(C_GQ + 1, C_AB):
                feat(n, n)
            pe.wait_ge(sg("ap"), 1)
            prob_t(0)
            prob_t(1)
            gemm_feat(pe, C_AB, C_AB, bank_of(C_AB), ntiles=1)
            weighted_values(0)
            prob_t(2)
            weighted_values(1)
            prob_t(3)
            weighted_values(2)
            weighted_values(3)
            feat(C_Z, C_Z)
            pe.wait_ge(s_small, 48)
            barrier(pe, 0)
            for g in range(2):
                pe.wait_ge(sg("gsq"), g + 1)
                for hp in range(4):
                    last = nc.tensor.matmul(bank[4 + 2 * g + hp // 2][:, (hp % 2) * S:(hp % 2 + 1) * S], BLOCK,
                                            ar(1024 * g, 4, S)[:, hp, :], start=True, stop=True)
                last.then_inc(sg("gss"), 1)
            feat(C_Z + 1, C_Z + 1)
            pe.wait_ge(sg("grs"), 2)
            pe.wait_ge(sg("rows"), 1)
            for i in range(2):
                t = slice(i * P, (i + 1) * P)
                nc.tensor.transpose(bank[4][:, i * 8:i * 8 + 8], rows[0:8, R_G, t], IDENT[0:8, 0:8])
                nc.tensor.transpose(bank[5][:, i * 8:i * 8 + 8], rows[32:40, R_B, t], IDENT[32:40, 32:40])
                last = nc.tensor.transpose(bank[4][:, 32 + i * 8:40 + i * 8], rows[0:8, R_L, t], IDENT[0:8, 0:8])
            last.then_inc(sg("colT"), 1)
            for hp in range(4):
                last = nc.tensor.matmul(bank[6 + hp // 2][:, (hp % 2) * S:(hp % 2 + 1) * S], sel[0:8, hp, :],
                                        rows[0:8, R_G, :], start=True, stop=True)
            last.then_inc(sg("gpair"), 1)
            pe.wait_ge(sg("cols"), 1)
            pe.wait_ge(sg("qkn"), 1)
            for hp in range(4):
                last = nc.tensor.matmul(bank[4 + hp // 2][:, (hp % 2) * S:(hp % 2 + 1) * S], sel[32:40, hp, :],
                                        rows[32:40, R_B, :], start=True, stop=True)
            last.then_inc(sg("bpair"), 1)
            pe.wait_ge(sg("EQ"), 1)
            for w, src in enumerate((vT, kT)):
                if w:
                    pe.wait_ge(sg("tk"), 1)
                for i in range(2):
                    for hp in range(4):
                        last = nc.tensor.transpose(bank[6 + i][:, hp * P:(hp + 1) * P],
                                                   src[:, hp, i * P:(i + 1) * P], IDENT)
                last.then_inc(sg("tok"), 1)
            pe.wait_ge(sg("tk"), 2)
            pe.wait_ge(sg("kb"), 1)
            for hf in range(2):
                if hf:
                    pe.wait_ge(sg("lev"), 1)
                for g in range(2):
                    for a, h in enumerate(heads_of(2 * hf + g)):
                        last = nc.tensor.matmul(bank[4 + g][:, a * S:(a + 1) * S], sel[0:8, 4 + h, :],
                                                rows[0:8, R_G, :], start=True, stop=True)
                last.then_inc(sg("gb"), 1)
                pe.wait_ge(sg("DTx"), hf + 1)
                for g in range(2):
                    for dst, rhs in ((4 + g, kbT), (6 + g, qT)):
                        for a, h in enumerate(heads_of(2 * hf + g)):
                            r = slice(64 * (h % 2), 64 * (h % 2) + 64)
                            for i in range(2):
                                t = slice(i * P, (i + 1) * P)
                                q = 2 * a + i
                                last = nc.tensor.matmul(bank[dst][:, q * P:(q + 1) * P], kT[r, h // 2, t],
                                                        rhs[r, h // 2, t], start=True, stop=True)
                last.then_inc(sg("NA"), 1)
                pe.wait_ge(sg("N"), hf + 1)
                for q in range(8):
                    last = nc.tensor.transpose(bank[4 + q // 4][:, (q % 4) * P:(q % 4 + 1) * P], HN[:, q, :], IDENT)
                last.then_inc(sg("Mt"), 1)
                for l in range(1, 6):
                    e = 5 * hf + l - 1
                    pe.wait_ge(sg("Mm"), e + 1)
                    for g in range(2):
                        pe.wait_ge(sg("UT"), 2 * (e + hf) + g + 1)
                        for q in range(4):
                            last = nc.tensor.matmul(bank[4 + g][:, q * P:(q + 1) * P], HMm[:, 4 * g + q, :],
                                                    HN[:, 4 * g + q, :], start=True, stop=True)
                        last.then_inc(sg("Y"), 1)
                    for g in range(2):
                        pe.wait_ge(sg("Yc"), 2 * e + g + 1)
                        for q in range(4):
                            last = nc.tensor.matmul(bank[6 + g][:, q * P:(q + 1) * P], HT[:, 4 * g + q, :],
                                                    YB[:, g, q, :], start=True, stop=True)
                        if l < 5:
                            for q in range(4):
                                last = nc.tensor.matmul(bank[2 + g][:, q * P:(q + 1) * P], YB[:, g, q, :],
                                                        HT[:, 4 * g + q, :], start=True, stop=True)
                        last.then_inc(sg("X"), 1)
                pe.wait_ge(sg("UT"), 12 * (hf + 1))
                for i in range(2):
                    for g in range(2):
                        for a, h in enumerate(heads_of(2 * hf + g)):
                            q = 4 * g + 2 * a + i
                            hh = h - 4 * hf
                            nc.tensor.matmul(bank[4][:, i * S + hh * HD:i * S + (hh + 1) * HD], HN[:, q, :],
                                             bv[:, i, h * HD:(h + 1) * HD], start=True, stop=True)
                            last = nc.tensor.matmul(bank[6][64 * (h % 2):64 * (h % 2) + 64,
                                                            (hh // 2) * S + i * P:(hh // 2) * S + (i + 1) * P],
                                             kbg[:, i, h * HD:(h + 1) * HD], HN[:, q, :], start=True, stop=True)
                last.then_inc(sg("uw"), 1)
            barrier(pe, 1)
            for c in range(4):
                i, r = c // 2, slice(64 * (c % 2), 64 * (c % 2) + 64)
                t = slice(c * CH, (c + 1) * CH)
                pe.wait_ge(sg("S"), c + 1)
                for hp in range(4):
                    last = nc.tensor.matmul(bank[4][r, hp * P:(hp + 1) * P], wT[:, hp, t], St[:, hp, :],
                                            start=True, stop=True)
                last.then_inc(sg("wS"), 1)
                pe.wait_ge(sg("vn"), c + 1)
                if c < 3:
                    for hp in range(4):
                        last = nc.tensor.matmul(bank[6][:, hp * P:(hp + 1) * P], kdec[r, i, hp * P:(hp + 1) * P],
                                                vn[r, i, hp * P:(hp + 1) * P], start=True, stop=True)
                    last.then_inc(sg("kv"), 1)
                if c:
                    pe.wait_ge(sg("oc"), c)
                for hp in range(4):
                    nc.tensor.matmul(bank[5][:, hp * CH:(hp + 1) * CH], St[:, hp, :], qd[:, hp, t],
                                     start=True, stop=False, skip_group_check=True)
                    for h2 in range(2):
                        h = 2 * hp + h2
                        g = 2 * (h // 4) + h % 2
                        q = 4 * g + 2 * ((h % 4) // 2) + i
                        last = nc.tensor.matmul(bank[5][64 * h2:64 * h2 + 64, hp * CH:(hp + 1) * CH],
                                                vn[r, i, h * HD:(h + 1) * HD], AT[r, q, 64 * (c % 2):64 * (c % 2) + 64],
                                                start=False, stop=True, skip_group_check=True)
                last.then_inc(sg("o"), 1)
            pe.wait_ge(sg("osq"), 1)
            for hp in range(4):
                last = nc.tensor.matmul(bank[6 + hp // 2][:, (hp % 2) * S:(hp % 2 + 1) * S], BLOCK, sqo[:, hp, :],
                                        start=True, stop=True)
            last.then_inc(sg("oss"), 1)
            for j in range(4):
                feat(C_OUT + j, U_OUT + j, prod=1 if j == 0 else None)
            stat_sum(pe, 1)

            def open_acc(pe):
                for b in range(4, 8):
                    nc.tensor.matmul(bank[b][:, :], zeros[:, 0:P], zeros[:, :], start=True, stop=False,
                                     skip_group_check=True)

            gemm_feat(pe, C_FF, U_FF, bank_of(U_FF), prod=2)
            stat_sum(pe, 2)
            open_acc(pe)
            with pe.Fori(0, (FF_STEPS - 1) // 3) as i:
                for j in range(3):
                    n = C_FF + 1 + 2 * j
                    gemm_feat(pe, n, U_FF + 1 + j, bank[ff_bank(j + 1)], i=i, di=3)
                    gemm_down(pe, n + 1, j % 3, j + 1, i, 3)
            gemm_down(pe, C_HF - 1, (FF_STEPS - 1) % 3, FF_STEPS)
            stat_sum(pe, 3)
            feat(C_HF, U_HG, prod=3)
            stat_sum(pe, 4)
            barrier(pe, 2)
            pe.drain().then_inc(s_bar, 1)
            for j in range(1, 8):
                feat(C_HF + j, U_HG + j)
            pe.wait_ge(s_rs, 5)
            for i in range(2):
                last = nc.tensor.matmul(bank[7][:, i:i + 1], rstd[0:1, i * P:(i + 1) * P], one_t[0:1, 0:1],
                                        start=True, stop=True)
            last.then_inc(s_rc[1], 1)
            for j in range(8, 12):
                gemm_tok(pe, C_HF + j, U_HG + j, bank_of(U_HG + j))
            for j in range(12, 16):
                feat(C_HF + j, U_HG + j)
            pe.wait_ge(s_bar, 16)
            for l in range(-1, 8):
                if l >= 0:
                    pe.wait_ge(sg("hQK"), l + 1)
                    pe.wait_ge(sg("hQd"), l + 1)
                for b in range(4):
                    if l >= 0:
                        pe.wait_ge(sg("hC"), 4 * l + b + 1)
                    if l == 7 and b >= 2:
                        continue
                    if l == 7:
                        for q in range(4):
                            h = 4 * b + q
                            last = nc.tensor.matmul(bank[4 + b][:, q * P:(q + 1) * P], QK[1][:, h, 0:P],
                                                    QK[1][:, h, P:S], start=True, stop=True)
                    else:
                        for q in range(4):
                            h, i = 2 * b + q // 2, q % 2
                            t = slice(i * P, (i + 1) * P)
                            lhs = HK if l < 0 else QK[l % 2]
                            rhs = HQ if l < 0 else QK[l % 2]
                            last = nc.tensor.matmul(bank[4 + b][:, q * P:(q + 1) * P], lhs[:, h, t],
                                                    rhs[:, h, t], start=True, stop=True)
                    if l >= 0:
                        last.then_inc(sg("hS"), 2 if l == 7 else 1)
                    else:
                        last.then_inc(sg("hD"), 1)
            pe.wait_ge(sg("off"), 1)
            pe.wait_ge(sg("hC"), 32)
            for h in range(8):
                o = bank[4 + h // 2][:, (h % 2) * S:(h % 2 + 1) * S]
                v0, v1 = HV[:, 0, h * P:(h + 1) * P], HV[:, 1, h * P:(h + 1) * P]
                nc.tensor.matmul(o[:, 0:P], v0, HAT[:, h, 0, :], start=True, stop=True)
                nc.tensor.matmul(o[:, P:S], v0, OFF[:, h, :], start=True, stop=False)
                last = nc.tensor.matmul(o[:, P:S], v1, HAT[:, h, 1, :], start=False, stop=True)
                if h % 2:
                    last.then_inc(sg("ho"), 1)
            for b in range(4):
                pe.wait_ge(sg("hsq"), b + 1)
                for h in (2 * b, 2 * b + 1):
                    last = nc.tensor.matmul(bank[2 + b][:, (h % 2) * S:(h % 2 + 1) * S], mean_mat[:, :],
                                            HB[:, h, :], start=True, stop=True)
                last.then_inc(sg("hss"), 1)
            for j in range(4):
                feat(C_HOUT + j, U_HOUT + j, prod=4 if j == 0 else None)

            def swiglu_pe(c, u, e, r, step0):
                for j in range(2):
                    feat(c + j, u + j, prod=e if j == 0 else None)
                    if j == 0:
                        stat_sum(pe, r)
                open_acc(pe)
                h0 = FF_STEPS + step0 + (4 if c == C_FB else 0)
                with pe.Fori(0, (FF2_STEPS - 1) // 2) as i:
                    for j in range(2):
                        n = c + 2 + 3 * j
                        for t in range(2):
                            uu = u + 2 + 2 * j + t
                            gemm_feat(pe, n + t, uu, bank_of(uu), i=i, di=4)
                        gemm_down(pe, n + 2, j % 2, h0 + j + 1, i, 2)
                gemm_down(pe, c + 3 * FF2_STEPS - 1, (FF2_STEPS - 1) % 2, h0 + FF2_STEPS)

            swiglu_pe(C_FA, U_FA, 5, 5, 0)
            feat(C_LU, U_LU, prod=6)
            stat_sum(pe, 6)
            barrier(pe, 4)
            for j in range(1, 4):
                feat(C_LU + j, U_LU + j)
            for gate in range(2):
                pe.wait_ge(s_wlo, C_LA + gate + 1)
            for b in range(4):
                pe.wait_ge(s_hlo, H_GATES + b + 1)
                for gate in range(2):
                    n, u = C_LA + gate, U_LA + 2 * b + gate
                    wh, wl = slot(w_hi, n, "up"), slot(w_lo, n, "up")
                    pe.wait_ge(s_free, u if u == U_LA else u - 1)
                    for t in range(2):
                        for k in range(2):
                            last = pair_mm(bank_of(u)[:, t * S:(t + 1) * S], wh[:, 2 * b + k, t * P:(t + 1) * P],
                                           wl[:, 2 * b + k, t * P:(t + 1) * P],
                                           h_hi[:, b % 3, k * S:(k + 1) * S], h_lo[:, b % 3, k * S:(k + 1) * S],
                                           k == 0, k == 1)
                    last.then_inc(s_used if b == 3 else s_gate, 1)
            pe.wait_ge(s_free, U_LY)
            for j in range(4):
                feat(C_LY + j, U_LY + j)
            for j in range(4):
                feat(C_LOUT + j, U_LOUT + j, prod=7 if j == 0 else None)
            swiglu_pe(C_FB, U_FB, 8, 7, FF2_STEPS)
            stat_sum(pe, 8)
            for i in range(2):
                for k in range(KT):
                    pe.wait_ge(sg("y"), k + 1)
                    last = nc.tensor.transpose(bank[4 + 2 * i + k // 4][:, (k % 4) * P:(k % 4 + 1) * P],
                                               yT[:, k, i * P:(i + 1) * P], IDENT)
                last.then_inc(sg("yt"), 1)
            barrier(pe, 5)

        @block.vector
        def _(dve):
            V = nc.vector

            def fence():
                dve.drain()

            def evac_scaled(u, dst):
                dve.wait_ge(s_used, done(u))
                V.tensor_tensor(dst, b2(bank_of(u)), rb2, ALU.mult).then_inc(s_free, 1)

            def evac_tok(u, dst):
                dve.wait_ge(s_used, done(u))
                for i in range(2):
                    last = V.tensor_scalar(dst[:, i, :], bank_of(u)[:, i * COLS:(i + 1) * COLS], rcol[:, i:i + 1],
                                           None, ALU.mult)
                last.then_inc(s_free, 1)

            def add_result(dve, u, j):
                dve.wait_ge(s_used, done(u))
                x = xT[:, 2 * j:2 * j + 2, :]
                V.tensor_tensor(x, x, b2(bank_of(u)), ALU.add).then_inc(s_free, 1)

            for k in range(4):
                dve.wait_ge(sg("xt"), k + 1)
                V.tensor_copy(x_pair(k), b2(bank[4 + k])).then_inc(s_x, 1)
            dve.wait_ge(s_vec, 16)
            lo_part(dve, 0)
            x_parts_lo(dve, 0, xT, ("pre_mix", 0))
            lo_part(dve, 1)
            lo_ahead(dve, 0)
            stat_recip(dve, 0)
            dve.wait_ge(s_const, 1)
            dsts = {}
            for j in range(2):
                dsts[C_AQ + j] = a_q[:, 2 * j:2 * j + 2, :]
                dsts[C_AK + j] = a_k[:, 2 * j:2 * j + 2, :]
            for g in range(3):
                for j in range(2):
                    dsts[C_GQ + 2 * g + j] = GP[:, 4 * g + 2 * j:4 * g + 2 * j + 2, 3:3 + S]

            def biased_logits(p):
                if p == 0:
                    dve.wait_ge(s_bias[3], 32)
                dve.wait_ge(sg("as"), p + 1)
                for h2 in range(2):
                    b, h = bank[4 + 2 * (p % 2) + h2], 2 * p + h2
                    V.scalar_tensor_tensor(Lg[:, h, 0:256], b[:, 0:256], HD ** -0.5, biasM[:, h, :],
                                           ALU.mult, ALU.add)
                    last = V.scalar_tensor_tensor(Lg[:, h, 256:384], b[:, 256:384], HD ** -0.5,
                                                  biasM[:, h, P:S], ALU.mult, ALU.add)
                last.then_inc(sg("al"), 1)

            def maxima():
                fence()
                mx2 = nmx.rearrange("p (h t) -> p h t", t=2)
                V.tensor_reduce(mx2[:, :, 0:1], Lg[:, :, 0:256], AX, ALU.max)
                V.tensor_reduce(mx2[:, :, 1:2], Lg[:, :, 256:384], AX, ALU.max)
                fence()
                V.tensor_scalar(nmx, nmx, -1.0, None, ALU.mult)
                dve.drain().then_inc(sg("am"), 1)

            def normalise():
                dve.wait_ge(sg("ae"), 1)
                V.reciprocal(sums, sums)
                fence()
                sm2 = sums.rearrange("p (h t) -> p h t", t=2)
                V.tensor_tensor(Lg[:, :, 0:256], Lg[:, :, 0:256], sm2[:, :, 0:1].to_broadcast([P, 8, 256]), ALU.mult)
                V.tensor_tensor(Lg[:, :, 256:384], Lg[:, :, 256:384], sm2[:, :, 1:2].to_broadcast([P, 8, P]),
                                ALU.mult)
                dve.drain().then_inc(sg("ap"), 1)

            def transposed(p):
                dve.wait_ge(sg("at"), p + 1)
                if p >= 2:
                    dve.wait_ge(sg("ao"), p - 1)
                for h2 in range(2):
                    last = V.tensor_copy(PTs[:, p % 2, h2, :], bank[4 + 2 * (p % 2) + h2][:, 0:384])
                last.then_inc(sg("apt"), 1)

            for n in range(0, C_AB + 1):
                if n:
                    lo_ahead(dve, n)
                if n == C_AB:
                    transposed(0)
                    transposed(1)
                if n in dsts:
                    evac_scaled(n, dsts[n])
                elif n in (C_AV, C_AV + 1):
                    if n == C_AV:
                        dve.wait_ge(s_rc[0], 1)
                        V.tensor_copy(rcol[:, :], bank[5][:, 0:2])
                        fence()
                    evac_tok(n, a_v[:, :, (n - C_AV) * COLS:(n - C_AV + 1) * COLS])
                elif n == C_AB:
                    dve.wait_ge(s_used, n + 1)
                    dve.wait_ge(s_gr, 16)
                    b = bank_of(n)
                    V.tensor_tensor(rows[0:8, R_A, :], b[0:8, 0:S], rstd[0:8, :], ALU.mult)
                    V.tensor_tensor(rows[32:40, R_B, :], b[32:40, 0:S], rstd[32:40, :], ALU.mult
                                    ).then_inc(s_free, 1)
                    fence()
                    V.tensor_scalar(rows[0:8, R_A, :], rows[0:8, R_A, :], gdn_rows[:, 1:2], None, ALU.add)
                if n == C_AV:
                    dve.drain().then_inc(sg("aqk"), 1)
                if n == C_GQ + 1:
                    dve.drain().then_inc(sg("gp"), 1)
                if n == C_GK + 1:
                    dve.drain().then_inc(sg("gp"), 1)
                if n == C_AV + 1:
                    biased_logits(0)
                    biased_logits(1)
                if n == C_GQ:
                    biased_logits(2)
                    biased_logits(3)
                if n == C_GQ + 1:
                    maxima()
                if n == C_GV:
                    normalise()
            dve.drain().then_inc(sg("ab"), 1)
            transposed(2)
            transposed(3)
            for j in range(2):
                dve.wait_ge(sg("ao"), 2 * j + 2)
                V.tensor_copy(mixA[:, 2 * j:2 * j + 2, :], b2(bank[3 - j]))
            dve.wait_ge(sg("sp"), 1)
            V.scalar_tensor_tensor(rows[0:8, R_A, :], rows[0:8, R_A, :], 0.0, rows[0:8, R_T, :], ALU.max, ALU.add)
            fence()
            V.tensor_scalar(rows[0:8, R_A, :], rows[0:8, R_A, :], gdn_rows[:, 0:1], -1.0, ALU.mult, ALU.mult)
            fence()
            V.tensor_tensor_scan(rows[0:8, R_G, :], reset[0:8, :], rows[0:8, R_A, :], 0.0, ALU.mult, ALU.add)
            fence()
            rg = rows[0:8, R_G, :].rearrange("p (c t) -> p c t", t=CH)
            V.tensor_tensor(rows[0:8, R_L, :].rearrange("p (c t) -> p c t", t=CH),
                            rg[:, :, CH - 1:CH].to_broadcast([8, 4, CH]), rg, ALU.subtract)
            dve.drain().then_inc(sg("rows"), 1)
            dve.wait_ge(s_small, 48)
            barrier(dve, 0)
            for k in range(4):
                V.tensor_scalar(vT[:, k, :], GP[:, 8 + k, 0:S], vec("conv_w", 8 + k), None, ALU.mult)
            for tap in range(1, 4):
                fence()
                for k in range(4):
                    V.scalar_tensor_tensor(vT[:, k, :], GP[:, 8 + k, tap:tap + S], vec("conv_w", 12 * tap + 8 + k),
                                           vT[:, k, :], ALU.mult, ALU.add)
            dve.drain().then_inc(sg("conv"), 1)
            dve.wait_ge(sg("silu"), 3)
            dve.wait_ge(sg("gsq"), 2)
            for g, dst in enumerate((qT, kT)):
                dve.wait_ge(sg("grs"), g + 1)
                V.scalar_tensor_tensor(dst, dst, HD ** -0.5 if g == 0 else 1.0, ar(2048 + 1024 * g, 4, S),
                                       ALU.mult, ALU.mult)
            fence()
            dve.drain().then_inc(sg("qkn"), 1)
            dve.wait_ge(sg("bpair"), 1)
            for j in range(2):
                V.tensor_tensor(kbT[:, 2 * j:2 * j + 2, :], kT[:, 2 * j:2 * j + 2, :], b2(bank[4 + j]), ALU.mult)
            dve.drain().then_inc(sg("kb"), 1)
            dve.wait_ge(sg("EQ"), 1)
            V.tensor_tensor(qd, qT, EQ, ALU.mult)
            dve.wait_ge(sg("cols"), 1)
            V.tensor_tensor(gecol, bcol, ecol, ALU.mult)
            fence()

            def col64(c, i):
                return c[:, i, :].unsqueeze(2).to_broadcast([P, 8, HD])

            def h64(t):
                return t.rearrange("p (h d) -> p h d", d=HD)
            dve.wait_ge(sg("tok"), 1)
            for i in range(2):
                V.tensor_tensor(h64(bv[:, i, :]), h64(bank[6 + i][:, :]), col64(bcol, i), ALU.mult)
            dve.drain().then_inc(sg("tk"), 1)
            dve.wait_ge(sg("tok"), 2)
            for i in range(2):
                V.tensor_tensor(h64(kbg[:, i, :]), h64(bank[6 + i][:, :]), col64(gecol, i), ALU.mult)
                V.tensor_tensor(h64(kdec[:, i, :]), h64(bank[6 + i][:, :]), col64(kcol, i), ALU.mult)
            dve.drain().then_inc(sg("tk"), 1)
            i4 = IDENT.unsqueeze(1).to_broadcast([P, 4, P])
            for hf in range(2):
                dve.wait_ge(sg("gb"), hf + 1)
                for g in range(2):
                    for a, h in enumerate(heads_of(2 * hf + g)):
                        for i in range(2):
                            V.tensor_scalar(HM[:, 4 * g + 2 * a + i, :],
                                            bank[4 + g][:, a * S + i * P:a * S + (i + 1) * P],
                                            gcol[:, i, h:h + 1], 0.0, ALU.subtract, ALU.min)
                dve.drain().then_inc(sg("DTx"), 1)
                dve.wait_ge(sg("DTe"), hf + 1)
                V.tensor_tensor(HM, HM, CAUSAL.unsqueeze(1).to_broadcast([P, 8, P]), ALU.mult)
                fence()
                dve.wait_ge(sg("NA"), hf + 1)
                for g in range(2):
                    m = HM[:, 4 * g:4 * g + 4, :]
                    V.tensor_tensor(HN[:, 4 * g:4 * g + 4, :], bank[4 + g][:, :].rearrange("p (a b) -> p a b", a=4),
                                    m, ALU.mult)
                    V.tensor_tensor(AT[:, 8 * hf + 4 * g:8 * hf + 4 * g + 4, :],
                                    bank[6 + g][:, :].rearrange("p (a b) -> p a b", a=4), m, ALU.mult)
                dve.drain().then_inc(sg("N"), 1)
                dve.wait_ge(sg("M"), hf + 1)
                for g in range(2):
                    s4 = slice(4 * g, 4 * g + 4)
                    V.tensor_tensor(HN[:, s4, :], HN[:, s4, :], masks[:, 0, :].unsqueeze(1).to_broadcast([P, 4, P]),
                                    ALU.mult)
                    V.tensor_tensor(HT[:, s4, :], HM[:, s4, :], masks[:, 7, :].unsqueeze(1).to_broadcast([P, 4, P]),
                                    ALU.mult)
                    fence()
                    V.tensor_tensor(HN[:, s4, :], i4, HN[:, s4, :], ALU.subtract)
                    V.tensor_tensor(HT[:, s4, :], i4, HT[:, s4, :], ALU.subtract)
                    dve.drain().then_inc(sg("UT"), 1)
                for l in range(1, 6):
                    e = 5 * hf + l - 1
                    for g in range(2):
                        s4 = slice(4 * g, 4 * g + 4)
                        dve.wait_ge(sg("X"), 2 * e + g + 1)
                        V.tensor_tensor(HN[:, s4, :], HN[:, s4, :],
                                        bank[6 + g][:, :].rearrange("p (a b) -> p a b", a=4), ALU.subtract)
                        if l < 5:
                            V.tensor_tensor(HT[:, s4, :], HT[:, s4, :],
                                            bank[2 + g][:, :].rearrange("p (a b) -> p a b", a=4), ALU.subtract)
                        dve.drain().then_inc(sg("UT"), 1)
                dve.wait_ge(sg("uw"), hf + 1)
                for i in range(2):
                    V.tensor_copy(bv[:, i, 256 * hf:256 * hf + 256], bank[4][:, i * S:(i + 1) * S])
                dve.wait_ge(sg("uwc"), hf + 1)
                dve.drain().then_inc(sg("lev"), 1)
            barrier(dve, 1)
            for c in range(4):
                i, r = c // 2, slice(64 * (c % 2), 64 * (c % 2) + 64)
                dve.wait_ge(sg("wS"), c + 1)
                V.tensor_tensor(vn[r, i, :], bv[r, i, :], bank[4][r, :], ALU.subtract).then_inc(sg("vn"), 1)
                if c < 3:
                    gl = EQ[:, :, c * CH + CH - 1:c * CH + CH]
                    dve.wait_ge(sg("kv"), c + 1)
                    if c == 0:
                        dve.wait_ge(sg("S"), 1)
                    for h2 in range(2):
                        hr = slice(64 * h2, 64 * h2 + 64)
                        V.tensor_tensor(St2[hr, :, hr], St[hr, :, hr], gl[hr, :, :].to_broadcast([64, 4, HD]), ALU.mult)
                    fence()
                    dve.wait_ge(sg("o"), c + 1)
                    for h2 in range(2):
                        hr = slice(64 * h2, 64 * h2 + 64)
                        V.tensor_tensor(St[hr, :, hr], St2[hr, :, hr],
                                        bank[6][hr, :].rearrange("p (a b) -> p a b", a=4)[:, :, hr], ALU.add)
                    dve.drain().then_inc(sg("S"), 1)
                if c < 2:
                    evac_scaled(C_Z + c, zs[:, 2 * c:2 * c + 2, :])
                    dve.drain().then_inc(sg("z"), 1)
                if c == 2:
                    lo_ahead(dve, C_Z)
            lo_ahead(dve, C_Z + 1)
            dve.wait_ge(sg("zs"), 1)
            dve.wait_ge(sg("oc"), 4)
            V.scalar_tensor_tensor(mixG, oT, vec("gdn_w", 0), zs, ALU.mult, ALU.mult)
            x_parts_lo(dve, 1, mixA, None, range(4))
            fence()
            dve.wait_ge(sg("ors"), 1)
            V.tensor_tensor(mixG, mixG, ro, ALU.mult)
            dve.drain().then_inc(sg("mixG"), 1)
            for k in range(4):
                dve.wait_ge(s_xhi, 8 + 4 + k + 1)
                V.tensor_tensor(x_lo[:, 4 + k, :], mixG[:, k, :], x_hi[:, 4 + k, :].bitcast(F32), ALU.subtract
                                ).then_inc(s_xlo, 1)
            for j in range(4):
                lo_ahead(dve, C_OUT + j)
                dve.wait_ge(s_used, done(U_OUT + j))
                V.tensor_copy(mT[:, 2 * j:2 * j + 2, :], b2(bank_of(U_OUT + j))).then_inc(s_free, 1)
                dve.drain().then_inc(s_mT, 1)

            def add_normed(r, w, e, w_next):
                stat_recip(dve, r)
                for j in range(4):
                    for k in (2 * j, 2 * j + 1):
                        V.scalar_tensor_tensor(mT[:, k, :], mT[:, k, :], vec(w, k), rstd[:, :], ALU.mult, ALU.mult)
                    fence()
                    V.tensor_tensor(x_pair(j), x_pair(j), mT[:, 2 * j:2 * j + 2, :], ALU.add).then_inc(s_x, 1)
                    if j:
                        x_parts_lo(dve, e, xT, w_next, (2 * j - 2, 2 * j - 1))
                x_parts_lo(dve, e, xT, w_next, (6, 7))

            def mlp_lo(hslot, count, i=None, d=0):
                dve.wait_ge(s_hhi, count + (0 if i is None else i * d))
                V.tensor_tensor(h_lo[:, hslot, :], FH[:, hslot, :], h_hi[:, hslot, :].bitcast(F32), ALU.subtract
                                ).then_inc(s_hlo, 1)

            def relu2(n, b, hslot, i=None):
                dve.wait_ge(s_used, n + 1 + (0 if i is None else i * 6))
                ft = FT[:, hslot, :]
                V.tensor_tensor(ft.rearrange("p (a b) -> p a b", a=2), b2(b), rb2, ALU.mult).then_inc(s_free, 1)
                fence()
                V.scalar_tensor_tensor(FH[:, hslot, :], ft, 0.0, ft, ALU.max, ALU.mult).then_inc(s_h, 1)

            add_normed(1, "post_mix", 2, ("pre_mlp", 0))
            lo_ahead(dve, C_FF)
            stat_recip(dve, 2)
            relu2(C_FF, bank_of(U_FF), 0)
            mlp_lo(0, 1)
            with dve.Fori(0, (FF_STEPS - 1) // 3) as i:
                for j in range(3):
                    n = C_FF + 1 + 2 * j
                    lo_ahead(dve, n, i)
                    relu2(n, bank[ff_bank(j + 1)], (j + 1) % 3, i)
                    lo_ahead(dve, n + 1, i)
                    mlp_lo((j + 1) % 3, j + 2, i, 3)
            lo_ahead(dve, C_HF - 1)
            dve.wait_ge(s_used, C_HF)
            for j in range(4):
                V.tensor_copy(mT[:, 2 * j:2 * j + 2, :], b2(bank[4 + j])).then_inc(s_mT, 1)
            fence()
            add_normed(3, "post_mlp", 3, ("norm_mix", 0))
            lo_ahead(dve, C_HF)
            stat_recip(dve, 4)
            barrier(dve, 2)
            l0, l1 = vecs[:, VEC["lb"]:VEC["lb"] + 8], vecs[:, VEC["lb"] + 8:VEC["lb"] + 16]
            LBV, OML = lbv[:, 0, :], lbv[:, 4, :]
            V.tensor_tensor(lbv[:, 1, :], l0, l1, ALU.max)
            fence()
            V.tensor_tensor(lbv[:, 2, :], l0, lbv[:, 1, :], ALU.subtract)
            V.tensor_tensor(lbv[:, 3, :], l1, lbv[:, 1, :], ALU.subtract)
            dve.drain().then_inc(sg("lb"), 1)
            for j in range(8):
                if j:
                    lo_ahead(dve, C_HF + j)
                evac_scaled(U_HG + j, (HX if j < 4 else HQ)[:, 2 * (j % 4):2 * (j % 4) + 2, :])
                if j == 3:
                    dve.drain().then_inc(sg("fl"), 1)
                    dve.wait_ge(sg("lbe"), 1)
                    V.tensor_tensor(lbv[:, 1, :], lbv[:, 2, :], lbv[:, 3, :], ALU.add)
                    fence()
                    V.reciprocal(lbv[:, 1, :], lbv[:, 1, :])
                    fence()
                    V.tensor_tensor(LBV, lbv[:, 2, :], lbv[:, 1, :], ALU.mult)
                    V.tensor_tensor(OML, lbv[:, 3, :], lbv[:, 1, :], ALU.mult)
                    fence()
                if j == 4:
                    dve.wait_ge(sg("sig"), 1)
                    for k in range(KT):
                        V.tensor_scalar(QK[0][:, k, :], QK[0][:, k, :], OML[:, k:k + 1], LBV[:, k:k + 1],
                                        ALU.mult, ALU.add)
                    dve.drain().then_inc(sg("f"), 1)
                    for k in range(KT):
                        V.tensor_scalar(HK[:, k, :], HK[:, k, :], OML[:, k:k + 1], None, ALU.mult)
                if j == 6:
                    dve.wait_ge(sg("logf"), 1)
                    for k in range(KT):
                        V.tensor_tensor_scan(HB[:, k, :], reset[:, :], HX[:, k, :], 0.0, ALU.mult, ALU.add)
            dve.drain().then_inc(sg("hq"), 1)
            dve.wait_ge(s_rc[1], 1)
            V.tensor_copy(rcol[:, :], bank[7][:, 0:2])
            fence()
            for j in range(4):
                lo_ahead(dve, C_HV + j)
                evac_tok(U_HG + 8 + j, HV[:, :, j * COLS:(j + 1) * COLS])
            barrier(dve, 3)

            def odd_exponents(l):
                if l >= 2:
                    dve.wait_ge(sg("hQK"), l - 1)
                if l < 6:
                    m = 1 << l
                    x = HXs[l % 2].rearrange("p k (b e m) -> p (k b) e m", e=2, m=m)
                    b = HB.rearrange("p k (b e m) -> p (k b) e m", e=2, m=m)
                    ref = b[:, :, 0, m - 1:m].to_broadcast([P, KT * S // (2 * m), m])
                    V.tensor_tensor(x[:, :, 1, :], b[:, :, 1, :], ref, ALU.subtract)
                else:
                    x = HXs[l % 2].rearrange("p k (c t) -> p k c t", t=CH)
                    b = HB.rearrange("p k (c t) -> p k c t", t=CH)
                    for c in ((1, 3) if l == 6 else (2,)):
                        V.tensor_copy(x[:, :, c, :], b[:, :, c, :])
                    if l == 7:
                        V.tensor_tensor(x[:, :, 3, :], b[:, :, 3, :], b[:, :, 2, CH - 1:CH].to_broadcast([P, KT, CH]),
                                        ALU.add)
                dve.drain().then_inc(sg("hX"), 1)

            def decayed_q(l):
                dve.wait_ge(sg("hE"), l + 1)
                q, x = QK[l % 2], HXs[l % 2]
                if l < 7:
                    m = 1 << l
                    v = lambda t: t.rearrange("p k (b e m) -> p (k b) e m", e=2, m=m)
                    V.tensor_tensor(v(q)[:, :, 1, :], v(HQ)[:, :, 1, :], v(x)[:, :, 1, :], ALU.mult)
                else:
                    V.tensor_tensor(q[:, :, P:S], HQ[:, :, P:S], x[:, :, P:S], ALU.mult)
                dve.drain().then_inc(sg("hQd"), 1)

            def place(l, semname, first):
                m = (IDENT if l < 0 else masks[:, l, :]).bitcast(I32).unsqueeze(1).to_broadcast([P, 4, P])
                for b in range(4):
                    dve.wait_ge(sg(semname), first + b + 1)
                    V.copy_predicated(HAT[:, 2 * b:2 * b + 2, :, :].rearrange("p h i t -> p (h i) t"), m,
                                      bank[4 + b][:, :].rearrange("p (a b) -> p a b", a=4)).then_inc(sg("hC"), 1)
                fence()

            odd_exponents(0)
            for j in range(4):
                lo_ahead(dve, C_HG + j)
                evac_scaled(U_HG + 12 + j, HG[:, 2 * j:2 * j + 2, :])
            dve.drain().then_inc(sg("hg"), 1)
            dve.wait_ge(sg("HAT0"), 1)
            for l in range(8):
                if l < 7:
                    odd_exponents(l + 1)
                decayed_q(l)
                if l == 0:
                    place(-1, "hD", 0)
                else:
                    place(l - 1, "hS", 4 * (l - 1))
            dve.wait_ge(sg("hgs"), 1)
            for b in range(4):
                dve.wait_ge(sg("ho"), b + 1)
                pair = slice(2 * b, 2 * b + 2)
                V.scalar_tensor_tensor(HX[:, pair, :], b2(bank[4 + b]), vec("hg_w", 0), HG[:, pair, :],
                                       ALU.mult, ALU.mult).then_inc(sg("hog"), 1)
            fence()
            for b in range(4):
                dve.wait_ge(sg("hrs"), b // 2 + 1)
                pair = slice(2 * b, 2 * b + 2)
                V.tensor_tensor(HX[:, pair, :], HX[:, pair, :], HQ[:, pair, :], ALU.mult).then_inc(sg("hm"), 1)
                if b:
                    x_parts_lo(dve, 4, HX, None, (2 * b - 2, 2 * b - 1))
            x_parts_lo(dve, 4, HX, None, (6, 7))
            for j in range(4):
                lo_ahead(dve, C_HOUT + j)
                add_result(dve, U_HOUT + j, j)
                dve.drain().then_inc(s_x, 1)

            def swiglu_dve(c, u, e, r, w, step0):
                x_parts_lo(dve, e, xT, w)
                lo_ahead(dve, c)
                stat_recip(dve, r)
                h0 = FF_STEPS + step0 + (4 if c == C_FB else 0)

                def gate(n, uu, hslot, i=None):
                    dve.wait_ge(s_used, n + 1 + (0 if i is None else i * 6))
                    V.tensor_tensor(FT[:, hslot, :].rearrange("p (a b) -> p a b", a=2), b2(bank_of(uu)), rb2,
                                    ALU.mult).then_inc(s_free, 1)
                    dve.drain().then_inc(s_g2, 1)

                def up(n, uu, hslot, i=None):
                    dve.wait_ge(s_used, n + 1 + (0 if i is None else i * 6))
                    V.tensor_tensor(FU[:, hslot, :].rearrange("p (a b) -> p a b", a=2), b2(bank_of(uu)), rb2,
                                    ALU.mult).then_inc(s_free, 1)
                    fence()

                def hidden(k, hslot, i=None):
                    dve.wait_ge(s_silu, k + 1 + (0 if i is None else i * 2))
                    V.tensor_tensor(FH[:, hslot, :], FS[:, hslot, :], FU[:, hslot, :], ALU.mult).then_inc(s_h, 1)

                gate(c, u, 0)
                lo_ahead(dve, c + 1)
                up(c + 1, u + 1, 0)
                hidden(step0, 0)
                mlp_lo(0, h0 + 1)

                def two_steps(i):
                    for j in range(2):
                        n, uu, hs = c + 2 + 3 * j, u + 2 + 2 * j, (j + 1) % 2
                        lo_ahead(dve, n, i)
                        gate(n, uu, hs, i)
                        lo_ahead(dve, n + 1, i)
                        up(n + 1, uu + 1, hs, i)
                        hidden(step0 + j + 1, hs, i)
                        lo_ahead(dve, n + 2, i)
                        mlp_lo(hs, h0 + j + 2, i, 2)

                with dve.Fori(0, swiglu_rounds(c)) as i:
                    two_steps(i)
                if c == C_FB:
                    two_steps(swiglu_rounds(c))
                lo_ahead(dve, c + 3 * FF2_STEPS - 1)

            def add_acc(chunks, e=None, w=None):
                dve.wait_ge(s_used, chunks)
                for j in range(4):
                    V.tensor_tensor(x_pair(j), x_pair(j), b2(bank[4 + j]), ALU.add).then_inc(s_x, 1)
                    if e is not None and j:
                        x_parts_lo(dve, e, xT, w, (2 * j - 2, 2 * j - 1))
                if e is not None:
                    x_parts_lo(dve, e, xT, w, (6, 7))

            swiglu_dve(C_FA, U_FA, 5, 5, ("norm_ffn", 0), 0)
            add_acc(C_LU, 6, ("norm_mix", 8))
            lo_ahead(dve, C_LU)
            stat_recip(dve, 6)
            barrier(dve, 4)
            V.memset(LU[:, :, 0:3], 0.0)
            def gate_input_lo(j):
                dve.wait_ge(s_hhi, H_GATES + j + 1)
                V.tensor_tensor(h_lo[:, j % 3, :].rearrange("p (a b) -> p a b", a=2), UC[:, 2 * j:2 * j + 2, :],
                                h_hi[:, j % 3, :].bitcast(F32).rearrange("p (a b) -> p a b", a=2), ALU.subtract
                                ).then_inc(s_hlo, 1)

            for j in range(4):
                if j:
                    lo_ahead(dve, C_LU + j)
                evac_scaled(U_LU + j, LU[:, 2 * j:2 * j + 2, 3:3 + S])
                fence()
                for k in (2 * j, 2 * j + 1):
                    V.tensor_scalar(UC[:, k, :], LU[:, k, 0:S], vec("lconv_w", k), vec("lconv_b", k),
                                    ALU.mult, ALU.add)
                for tap in range(1, 4):
                    fence()
                    for k in (2 * j, 2 * j + 1):
                        V.scalar_tensor_tensor(UC[:, k, :], LU[:, k, tap:tap + S], vec("lconv_w", 8 * tap + k),
                                               UC[:, k, :], ALU.mult, ALU.add)
                dve.drain().then_inc(sg("uc"), 1)
                if j:
                    gate_input_lo(j - 1)
            gate_input_lo(3)
            lo_ahead(dve, C_LA)
            dve.wait_ge(sg("lam"), 1)
            y, z, z2, acc = lbv[:, 3, :], lbv[:, 0, :], lbv[:, 1, :], lbv[:, 2, :]
            V.tensor_scalar(z, y, 2.0, None, ALU.add)
            fence()
            V.reciprocal(z, z)
            fence()
            V.tensor_tensor(z, z, y, ALU.mult)
            fence()
            V.tensor_tensor(z2, z, z, ALU.mult)
            fence()
            V.tensor_scalar(acc, z2, 1.0 / 17, 1.0 / 15, ALU.mult, ALU.add)
            for c in (13, 11, 9, 7, 5, 3, 1):
                fence()
                V.tensor_tensor(acc, acc, z2, ALU.mult)
                fence()
                V.tensor_scalar(acc, acc, 1.0 / c, None, ALU.add)
            fence()
            V.scalar_tensor_tensor(acc, acc, 2.0, z, ALU.mult, ALU.mult)
            V.tensor_scalar(y, vecs[:, VEC["lam"]:VEC["lam"] + 8], -1.0, 0.0, ALU.mult, ALU.max)
            fence()
            V.tensor_tensor(y, y, acc, ALU.add)
            fence()
            V.tensor_scalar(lbv[:, 1, :], y, -8.0, None, ALU.mult)
            V.tensor_scalar(lbv[:, 2, :], y, 8.0, None, ALU.mult)
            dve.drain().then_inc(sg("spl"), 1)
            lo_ahead(dve, C_LX)
            dve.wait_ge(sg("ri"), 1)
            V.tensor_tensor(LI, LI, UC, ALU.mult)
            fence()
            for j in range(2):
                lo_ahead(dve, C_LY + j)
                evac_scaled(U_LY + j, LY[:, 2 * j:2 * j + 2, :])
            dve.wait_ge(sg("le"), 1)
            V.tensor_tensor(LI, LI, LE, ALU.mult)
            evac_scaled(U_LY + 2, LY[:, 4:6, :])
            dve.drain().then_inc(sg("ly"), 1)
            dve.wait_ge(sg("ab2"), 1)

            def scanned_lo(j):
                for k in (2 * j, 2 * j + 1):
                    dve.wait_ge(s_xhi, 8 * 7 + k + 1)
                    V.tensor_tensor(x_lo[:, k, :], HS[:, k, :], x_hi[:, k, :].bitcast(F32), ALU.subtract
                                    ).then_inc(s_xlo, 1)

            for j in range(4):
                t = slice(2 * j, 2 * j + 2)
                V.tensor_tensor(LI[:, t, :], LI[:, t, :], LB[:, t, :], ALU.mult)
                fence()
                for k in (2 * j, 2 * j + 1):
                    V.tensor_tensor_scan(LR[:, k, :], LA[:, k, :], LI[:, k, :], 0.0, ALU.mult, ALU.add)
                fence()
                if j == 0:
                    lo_ahead(dve, C_LY + 2)
                dve.wait_ge(sg("gelu"), 2 if j == 3 else 1)
                V.tensor_tensor(HS[:, t, :], LR[:, t, :], LY[:, t, :], ALU.mult)
                dve.drain().then_inc(sg("lm"), 1)
                if j == 1:
                    evac_scaled(U_LY + 3, LY[:, 6:8, :])
                    dve.drain().then_inc(sg("ly"), 1)
                if j >= 2:
                    scanned_lo(j - 2)
            scanned_lo(2)
            scanned_lo(3)
            lo_ahead(dve, C_LY + 3)
            for j in range(4):
                lo_ahead(dve, C_LOUT + j)
                add_result(dve, U_LOUT + j, j)
                dve.drain().then_inc(s_x, 1)
            swiglu_dve(C_FB, U_FB, 8, 7, ("norm_ffn", 8), FF2_STEPS)
            add_acc(N_CHUNKS)
            stat_recip(dve, 8)
            for k in range(KT):
                V.scalar_tensor_tensor(yT[:, k, :], xT[:, k, :], vec("final", k), rstd[:, :], ALU.mult, ALU.mult
                                       ).then_inc(sg("y"), 1)
            dve.wait_ge(sg("yt"), 2)
            for j in range(2):
                V.tensor_copy(ytok[:, 1, 512 * j:512 * j + 512], bank[6 + j][:, :])
            dve.wait_ge(s_y, 1)
            dve.drain().then_inc(s_y, 1)
            barrier(dve, 5)


_WEIGHTS = ["w_in", "w_out", "w_up", "w_down", "hgrn_w_in_2", "hgrn_w_out_2", "lru_w_in_2", "lru_wa_2",
            "lru_wx_2", "lru_w_out_2", "ffn_w_in_2", "ffn_w_out_2"]
_OTHERS = ["x"]


def lay_out(inputs):
    a = {n: np.ascontiguousarray(inputs[n]) for n in _WEIGHTS + _OTHERS}

    def columns(v):
        v = np.asarray(v)
        return v.reshape(-1, P).T

    parts = [columns(inputs[n]) for n in ("pre_mix_norm", "post_mix_norm", "pre_mlp_norm", "post_mlp_norm",
                                          "norm_mix_2", "norm_ffn_2", "norm_final_2", "conv_w")]
    parts.append(np.concatenate([np.asarray(inputs["gdn_norm_w"])[0]] * 2)[:, None])
    parts.append(columns(inputs["hgrn_lb_2"]))
    parts += [columns(inputs[n]) for n in ("hgrn_norm_2", "lru_conv_w_2", "lru_conv_b_2", "lru_ba_2", "lru_bx_2",
                                           "lru_lambda_2")]
    a["rel_t"] = np.ascontiguousarray(np.asarray(inputs["rel_bias"]).T)
    a["gdn_rows"] = np.stack([np.asarray(inputs["A_log"])[0], np.asarray(inputs["dt_bias"])[0]], 1)
    a["vecs"] = np.ascontiguousarray(np.concatenate(parts, 1))
    a["masks"], a["sel"], a["hot"] = shape_constants()
    return a


def program(nc, arrays):
    io = {n: nc.dram_tensor(f"in_{n}", a.shape, mybir.dt.from_np(a.dtype), kind="ExternalInput").ap()
          for n, a in arrays.items()}
    io["out"] = nc.dram_tensor("result", (1, S, D), F32, kind="ExternalOutput").ap()
    build(nc, io)


def kernel(**inputs):
    import concourse.bacc as bacc
    from concourse.bass_utils import run_bass_kernel_spmd

    nc = bacc.Bacc("TRN2", target_bir_lowering=False, num_devices=1)
    arrays = lay_out(inputs)
    program(nc, arrays)
    r = run_bass_kernel_spmd(nc, [{f"in_{n}": a for n, a in arrays.items()}], core_ids=[0])
    return r.results[0]["result"]
```
